# Optimizing a Trainium2 kernel written in Bass

```python
import math
import jax, jax.numpy as jnp
from jax import lax
import numpy as np

D_MODEL = 1024
BATCH = 1
SEQ = 512
DEPTH = 2
DEC_BATCH = 8
DEC_SEQ = 4
PAST_LEN = 4096
PAGE_SIZE = 128

N_EVEN = (DEPTH + 1) // 2
N_ODD = DEPTH // 2
D_A = D_MODEL // 2
CONV_W = 31
D_B = D_MODEL // 2
POOL_WINDOWS = (2, 4, 8, 16)
N_POOL_GROUPS = len(POOL_WINDOWS)
POOL_G = D_B // N_POOL_GROUPS
MAX_WIN = max(POOL_WINDOWS)
D_C = D_MODEL
H_C = 8
DH_C = D_C // H_C
CHUNK = 128
D_FF = 4 * D_MODEL
N_MOD = 6
EPS = 1e-6

kernel_name = "hybrid_conv_pool_gmlp_decoder_step"

def rmsnorm(x, g):
    xf = x.astype(jnp.float32)
    y = xf * lax.rsqrt(jnp.mean(xf * xf, axis=-1, keepdims=True) + EPS)
    return (y * g.astype(jnp.float32)).astype(x.dtype)

def layernorm(x, g, b):
    xf = x.astype(jnp.float32)
    mu = jnp.mean(xf, axis=-1, keepdims=True)
    xc = xf - mu
    var = jnp.mean(xc * xc, axis=-1, keepdims=True)
    y = xc * lax.rsqrt(var + EPS) * g.astype(jnp.float32) + b.astype(jnp.float32)
    return y.astype(x.dtype)

def adaln(c, w_ada, b_ada):
    mod = jax.nn.silu(c) @ w_ada + b_ada
    mod = mod.reshape(c.shape[0], N_MOD, D_MODEL)[:, :, None, :]
    return [mod[:, i] for i in range(N_MOD)]

def even_mixer(h, conv_hist, pool_hist, pos0, w_in, w_dw, b_dw, g_cln, b_cln, w_pool, s_pool, w_out):
    T = h.shape[1]
    z = h @ w_in
    a_val, a_gate, p_in = z[..., :D_A], z[..., D_A:2 * D_A], z[..., 2 * D_A:]
    a = a_val * jax.nn.sigmoid(a_gate)
    a_ext = jnp.concatenate([conv_hist.astype(a.dtype), a], axis=1)
    conv = lax.conv_general_dilated(
        a_ext, w_dw[:, None, :], window_strides=(1,), padding='VALID',
        dimension_numbers=('NWC', 'WIO', 'NWC'), feature_group_count=D_A) + b_dw
    a_out = jax.nn.silu(layernorm(conv, g_cln, b_cln))
    P = MAX_WIN - 1
    p_ext = jnp.concatenate([pool_hist.astype(p_in.dtype), p_in], axis=1)
    cs = jnp.cumsum(p_ext.astype(jnp.float32), axis=1)
    cs = jnp.concatenate([jnp.zeros_like(cs[:, :1]), cs], axis=1)
    pos = pos0 + jnp.arange(T) + 1
    diffs = []
    for gi, w in enumerate(POOL_WINDOWS):
        sl = slice(gi * POOL_G, (gi + 1) * POOL_G)
        win_sum = cs[:, P + 1:P + 1 + T, sl] - cs[:, P + 1 - w:P + 1 - w + T, sl]
        cnt = jnp.minimum(w, pos).astype(jnp.float32)[None, :, None]
        diffs.append((win_sum / cnt).astype(p_in.dtype) - p_in[..., sl])
    d = jnp.stack(diffs, axis=2)
    b_out = jnp.einsum('btgi,gio->btgo', d, w_pool).reshape(h.shape[0], T, D_B) * s_pool
    out = jnp.concatenate([a_out, b_out], axis=-1) @ w_out
    return out, a_ext[:, -(CONV_W - 1):], p_ext[:, -(MAX_WIN - 1):]

def odd_mixer(h, w_in, g_v, b_v, w_s, b_s, w_out):
    B, T, _ = h.shape
    z = h @ w_in
    u, v = z[..., :D_C], z[..., D_C:]
    v = layernorm(v, g_v, b_v)
    L = min(T, CHUNK)
    n = T // L
    vc = v.reshape(B, n, L, H_C, DH_C)
    mask = jnp.tril(jnp.ones((CHUNK, CHUNK), dtype=w_s.dtype))
    ws = (w_s * mask)[:, :L, :L]
    s = jnp.einsum('hts,bnshd->bnthd', ws, vc) + b_s[:, :L].T[None, None, :, :, None]
    y = u * s.reshape(B, T, D_C)
    return y @ w_out, v

def trunk(x, c, conv_hist, pool_hist, pos0,
          w_ada, b_ada, g_mix, g_ffn, w_in_ab, w_dw, b_dw, g_conv_ln, b_conv_ln,
          w_pool, s_pool, w_out_ab, w_in_c, g_v_ln, b_v_ln, w_spatial, b_spatial,
          w_out_c, w_ffn1, w_ffn2, g_final):
    new_conv, new_pool, new_v = [], [], []
    for l in range(DEPTH):
        sh1, sc1, gt1, sh2, sc2, gt2 = adaln(c, w_ada[l], b_ada[l])
        h = rmsnorm(x, g_mix[l]) * (1 + sc1) + sh1
        if l % 2 == 0:
            i = l // 2
            out, ch, ph = even_mixer(h, conv_hist[i], pool_hist[i], pos0, w_in_ab[i], w_dw[i], b_dw[i],
                                     g_conv_ln[i], b_conv_ln[i], w_pool[i], s_pool[i], w_out_ab[i])
            new_conv.append(ch)
            new_pool.append(ph)
        else:
            j = l // 2
            out, vrows = odd_mixer(h, w_in_c[j], g_v_ln[j], b_v_ln[j], w_spatial[j], b_spatial[j], w_out_c[j])
            new_v.append(vrows)
        x = x + gt1 * out
        h = rmsnorm(x, g_ffn[l]) * (1 + sc2) + sh2
        f = jnp.square(jax.nn.relu(h @ w_ffn1[l])) @ w_ffn2[l]
        x = x + gt2 * f
    return rmsnorm(x, g_final), jnp.stack(new_conv), jnp.stack(new_pool), jnp.stack(new_v)

def setup_inputs(seed: int = 0) -> dict:
    key = jax.random.key(seed)
    ks = iter(jax.random.split(key, 40))
    f32 = jnp.float32
    nrm = lambda shape, s: jax.random.normal(next(ks), shape, f32) * s
    gain = lambda shape: 1.0 + nrm(shape, 0.1)
    return {
        "x_prompt": nrm((BATCH, SEQ, D_MODEL), 1.0),
        "x_sample": nrm((DEC_BATCH, DEC_SEQ, D_MODEL), 1.0),
        "c_prompt": nrm((BATCH, D_MODEL), 1.0),
        "c_sample": nrm((DEC_BATCH, D_MODEL), 1.0),
        "state_conv": nrm((N_EVEN, DEC_BATCH, CONV_W - 1, D_A), 0.5),
        "state_pool": nrm((N_EVEN, DEC_BATCH, MAX_WIN - 1, D_B), 1.0),
        "w_ada": nrm((DEPTH, D_MODEL, N_MOD * D_MODEL), 0.5 * D_MODEL ** -0.5),
        "b_ada": nrm((DEPTH, N_MOD * D_MODEL), 0.1),
        "g_mix": gain((DEPTH, D_MODEL)),
        "g_ffn": gain((DEPTH, D_MODEL)),
        "w_in_ab": nrm((N_EVEN, D_MODEL, 2 * D_A + D_B), D_MODEL ** -0.5),
        "w_dw": nrm((N_EVEN, CONV_W, D_A), CONV_W ** -0.5),
        "b_dw": nrm((N_EVEN, D_A), 0.02),
        "g_conv_ln": gain((N_EVEN, D_A)),
        "b_conv_ln": nrm((N_EVEN, D_A), 0.02),
        "w_pool": nrm((N_EVEN, N_POOL_GROUPS, POOL_G, POOL_G), POOL_G ** -0.5),
        "s_pool": gain((N_EVEN, D_B)),
        "w_out_ab": nrm((N_EVEN, D_A + D_B, D_MODEL), (D_A + D_B) ** -0.5),
        "w_in_c": nrm((N_ODD, D_MODEL, 2 * D_C), D_MODEL ** -0.5),
        "g_v_ln": gain((N_ODD, D_C)),
        "b_v_ln": nrm((N_ODD, D_C), 0.02),
        "w_spatial": nrm((N_ODD, H_C, CHUNK, CHUNK), CHUNK ** -0.5),
        "b_spatial": gain((N_ODD, H_C, CHUNK)),
        "w_out_c": nrm((N_ODD, D_C, D_MODEL), D_C ** -0.5),
        "w_ffn1": nrm((DEPTH, D_MODEL, D_FF), D_MODEL ** -0.5),
        "w_ffn2": nrm((DEPTH, D_FF, D_MODEL), D_FF ** -0.5),
        "g_final": gain((D_MODEL,)),
    }

def reference(x_prompt, x_sample, c_prompt, c_sample, state_conv, state_pool,
              w_ada, b_ada, g_mix, g_ffn, w_in_ab, w_dw, b_dw, g_conv_ln, b_conv_ln,
              w_pool, s_pool, w_out_ab, w_in_c, g_v_ln, b_v_ln, w_spatial, b_spatial,
              w_out_c, w_ffn1, w_ffn2, g_final):
    weights = (w_ada, b_ada, g_mix, g_ffn, w_in_ab, w_dw, b_dw, g_conv_ln, b_conv_ln,
               w_pool, s_pool, w_out_ab, w_in_c, g_v_ln, b_v_ln, w_spatial, b_spatial,
               w_out_c, w_ffn1, w_ffn2, g_final)
    conv0 = jnp.zeros((N_EVEN, x_prompt.shape[0], CONV_W - 1, D_A), x_prompt.dtype)
    pool0 = jnp.zeros((N_EVEN, x_prompt.shape[0], MAX_WIN - 1, D_B), x_prompt.dtype)
    y_prompt, new_conv_prompt, new_pool_prompt, _ = trunk(
        x_prompt, c_prompt, conv0, pool0, 0, *weights)
    y_sample, new_conv_sample, new_pool_sample, new_v_sample = trunk(
        x_sample, c_sample, state_conv, state_pool, PAST_LEN, *weights)
    return (y_prompt, y_sample, new_conv_prompt, new_pool_prompt,
            new_conv_sample, new_pool_sample, new_v_sample)


_drawn_inputs = setup_inputs


def setup_inputs(seed=0):
    import zlib

    import numpy as np

    out = dict(_drawn_inputs(seed))
    spreads = {}
    factors = {'b_dw': 8.0, 'g_conv_ln': 3.177, 'b_conv_ln': 23.103, 'b_v_ln': 2.96, 's_pool': 2.822}
    for name, (base, spread) in spreads.items():
        noise = np.random.default_rng([zlib.crc32(name.encode()), seed]).standard_normal(out[name].shape)
        drawn = base * np.exp(spread * noise) if base else spread * noise
        out[name] = __import__('jax').numpy.asarray(drawn.astype(out[name].dtype))
    for name, factor in factors.items():
        out[name] = (out[name] * factor).astype(out[name].dtype)
    return out
```

```python
from contextlib import ExitStack

import concourse.bass as bass
from concourse import mybir

ALU = mybir.AluOpType
ACT = mybir.ActivationFunctionType
F32 = mybir.dt.float32
F32R = mybir.dt.float32r
AX_X = mybir.AxisListType.X

P = 128
D = 1024
KT = D // P
SEQ, BATCH_S, SEQ_S = 512, 8, 4
HP, HB = SEQ // 2, BATCH_S // 2
HS = HB * SEQ_S
HALF = HP + HS
TOK = 2 * HALF
NS = BATCH_S * SEQ_S
DA = D // 2
AT = DA // P
TAPS = 31
HIST = TAPS - 1
PHIST = 15
WINDOWS = (2, 4, 8, 16)
FF = 4 * D
QUARTERS = FF // D
HEADS = 8
CHUNK = 128
CHUNKS = SEQ // CHUNK
NCOND = 1 + BATCH_S
NMOD = 6
EPS = 1e-6
BN = 256
RAW = 4
PAIRS = 4
IN_AB = (("value", 0), ("gate", 0), ("value", 2), ("gate", 2), ("pool", 0), ("pool", 2))
MIX_BLOCKS_IN = len(IN_AB)
DIAGS = 8
OUT_BLOCKS = D // BN
FFN_BLOCKS = 2 * OUT_BLOCKS
CPM = 4
SH1, SC1, GT1, SH2, SC2, GT2 = range(NMOD)


MOD_AFTER = {1: GT1, 3: SH2, 4: SC2}


class Own:

    def __init__(self, eng, sem):
        self.eng, self.sem, self.n = eng, sem, 0

    def step(self, instruction):
        instruction.then_inc(self.sem, 1)
        self.n += 1
        return self.n

    def after(self, n):
        self.eng.wait_ge(self.sem, n)


def plan():
    tile, item, block = {}, {}, {}
    blocks = chunks = 0
    order = []

    def tiles(*names):
        for n in names:
            assert n not in tile
            tile[n] = len(tile_list)
            tile_list.append(n)

    tile_list = []

    def load(name, is_block):
        nonlocal blocks, chunks
        item[name] = len(order)
        if is_block:
            block[name] = blocks
            blocks += 1
            order.append(("block", blocks))
        elif name[3] < CPM - 1:
            chunks += 1
            order.append(("ada", chunks))
        else:
            order.append(("tile", tile[name[:3]]))

    def load_ada(layer, i):
        for c in range(CPM):
            load(("ada", layer, i, c), False)

    tiles("vec", "cT")
    tiles(*[("x", k) for k in range(KT)])
    tiles(("stat", 0), ("ada", 0, SH1), ("ada", 0, SC1))
    tiles(*[("conv_hist", j) for j in range(AT)], "pool_hist")
    for b, (kind, m) in enumerate(IN_AB):
        tiles((kind, m), (kind, m + 1))
        if b in MOD_AFTER:
            tiles(("ada", 0, MOD_AFTER[b]))
    tiles("conv_pe", *[("pool_mix", g) for g in range(AT)], "conv_mean")
    tiles(("ada", 0, GT2), ("ada", 1, SH1), "conv_var", ("ada", 1, SC1), ("ada", 1, SH2))
    tiles("conv_state", "pool_state")
    tiles(*[("out_ab", m) for m in range(KT)], ("ada", 1, SC2), ("stat", 1))
    tiles(*[("ffn", 0, q, m) for q in range(QUARTERS) for m in range(2 * KT)])
    tiles(("ada", 1, GT1), ("stat", 2), "ws", ("u", 0), ("u", 1))
    for b in range(OUT_BLOCKS):
        tiles(("v", b), ("v_sample", b))
    tiles(*[("u", m) for m in range(2, KT)], "rep", *[("spatial", h) for h in range(HEADS)])
    tiles(*[("out_c", m) for m in range(KT)], ("ada", 1, GT2), ("stat", 3))
    tiles(*[("ffn", 1, q, m) for q in range(QUARTERS) for m in range(2 * KT)])
    tiles(("stat", 4), *[("y", c) for c in range(CHUNKS)], ("y_sample", 0), ("y_sample", 1))

    load_ada(0, SH1)
    load(("in_ab", 0), True)
    load_ada(0, SC1)
    load(("in_ab", 1), True)
    for b in range(2, MIX_BLOCKS_IN):
        load(("in_ab", b), True)
        if b - 1 in MOD_AFTER:
            load_ada(0, MOD_AFTER[b - 1])
    load(("out_ab", 0), True)
    load(("out_ab", 1), True)
    load_ada(0, GT2)
    load_ada(1, SH1)
    load_ada(1, SC1)
    load_ada(1, SH2)
    for b in range(2, OUT_BLOCKS):
        load(("out_ab", b), True)
    for layer, gate in ((0, SC2), (1, GT2)):
        for q in range(QUARTERS):
            for j in range(FFN_BLOCKS):
                load(("ffn", layer, q, j), True)
                if q == 0 and j == 0:
                    load_ada(1, gate)
        if layer == 0:
            load(("in_u", 0), True)
            load_ada(1, GT1)
            for b in range(OUT_BLOCKS):
                load(("in_v", b), True)
            for b in range(1, OUT_BLOCKS):
                load(("in_u", b), True)
            for b in range(OUT_BLOCKS):
                load(("out_c", b), True)
    last = {("in_ab", b): tile[(kind, m + 1)] for b, (kind, m) in enumerate(IN_AB)}
    for b in range(OUT_BLOCKS):
        last[("in_v", b)] = tile[("v_sample", b)]
        for name, t in (("out_ab", "out_ab"), ("out_c", "out_c"), ("in_u", "u")):
            last[(name, b)] = tile[(t, 2 * b + 1)]
    last_tile = {n: last[name] if name in last else tile[(*name[:3], 2 * name[3] + 1)] for name, n in block.items()}
    return tile, item, block, last_tile, order


def hybrid_decoder_step(nc, I, O):
    tile_of, item_of, block_of, last_tile_of, order = plan()
    ctx = ExitStack()
    with ctx:
        def sb(name, shape, dt=F32, where=ctx):
            return where.enter_context(nc.sbuf_tensor(name, shape, dt))

        def sem(name):
            return ctx.enter_context(nc.semaphore(name))

        x = sb("x", [P, KT, 2, HALF])
        act_hi = sb("act_hi", [P, KT, 2, HALF], F32R)
        act_lo = sb("act_lo", [P, KT, 2, HALF], F32R)
        in_s_hi = sb("in_s_hi", [P, KT, NS], F32R)
        in_s_lo = sb("in_s_lo", [P, KT, NS], F32R)
        w_hi = sb("w_hi", [P, 2, KT, BN], F32R)
        w_lo = sb("w_lo", [P, 2, KT, BN], F32R)
        raw = sb("raw", [P, RAW, KT * BN])
        work = sb("work", [P, 2, 2, HALF])
        piece = sb("piece", [P, 2, 2, HALF])
        sq = sb("sq", [P, 2, 2, HALF])
        ss = sb("ss", [P, 2, HALF])
        rstd = sb("rstd", [P, 2, HALF])
        gated_s = sb("gated_s", [P, 2, HS * 2])
        scaled_s = sb("scaled_s", [P, 2, NS])
        ident = sb("ident", [P, P])
        ones_d = sb("ones_d", [P, P])
        ones_a = sb("ones_a", [P, P])
        eps = sb("eps", [P, 1])
        NVEC = 4 * KT + KT + 4 * AT
        NB_ADA = 2 * NMOD * KT
        NTAP = TAPS * AT
        vec = sb("vec", [P, NVEC + NB_ADA + NTAP])
        cT = sb("cT", [P, KT, 32])
        mod_t = sb("mod_t", [P, KT, 32])
        mod = sb("mod", [P, 2, NMOD, KT, NCOND])
        scale = sb("scale", [P, KT, NCOND])
        inv_count = sb("inv_count", [P, AT, 16])
        w_pool_sb = sb("w_pool_sb", [P, AT, P])
        replicate = sb("replicate", [P, BATCH_S, SEQ_S])
        same_seq = sb("same_seq", [NS, BATCH_S])
        lnst = sb("lnst", [P, CHUNKS + 1, 4])

        g_mix_v = vec[:, 0:2 * KT].rearrange("p (l k) -> p l k", l=2)
        g_ffn_v = vec[:, 2 * KT:4 * KT].rearrange("p (l k) -> p l k", l=2)
        g_final_v = vec[:, 4 * KT:5 * KT]
        b_dw_v, g_cln_v, b_cln_v, s_pool_v = [vec[:, 5 * KT + i * AT:5 * KT + (i + 1) * AT] for i in range(4)]
        b_ada_v = vec[:, NVEC:NVEC + NB_ADA].rearrange("p (l i k) -> p l i k", l=2, i=NMOD)
        w_dw_v = vec[:, NVEC + NB_ADA:].rearrange("p (t j) -> p t j", j=AT)

        with ExitStack() as zone:
            a_ext = sb("a_ext", [P, AT, HIST + SEQ], where=zone)
            a_ext_s = sb("a_ext_s", [P, AT, BATCH_S, HIST + SEQ_S], where=zone)
            p_ext = sb("p_ext", [P, AT, PHIST + SEQ], where=zone)
            p_ext_s = sb("p_ext_s", [P, AT, BATCH_S, PHIST + SEQ_S], where=zone)
            with ExitStack() as early:
                x_rows = sb("x_rows", [P, CHUNKS, D], where=early)
                xs_rows = sb("xs_rows", [HS, 2, D], where=early)
                c_rows = sb("c_rows", [32, D], where=early)
                vec_rows = sb("vec_rows", [P, 3, P], where=early)
                conv_rows = sb("conv_rows", [4 * HIST, 2, DA], where=early)
                pool_rows = sb("pool_rows", [BATCH_S * PHIST, DA], where=early)
            with ExitStack() as late:
                acc = sb("acc", [P, AT, 2, HALF], where=late)
                diag = sb("diag", [P, DIAGS, P], where=late)
                acc_odd = sb("acc_odd", [P, 2, SEQ], where=late)
                win = sb("win", [P, AT, 2, HALF], where=late)
                sum_p = sb("sum_p", [P, 2, PHIST + SEQ], where=late)
                sum_s = sb("sum_s", [P, 2, BATCH_S, PHIST + SEQ_S], where=late)
                new_s = sb("new_s", [P, 2, AT, NS], where=late)
                prod = sb("prod", [P, SEQ_S, BATCH_S, TAPS], where=late)
        with ExitStack() as zone:
            f_hi = sb("f_hi", [P, KT, 2, HALF], F32R, where=zone)
            f_lo = sb("f_lo", [P, KT, 2, HALF], F32R, where=zone)
        with ExitStack() as zone:
            u = sb("u", [P, KT, 2, HALF], where=zone)
            v = sb("v", [P, CHUNKS, D], where=zone)
            v_s = sb("v_s", [NS, D], where=zone)
            ws_t = sb("ws_t", [P, HEADS, CHUNK], where=zone)
            b_s = sb("b_s", [P, HEADS, CHUNK], where=zone)
            g_v = sb("g_v", [P, D], where=zone)
            b_v = sb("b_v", [P, D], where=zone)
            ws_seq = sb("ws_seq", [NS, HEADS, BATCH_S, SEQ_S], where=zone)
        ws_rows = v[:, 0, :].rearrange("p (h s) -> p h s", h=HEADS)
        with ExitStack() as zone:
            y_t = sb("y_t", [P, KT, 2, HALF], where=zone)
            y_rows = sb("y_rows", [P, CHUNKS, D], where=zone)
            ys_rows = sb("ys_rows", [HS, 2, D], where=zone)
        state_rows = win[0:32].rearrange("p j h t -> p (j h t)")[:, 0:4 * DA].rearrange("p (i c) -> p i c", i=4)

        psum = ctx.enter_context(nc.psum_tensor("psum", [P, 2 * PAIRS, 512], F32))

        def pair(t):
            return psum[:, 2 * (t % PAIRS):2 * (t % PAIRS) + 2, :]

        def uses(t):
            return t // PAIRS + 1

        def full(eng, t, per=None):
            eng.wait_ge(psum_full[t % PAIRS], uses(t) if per is None else per + uses(t))

        def freed(eng, t, per=None):
            eng.wait_ge(psum_free[t % PAIRS], uses(t) if per is None else per + uses(t))

        def prompt(ap):
            return ap[:, :, 0:HP]

        def sample(ap):
            return ap[:, :, HP:HALF].rearrange("p h (b t) -> p h b t", t=SEQ_S)

        def per_seq(ap9):
            return ap9[:, 1:NCOND].rearrange("p (h b) -> p h b", h=2).unsqueeze(3).broadcast_to([P, 2, HB, SEQ_S])

        def flat(ap):
            return ap.rearrange("p h t -> p (h t)")

        psum_full = [sem(f"psum_full{i}") for i in range(PAIRS)]
        psum_free = [sem(f"psum_free{i}") for i in range(PAIRS)]
        raw_full = [sem(f"raw_full{i}") for i in range(RAW)]
        w_hi_ready, w_lo_ready, ada_used = sem("w_hi_ready"), sem("w_lo_ready"), sem("ada_used")
        vec_loaded, c_loaded, x_loaded, hist_loaded, pool_w_loaded = (
            sem("vec_loaded"), sem("c_loaded"), sem("x_loaded"), sem("hist_loaded"), sem("pool_w_loaded"))
        odd_loaded = sem("odd_loaded")
        pool_step, act_step, dve_step = sem("pool_step"), sem("act_step"), sem("dve_step")
        consts_ready, c_zeroed, pads_ready = sem("consts_ready"), sem("c_zeroed"), sem("pads_ready")
        c_sigmoid, c_silu = sem("c_sigmoid"), sem("c_silu")
        sq_ready, ss_added, root_ready = sem("sq_ready"), sem("ss_added"), sem("root_ready")
        piece_ready, piece_hi, piece_lo = sem("piece_ready"), sem("piece_hi"), sem("piece_lo")
        x_prompt_done, x_sample_done = sem("x_prompt_done"), sem("x_sample_done")
        a_ready, conv_step = sem("a_ready"), sem("conv_step")
        p_ready, win_ready, pool_in_ready = sem("p_ready"), sem("win_ready"), sem("pool_in_ready")
        centred, norm_ready, silu_ready = sem("centred"), sem("norm_ready"), sem("silu_ready")
        diag_ready, diag_used, xr_ready, scale_ready = sem("diag_ready"), sem("diag_used"), sem("xr_ready"), sem("scale_ready")
        new_s_ready, in_s_ready = sem("new_s_ready"), sem("in_s_ready")
        out_stored, rows_stored, y_ready, ws_masked = sem("out_stored"), sem("rows_stored"), sem("y_ready"), sem("ws_masked")
        v_centred, v_sq, v_var, v_root, v_ready = (
            sem("v_centred"), sem("v_sq"), sem("v_var"), sem("v_root"), sem("v_ready"))

        U_MIX_IN, U_MIX_OUT, U_FFN_IN0, U_FFN0 = 0, KT, 2 * KT, 3 * KT
        U_ODD_IN = U_FFN0 + QUARTERS * KT
        U_ODD_OUT = U_ODD_IN + KT
        U_FFN_IN1 = U_ODD_OUT + KT
        U_FFN1 = U_FFN_IN1 + KT
        G_EVEN = 0
        G_FFN0 = KT
        G_ODD = G_FFN0 + QUARTERS * KT
        G_FFN1 = G_ODD + KT
        G_END = G_FFN1 + QUARTERS * KT
        STATE_STORES = 16 * (4 + 2)

        block = ctx.enter_context(nc.Block())

        @block.sync
        def _(sp):
            def buffer_free(i):
                if i >= RAW:
                    kind, n = order[i - RAW]
                    if kind == "tile":
                        sp.wait_ge(psum_full[n % PAIRS], uses(n))
                    else:
                        sp.wait_ge(w_lo_ready if kind == "block" else ada_used, n)

            def load(name, src, shape):
                i = item_of[name]
                buffer_free(i)
                dst = raw[:, i % RAW, :].rearrange(shape[0], **shape[1])
                sp.dma_start(dst, src).then_inc(raw_full[i % RAW], 16)

            def load_block(name, w, rows, cols):
                load(name, w[rows:rows + D, cols:cols + BN].rearrange("(k p) n -> p k n", p=P),
                     ("p (k n) -> p k n", {"k": KT}))

            def load_ada(layer, i):
                for c in range(CPM):
                    load(("ada", layer, i, c),
                         I["w_ada"][layer, 2 * P * c:2 * P * (c + 1), i * D:(i + 1) * D].rearrange("(k p) n -> p k n", p=P),
                         ("p (k n) -> p k n", {"k": 2}))

            def load_ffn(layer, modulation):
                w1, w2 = I["w_ffn1"][layer], I["w_ffn2"][layer]
                first = item_of[("ffn", layer, 0, 1)] - 1
                blocks = block_of[("ffn", layer, 0, 0)]
                load_block(("ffn", layer, 0, 0), w1, 0, 0)
                load_ada(1, modulation)
                for j in range(1, OUT_BLOCKS):
                    load_block(("ffn", layer, 0, j), w1, 0, j * BN)
                full(sp, tile_of[("ada", 1, modulation)])
                with sp.Fori(0, QUARTERS - 1) as q:
                    for j in range(FFN_BLOCKS):
                        i = first + OUT_BLOCKS + j
                        sp.wait_ge(w_lo_ready, q * FFN_BLOCKS + (blocks + j + 1))
                        if j < OUT_BLOCKS:
                            src = w2[bass.ds(q * D, D), j * BN:(j + 1) * BN]
                        else:
                            src = w1[:, bass.ds(q * D + (D + (j - OUT_BLOCKS) * BN), BN)]
                        sp.dma_start(raw[:, i % RAW, :].rearrange("p (k n) -> p k n", k=KT),
                                     src.rearrange("(k p) n -> p k n", p=P)).then_inc(raw_full[i % RAW], 16)
                for j in range(OUT_BLOCKS):
                    load_block(("ffn", layer, QUARTERS - 1, OUT_BLOCKS + j), w2, (QUARTERS - 1) * D, j * BN)

            sp.wait_ge(c_zeroed, 1)
            sp.dma_start(c_rows[0:1, :], I["c_prompt"]).then_inc(c_loaded, 16)
            sp.dma_start(c_rows[1:NCOND, :], I["c_sample"]).then_inc(c_loaded, 16)
            sp.dma_start(x_rows[:, :, :], I["x_prompt"][0].rearrange("(c p) d -> p c d", p=P)).then_inc(x_loaded, 16)
            sp.dma_start(xs_rows[:, :, :], I["x_sample"].rearrange("(h b) t d -> (b t) h d", h=2)).then_inc(x_loaded, 16)
            w_in = I["w_in_ab"][0]

            def load_in(b):
                kind, m = IN_AB[b]
                load_block(("in_ab", b), w_in, 0, {"value": 0, "gate": DA, "pool": 2 * DA}[kind] + m * P)

            load_ada(0, SH1)
            load_in(0)
            load_ada(0, SC1)
            load_in(1)
            for b in range(2, MIX_BLOCKS_IN):
                load_in(b)
                if b - 1 in MOD_AFTER:
                    load_ada(0, MOD_AFTER[b - 1])
            keep = HIST - SEQ_S
            sp.dma_start(O["new_conv_sample"][0, :, 0:keep, :], I["state_conv"][0, :, SEQ_S:HIST, :]).then_inc(out_stored, 16)
            keep_p = PHIST - SEQ_S
            sp.dma_start(O["new_pool_sample"][0, :, 0:keep_p, :], I["state_pool"][0, :, SEQ_S:PHIST, :]).then_inc(out_stored, 16)
            for b in range(2):
                load_block(("out_ab", b), I["w_out_ab"][0], 0, b * BN)
            load_ada(0, GT2)
            load_ada(1, SH1)
            load_ada(1, SC1)
            load_ada(1, SH2)
            for b in range(2, OUT_BLOCKS):
                load_block(("out_ab", b), I["w_out_ab"][0], 0, b * BN)
            freed(sp, tile_of["conv_state"])
            freed(sp, tile_of["pool_state"])
            sp.dma_start(O["new_conv_prompt"][0, 0], state_rows[NS - HIST:NS, 0, :]).then_inc(out_stored, 16)
            sp.dma_start(O["new_conv_sample"][0, :, keep:HIST, :], state_rows[0:NS, 1, :]).then_inc(out_stored, 16)
            sp.dma_start(O["new_pool_prompt"][0, 0], state_rows[NS - PHIST:NS, 2, :]).then_inc(out_stored, 16)
            sp.dma_start(O["new_pool_sample"][0, :, keep_p:PHIST, :], state_rows[0:NS, 3, :]).then_inc(out_stored, 16)
            load_ffn(0, SC2)
            load_block(("in_u", 0), I["w_in_c"][0], 0, 0)
            load_ada(1, GT1)
            sp.wait_ge(x_sample_done, G_ODD)
            sp.dma_start(ws_rows, I["w_spatial"][0].rearrange("h t s -> t h s")).then_inc(odd_loaded, 16)
            sp.dma_start(b_s[:, :, :], I["b_spatial"][0].partition_broadcast(P)).then_inc(odd_loaded, 16)
            sp.dma_start(g_v[:, :], I["g_v_ln"][0].partition_broadcast(P)).then_inc(odd_loaded, 16)
            sp.dma_start(b_v[:, :], I["b_v_ln"][0].partition_broadcast(P)).then_inc(odd_loaded, 16)
            for b in range(OUT_BLOCKS):
                load_block(("in_v", b), I["w_in_c"][0], 0, D + b * BN)
            for b in range(1, OUT_BLOCKS):
                load_block(("in_u", b), I["w_in_c"][0], 0, b * BN)
            for b in range(OUT_BLOCKS):
                load_block(("out_c", b), I["w_out_c"][0], 0, b * BN)
            sp.wait_ge(v_ready, CHUNKS + 1)
            sp.dma_start(O["new_v_sample"][0].rearrange("b t d -> (b t) d"), v_s[:, :]).then_inc(out_stored, 16)
            load_ffn(1, GT2)
            for c in range(CHUNKS):
                freed(sp, tile_of[("y", c)])
                sp.dma_start(O["y_prompt"][0, c * CHUNK:(c + 1) * CHUNK, :], y_rows[:, c, :]).then_inc(rows_stored, 16)
            for h in range(2):
                freed(sp, tile_of[("y_sample", h)])
            sp.dma_start(O["y_sample"].rearrange("(h b) t d -> (b t) h d", h=2), ys_rows[:, :, :]).then_inc(rows_stored, 16)
            sp.wait_ge(out_stored, STATE_STORES + 16)
            sp.wait_ge(rows_stored, 16 * (CHUNKS + 1))

        @block.gpsimd
        def _(pool):
            own = Own(pool, pool_step)
            g = nc.gpsimd
            g.memset(c_rows[:, :], 0.0).then_inc(c_zeroed, 1)
            zero = own.step(g.memset(ident[:, :], 0.0))
            own.after(zero)
            g.affine_select(out=ident[:, :], in_=ident[:, :], compare_op=ALU.not_equal, fill=1.0, base=0,
                            pattern=[[-1, P]], channel_multiplier=1).then_inc(consts_ready, 1)
            g.memset(ones_d[:, :], 1.0 / D).then_inc(consts_ready, 1)
            g.memset(ones_a[:, :], 1.0 / DA).then_inc(consts_ready, 1)
            g.memset(eps[:, :], EPS).then_inc(consts_ready, 1)
            g.memset(a_ext[:, :, 0:HIST], 0.0).then_inc(pads_ready, 1)
            g.memset(p_ext[:, :, 0:PHIST], 0.0).then_inc(pads_ready, 1)
            for i, w in enumerate(WINDOWS):
                full = own.step(g.memset(inv_count[:, i, :], 1.0 / w))
                own.after(full)
                for t in range(w - 1):
                    last = own.step(g.memset(inv_count[:, i, t:t + 1], 1.0 / (t + 1)))
            own.after(last)
            m = own.step(g.memset(replicate[:, :, :], 0.0))
            own.after(m)
            m = own.step(g.affine_select(out=replicate[:, :, :], in_=replicate[:, :, :], compare_op=ALU.not_equal, fill=1.0,
                                         base=0, pattern=[[0, BATCH_S], [-1, SEQ_S]], channel_multiplier=1))
            m = own.step(g.memset(same_seq[:, :], 1.0))
            own.after(m)
            m = own.step(g.affine_select(out=same_seq[:, :], in_=same_seq[:, :], compare_op=ALU.is_ge, fill=0.0,
                                         base=0, pattern=[[-SEQ_S, BATCH_S]], channel_multiplier=1))
            own.after(m)
            g.affine_select(out=same_seq[:, :], in_=same_seq[:, :], compare_op=ALU.is_ge, fill=0.0,
                            base=SEQ_S - 1, pattern=[[SEQ_S, BATCH_S]], channel_multiplier=-1).then_inc(consts_ready, 1)
            def norm_pieces_samples(layer, sh, unit, nth):
                pool.wait_ge(scale_ready, nth + 1)
                for k in range(KT):
                    n = unit + k
                    pool.wait_ge(xr_ready, nth * KT + k + 1)
                    tmp = scaled_s[:, k % 2, :].rearrange("p (h b t) -> p h b t", h=2, t=SEQ_S)
                    done = own.step(g.tensor_tensor(tmp, sample(work[:, k % 2]), per_seq(scale[:, k, :]), ALU.mult))
                    own.after(done)
                    if n >= 2:
                        pool.wait_ge(piece_lo, n - 1)
                    g.tensor_tensor(sample(piece[:, n % 2]), tmp, per_seq(mod[:, layer, sh, k, :]), ALU.add)\
                     .then_inc(piece_ready, 1)

            norm_pieces_samples(0, SH1, U_MIX_IN, 0)
            pool.wait_ge(pads_ready, 2)
            freed(pool, tile_of["pool_hist"])
            for i in range(AT):
                pool.wait_ge(p_ready, i + 1)
                freed(pool, tile_of[("pool", i)])
                src_p, src_s = p_ext[:, i, :], p_ext_s[:, i, :, :]
                shift = 1
                for level in range(i + 1):
                    lo = 2 * shift - 1
                    dst_p, dst_s = sum_p[:, level % 2, :], sum_s[:, level % 2, :, :]
                    if level == i:
                        own.step(g.tensor_tensor(
                            prompt(win[:, i]), src_p[:, PHIST:PHIST + SEQ].rearrange("p (h t) -> p h t", h=2),
                            src_p[:, PHIST - shift:PHIST + SEQ - shift].rearrange("p (h t) -> p h t", h=2), ALU.add))
                        own.after(own.n)
                        g.tensor_tensor(
                            sample(win[:, i]),
                            src_s[:, :, PHIST:PHIST + SEQ_S].rearrange("p (h b) t -> p h b t", h=2),
                            src_s[:, :, PHIST - shift:PHIST + SEQ_S - shift].rearrange("p (h b) t -> p h b t", h=2),
                            ALU.add).then_inc(win_ready, 1)
                        pool.wait_ge(win_ready, i + 1)
                    else:
                        own.step(g.tensor_tensor(dst_p[:, lo:], src_p[:, lo:], src_p[:, lo - shift:PHIST + SEQ - shift],
                                                 ALU.add))
                        own.step(g.tensor_tensor(dst_s[:, :, lo:], src_s[:, :, lo:],
                                                 src_s[:, :, lo - shift:PHIST + SEQ_S - shift], ALU.add))
                        own.after(own.n)
                    src_p, src_s = dst_p, dst_s
                    shift *= 2
            norm_pieces_samples(0, SH2, U_FFN_IN0, 1)
            norm_pieces_samples(1, SH1, U_ODD_IN, 2)
            freed(pool, tile_of["ws"])
            g.affine_select(out=ws_t[:, :, :], in_=ws_t[:, :, :], compare_op=ALU.is_ge, fill=0.0, base=0,
                            pattern=[[0, HEADS], [1, CHUNK]], channel_multiplier=-1).then_inc(ws_masked, 1)
            norm_pieces_samples(1, SH2, U_FFN_IN1, 3)

        @block.tensor
        def _(pe):
            def take(t):
                if t >= PAIRS:
                    pe.wait_ge(psum_free[t % PAIRS], t // PAIRS)
                return pair(t)

            def give(t, mm):
                mm.then_inc(psum_full[t % PAIRS], 1)

            def product(out, left, right, start, stop):
                for n, (a, b) in enumerate(((0, 0), (0, 1), (1, 0))):
                    mm = nc.tensor.matmul(out, left[a], right[b], start=start and n == 0, stop=stop and n == 2,
                                          skip_group_check=True)
                return mm

            def block_product(b, t, hi, lo, units, k_order=range(KT), per_b=None, per_t=None, per_u=None):
                slot = b % 2

                def at(n, per):
                    return n if per is None else per + n

                pe.wait_ge(w_lo_ready, at(b + 1, per_b))
                for m in range(2):
                    if t + m >= PAIRS:
                        pe.wait_ge(psum_free[(t + m) % PAIRS], at((t + m) // PAIRS, per_t))
                for n, k in enumerate(k_order):
                    if units is not None:
                        pe.wait_ge(piece_lo, at(units + n + 1, per_u))
                    for m in range(2):
                        out = pair(t + m)
                        cols = slice(m * P, (m + 1) * P)
                        for i, (a, c) in enumerate(((w_hi, hi), (w_hi, lo), (w_lo, hi))):
                            for h in range(2):
                                mm = nc.tensor.matmul(out[:, h, 0:HALF], a[:, slot, k, cols], c[:, k, h, :],
                                                      start=(n == 0 and i == 0), stop=(n == KT - 1 and i == 2),
                                                      skip_group_check=True)
                        if n == KT - 1:
                            if m == 0:
                                mm.then_inc(psum_full[t % PAIRS], 1)
                            else:
                                mm.then_inc(psum_full[(t + 1) % PAIRS], 1)

            def named_block(name, t_name, hi, lo, units, k_order=range(KT)):
                block_product(block_of[name], tile_of[t_name], hi, lo, units, k_order)

            def ada(layer, i):
                t = tile_of[("ada", layer, i)]
                out = take(t)
                for c in range(CPM):
                    it = item_of[("ada", layer, i, c)]
                    pe.wait_ge(raw_full[it % RAW], 16 * (it // RAW + 1))
                    chunk = raw[:, it % RAW, :].rearrange("p (k j g f) -> p k g j f", k=2, g=4, f=32)
                    for kk in range(2):
                        k = 2 * c + kk
                        for grp in range(4):
                            mm = nc.tensor.matmul(out[32 * grp:32 * grp + 32, 0, 0:2 * P], cT[:, k, :], chunk[:, kk, grp],
                                                  start=(k == 0), stop=(k == KT - 1), skip_group_check=True)
                    if c < CPM - 1:
                        mm.then_inc(ada_used, 1)
                give(t, mm)

            def stat(t, ones, count):
                out = take(t)
                pe.wait_ge(ss_added, count)
                for h in range(2):
                    mm = nc.tensor.matmul(out[:, h, 0:HALF], ones[:, :], ss[:, h, :], start=True, stop=True)
                give(t, mm)

            def ffn(layer, units_in, units):
                b0, t0 = block_of[("ffn", layer, 0, 0)], tile_of[("ffn", layer, 0, 0)]
                with pe.Fori(0, QUARTERS) as q:
                    per_b, per_t, per_u = q * FFN_BLOCKS, q * (2 * FFN_BLOCKS // PAIRS), q * KT
                    for j in range(OUT_BLOCKS):
                        block_product(b0 + j, t0 + 2 * j, act_hi, act_lo, None if j else units_in, per_b=per_b,
                                      per_t=per_t, per_u=q * 0)
                    for j in range(OUT_BLOCKS, FFN_BLOCKS):
                        block_product(b0 + j, t0 + 2 * j, f_hi, f_lo, None if j > OUT_BLOCKS else units, per_b=per_b,
                                      per_t=per_t, per_u=per_u)

            pe.wait_ge(consts_ready, 5)
            pe.wait_ge(vec_loaded, 16 * 9)
            out = take(tile_of["vec"])
            at = 0
            for i, n in enumerate((NVEC, NB_ADA, NTAP)):
                mm = nc.tensor.transpose(out[:, 0, at:at + n], vec_rows[0:n, i, :], ident[0:n, 0:n])
                at += n
            give(tile_of["vec"], mm)
            pe.wait_ge(c_silu, 1)
            out = take(tile_of["cT"])
            for k in range(KT):
                mm = nc.tensor.transpose(out[:, 0, 32 * k:32 * k + 32], c_rows[:, k * P:(k + 1) * P], ident[0:32, 0:32])
            give(tile_of["cT"], mm)
            pe.wait_ge(x_loaded, 32)
            for k in range(KT):
                out = take(tile_of[("x", k)])
                for c in range(CHUNKS):
                    nc.tensor.transpose(out[:, c // 2, (c % 2) * CHUNK:(c % 2 + 1) * CHUNK], x_rows[:, c, k * P:(k + 1) * P],
                                        ident[:, :])
                for h in range(2):
                    mm = nc.tensor.transpose(out[:, h, HP:HALF], xs_rows[:, h, k * P:(k + 1) * P], ident[0:HS, 0:HS])
                give(tile_of[("x", k)], mm)
            stat(tile_of[("stat", 0)], ones_d, KT)
            freed(pe, tile_of["cT"])
            ada(0, SH1)
            ada(0, SC1)
            pe.wait_ge(hist_loaded, 48)
            for j in range(AT):
                out = take(tile_of[("conv_hist", j)])
                for h in range(2):
                    mm = nc.tensor.transpose(out[:, h, 0:HB * HIST], conv_rows[:, h, j * P:(j + 1) * P],
                                             ident[0:HB * HIST, 0:HB * HIST])
                give(tile_of[("conv_hist", j)], mm)
            out = take(tile_of["pool_hist"])
            n = BATCH_S * PHIST
            for j in range(AT):
                mm = nc.tensor.transpose(out[:, 0, j * n:(j + 1) * n], pool_rows[:, j * P:(j + 1) * P], ident[0:n, 0:n])
            give(tile_of["pool_hist"], mm)
            for b, name in enumerate(IN_AB):
                named_block(("in_ab", b), name, act_hi, act_lo, None if b else U_MIX_IN)
                if b in MOD_AFTER:
                    ada(0, MOD_AFTER[b])
            out = take(tile_of["conv_pe"])
            pe.wait_ge(a_ready, 1)
            freed(pe, tile_of[("value", 0)])
            for tap in range(TAPS):
                pe.wait_ge(diag_ready, tap + 1)
                for h in range(2):
                    mm = nc.tensor.matmul(out[:, h, 0:HP], diag[:, tap % DIAGS, :],
                                          a_ext[:, 0, tap + h * HP:tap + (h + 1) * HP], start=(tap == 0),
                                          stop=(tap == TAPS - 1), skip_group_check=True)
                mm.then_inc(diag_used if tap < TAPS - 1 else psum_full[tile_of["conv_pe"] % PAIRS], 1)
            pe.wait_ge(pool_w_loaded, 16)
            for i in range(AT):
                out = take(tile_of[("pool_mix", i)])
                pe.wait_ge(pool_in_ready, i + 1)
                for h in range(2):
                    mm = nc.tensor.matmul(out[:, h, 0:HALF], w_pool_sb[:, i, :], win[:, i, h, :], start=True, stop=True)
                give(tile_of[("pool_mix", i)], mm)
            stat(tile_of["conv_mean"], ones_a, KT + AT)
            ada(0, GT2)
            ada(1, SH1)
            stat(tile_of["conv_var"], ones_a, KT + 2 * AT)
            ada(1, SC1)
            ada(1, SH2)
            out = take(tile_of["conv_state"])
            pe.wait_ge(new_s_ready, 2)
            for j in range(AT):
                nc.tensor.transpose(out[0:NS, 0, j * P:(j + 1) * P], a_ext[:, j, SEQ + HIST - NS:SEQ + HIST], ident[:, :])
                mm = nc.tensor.transpose(out[0:NS, 1, j * P:(j + 1) * P], new_s[:, 0, j, :], ident[:, :])
            give(tile_of["conv_state"], mm)
            out = take(tile_of["pool_state"])
            for j in range(AT):
                nc.tensor.transpose(out[0:NS, 0, j * P:(j + 1) * P], p_ext[:, j, SEQ + PHIST - NS:SEQ + PHIST], ident[:, :])
                mm = nc.tensor.transpose(out[0:NS, 1, j * P:(j + 1) * P], new_s[:, 1, j, :], ident[:, :])
            give(tile_of["pool_state"], mm)
            for b in range(OUT_BLOCKS):
                named_block(("out_ab", b), ("out_ab", 2 * b), act_hi, act_lo, None if b else U_MIX_OUT,
                            [*range(AT, KT), *range(AT)])
            ada(1, SC2)
            stat(tile_of[("stat", 1)], ones_d, 2 * KT + 2 * AT)
            ffn(0, U_FFN_IN0, U_FFN0)
            ada(1, GT1)
            stat(tile_of[("stat", 2)], ones_d, 3 * KT + 2 * AT)
            pe.wait_ge(odd_loaded, 64)
            out = take(tile_of["ws"])
            for h in range(HEADS):
                mm = nc.tensor.transpose(out[:, h // 4, (h % 4) * P:(h % 4 + 1) * P], ws_rows[:, h, :], ident[:, :])
            give(tile_of["ws"], mm)
            named_block(("in_u", 0), ("u", 0), act_hi, act_lo, U_ODD_IN)
            for b in range(OUT_BLOCKS):
                blk = block_of[("in_v", b)]
                pe.wait_ge(w_lo_ready, blk + 1)
                t = tile_of[("v", b)]
                out = take(t)
                for c in range(CHUNKS):
                    rows = slice((c % 2) * CHUNK, (c % 2 + 1) * CHUNK)
                    for k in range(KT):
                        mm = product(out[:, c // 2, (c % 2) * BN:(c % 2 + 1) * BN],
                                     (act_hi[:, k, c // 2, rows], act_lo[:, k, c // 2, rows]),
                                     (w_hi[:, blk % 2, k, :], w_lo[:, blk % 2, k, :]), k == 0, k == KT - 1)
                give(t, mm)
                t = tile_of[("v_sample", b)]
                out = take(t)
                pe.wait_ge(in_s_ready, 2)
                for k in range(KT):
                    mm = product(out[0:NS, 0, 0:BN], (in_s_hi[:, k, :], in_s_lo[:, k, :]),
                                 (w_hi[:, blk % 2, k, :], w_lo[:, blk % 2, k, :]), k == 0, k == KT - 1)
                give(t, mm)
            for b in range(1, OUT_BLOCKS):
                named_block(("in_u", b), ("u", 2 * b), act_hi, act_lo, None)
            out = take(tile_of["rep"])
            pe.wait_ge(ws_masked, 1)
            mm = nc.tensor.matmul(out[0:NS, 0, 0:HEADS * SEQ_S], replicate[:, :, :], ws_t[:, :, 0:SEQ_S], start=True, stop=True)
            give(tile_of["rep"], mm)
            pe.wait_ge(v_ready, CHUNKS + 1)
            freed(pe, tile_of["rep"])
            for h in range(HEADS):
                out = take(tile_of[("spatial", h)])
                cols = slice(h * P, (h + 1) * P)
                for c in range(CHUNKS):
                    nc.tensor.matmul(out[:, c // 2, (c % 2) * CHUNK:(c % 2 + 1) * CHUNK], v[:, c, cols], ws_t[:, h, :],
                                     start=True, stop=True, skip_group_check=True)
                for s in range(2):
                    mm = nc.tensor.matmul(out[:, s, HP:HALF], v_s[:, cols], ws_seq[:, h, s * HB:(s + 1) * HB, :],
                                          start=True, stop=True, skip_group_check=True)
                give(tile_of[("spatial", h)], mm)
            for b in range(OUT_BLOCKS):
                named_block(("out_c", b), ("out_c", 2 * b), act_hi, act_lo, None if b else U_ODD_OUT)
            ada(1, GT2)
            stat(tile_of[("stat", 3)], ones_d, 4 * KT + 2 * AT)
            ffn(1, U_FFN_IN1, U_FFN1)
            stat(tile_of[("stat", 4)], ones_d, 5 * KT + 2 * AT)
            pe.wait_ge(y_ready, KT)
            for c in range(CHUNKS):
                out = take(tile_of[("y", c)])
                for k in range(KT):
                    mm = nc.tensor.transpose(out[:, k // 4, (k % 4) * P:(k % 4 + 1) * P],
                                             y_t[:, k, c // 2, (c % 2) * CHUNK:(c % 2 + 1) * CHUNK], ident[:, :])
                give(tile_of[("y", c)], mm)
            for h in range(2):
                t = tile_of[("y_sample", h)]
                out = take(t)
                for k in range(KT):
                    mm = nc.tensor.transpose(out[0:HS, k // 4, (k % 4) * P:(k % 4 + 1) * P], y_t[:, k, h, HP:HALF],
                                             ident[:, :])
                give(t, mm)

        @block.scalar
        def _(act):
            own = Own(act, act_step)
            squares = [0]

            def weights_hi(b, i, t_used=None, per_b=None, per_i=None, per_t=None):
                def at(n, per):
                    return n if per is None else per + n
                act.wait_ge(raw_full[i % RAW], at(16 * (i // RAW + 1), per_i))
                if per_b is not None:
                    full(act, t_used, per_t)
                elif b >= 2:
                    full(act, last_tile_of[b - 2])
                nc.scalar.activation(w_hi[:, b % 2, :, :].rearrange("p k n -> p (k n)"), raw[:, i % RAW, :],
                                     ACT.Copy).then_inc(w_hi_ready, 1)

            def named_hi(name):
                weights_hi(block_of[name], item_of[name])

            def piece_to_hi(dst, n, per=None):
                act.wait_ge(piece_ready, n + 1 if per is None else per + (n + 1))
                nc.scalar.activation(flat(dst), flat(piece[:, n % 2]), ACT.Copy).then_inc(piece_hi, 1)

            def square(src, waits):
                n = squares[0]
                for s, c in waits:
                    act.wait_ge(s, c)
                if n >= 2:
                    act.wait_ge(ss_added, n - 1 + (AT if n >= KT else 0))
                nc.scalar.activation(flat(sq[:, n % 2]), flat(src), ACT.Square).then_inc(sq_ready, 1)
                squares[0] += 1

            def square_x(m, adds):
                square(x[:, m], [(x_prompt_done, adds + 1), (x_sample_done, adds + 1)])

            def norm_pieces_hi(layer, sh, unit, nth):
                act.wait_ge(scale_ready, nth + 1)
                for k in range(KT):
                    n = unit + k
                    act.wait_ge(xr_ready, nth * KT + k + 1)
                    if n >= 2:
                        act.wait_ge(piece_lo, n - 1)
                    done = own.step(nc.scalar.activation(prompt(piece[:, n % 2]), prompt(work[:, k % 2]), ACT.Identity,
                                                         bias=mod[:, layer, sh, k, 0:1], scale=scale[:, k, 0:1]))
                    own.after(done)
                    piece_to_hi(act_hi[:, k], n)

            def root(t, n):
                full(act, t)
                nc.scalar.activation(rstd[:, :, :], pair(t)[:, :, 0:HALF], ACT.Sqrt, bias=eps[:, 0:1]).then_inc(root_ready, 1)

            def relu(t, n, per_t=None, per_u=None):
                full(act, t, per_t)
                act.wait_ge(piece_ready, n - 1 if per_u is None else per_u + (n - 1))
                nc.scalar.activation(work[:, n % 2], pair(t)[:, :, 0:HALF], ACT.Relu).then_inc(psum_free[t % PAIRS], 1)

            def quarter(layer, q, units, adds=None, per=None, last=False, following=None):
                b0, i0, t0 = (block_of[("ffn", layer, q, 0)], item_of[("ffn", layer, q, 1)] - 1, tile_of[("ffn", layer, q, 0)])
                per_b = None if per is None else per * FFN_BLOCKS
                per_i = None if per is None else per * (16 * FFN_BLOCKS // RAW)
                per_t = None if per is None else per * (2 * FFN_BLOCKS // PAIRS)
                per_u = None if per is None else per * KT
                for j in range(FFN_BLOCKS):
                    if j < FFN_BLOCKS - 1 or not last:
                        weights_hi(b0 + j + 1, i0 + j + 1, t0 + 2 * j - 1, per_b, per_i, per_t)
                    elif following:
                        named_hi(following)
                    if last and j > OUT_BLOCKS:
                        for m in range(2 * (j - 1) - KT, 2 * j - KT):
                            square_x(m, adds + m)
                    if j < OUT_BLOCKS:
                        for m in range(2 * j, 2 * j + 2):
                            relu(t0 + m, units + m, per_t, per_u)
                            if m:
                                piece_to_hi(f_hi[:, m - 1], units + m - 1, per_u)
                    elif j == OUT_BLOCKS:
                        piece_to_hi(f_hi[:, KT - 1], units + KT - 1, per_u)

            def ffn(layer, units, adds, following=None):
                with act.Fori(0, QUARTERS - 1) as q:
                    quarter(layer, 0, units, per=q)
                done = (QUARTERS - 1) * KT
                quarter(layer, QUARTERS - 1, units + done, adds + done, last=True, following=following)
                for m in range(KT - 2, KT):
                    square_x(m, adds + done + m)

            act.dma_start(vec_rows[0:16, 0, :], I["g_mix"].rearrange("l (k p) -> (l k) p", p=P)).then_inc(vec_loaded, 16)
            act.dma_start(vec_rows[16:32, 0, :], I["g_ffn"].rearrange("l (k p) -> (l k) p", p=P)).then_inc(vec_loaded, 16)
            act.dma_start(vec_rows[32:40, 0, :], I["g_final"].rearrange("(k p) -> k p", p=P)).then_inc(vec_loaded, 16)
            for i, name in enumerate(("b_dw", "g_conv_ln", "b_conv_ln", "s_pool")):
                act.dma_start(vec_rows[40 + 4 * i:44 + 4 * i, 0, :],
                              I[name][0].rearrange("(k p) -> k p", p=P)).then_inc(vec_loaded, 16)
            act.dma_start(vec_rows[0:NB_ADA, 1, :], I["b_ada"].rearrange("l (k p) -> (l k) p", p=P)).then_inc(vec_loaded, 16)
            act.dma_start(vec_rows[0:NTAP, 2, :], I["w_dw"][0].rearrange("t (j p) -> (t j) p", p=P)).then_inc(vec_loaded, 16)
            act.dma_start(w_pool_sb[:, :, :], I["w_pool"][0].rearrange("g i o -> i g o")).then_inc(pool_w_loaded, 16)
            for h in range(2):
                act.dma_start(conv_rows[:, h, :], I["state_conv"][0, h * HB:(h + 1) * HB].rearrange("b r c -> (b r) c"))\
                   .then_inc(hist_loaded, 16)
            act.dma_start(pool_rows[:, :], I["state_pool"][0].rearrange("b r c -> (b r) c")).then_inc(hist_loaded, 16)

            act.wait_ge(c_loaded, 32)
            c_sig = sq[0:32].rearrange("p i h t -> p (i h t)")[:, 0:D]
            nc.scalar.activation(c_sig, c_rows[:, :], ACT.Sigmoid).then_inc(c_sigmoid, 1)
            full(act, tile_of["vec"])
            nc.scalar.activation(vec[:, :], pair(tile_of["vec"])[:, 0, 0:NVEC + NB_ADA + NTAP], ACT.Copy)\
              .then_inc(psum_free[tile_of["vec"] % PAIRS], 1)
            full(act, tile_of["cT"])
            nc.scalar.activation(cT.rearrange("p k c -> p (k c)"), pair(tile_of["cT"])[:, 0, 0:32 * KT], ACT.Copy)\
              .then_inc(psum_free[tile_of["cT"] % PAIRS], 1)
            for k in range(KT + 1):
                if k < KT:
                    t = tile_of[("x", k)]
                    full(act, t)
                    nc.scalar.activation(x[:, k], pair(t)[:, :, 0:HALF], ACT.Copy).then_inc(psum_free[t % PAIRS], 1)
                if k:
                    t = tile_of[("x", k - 1)]
                    square(x[:, k - 1], [(psum_free[t % PAIRS], uses(t))])
            act.wait_ge(consts_ready, 5)
            root(tile_of[("stat", 0)], 1)
            named_hi(("in_ab", 0))
            for j in range(AT):
                t = tile_of[("conv_hist", j)]
                full(act, t)
                nc.scalar.activation(a_ext_s[:, j, :, 0:HIST].rearrange("p (h b) r -> p h b r", h=2),
                                     pair(t)[:, :, 0:HB * HIST].rearrange("p h (b r) -> p h b r", r=HIST),
                                     ACT.Copy).then_inc(psum_free[t % PAIRS], 1)
            t = tile_of["pool_hist"]
            full(act, t)
            nc.scalar.activation(p_ext_s[:, :, :, 0:PHIST],
                                 pair(t)[:, 0, 0:AT * BATCH_S * PHIST].rearrange("p (j b r) -> p j b r", j=AT, r=PHIST),
                                 ACT.Copy).then_inc(psum_free[t % PAIRS], 1)
            norm_pieces_hi(0, SH1, U_MIX_IN, 0)
            for b in range(MIX_BLOCKS_IN):
                named_hi(("in_ab", b + 1) if b + 1 < MIX_BLOCKS_IN else ("out_ab", 0))
                kind, first = IN_AB[b]
                for m in range(first, first + 2):
                    t = tile_of[(kind, m)]
                    if kind == "gate":
                        full(act, t)
                        if m >= 2:
                            act.wait_ge(a_ready, m - 1)
                            freed(act, tile_of[("value", m - 2)])
                        nc.scalar.activation(work[:, m % 2], pair(t)[:, :, 0:HALF], ACT.Sigmoid).then_inc(psum_free[t % PAIRS], 1)
                    elif kind == "pool":
                        full(act, t)
                        nc.scalar.activation(p_ext[:, m, PHIST:PHIST + SEQ].rearrange("p (h t) -> p h t", h=2),
                                             prompt(pair(t)), ACT.Copy).then_inc(p_ready, 1)
                        nc.scalar.activation(p_ext_s[:, m, :, PHIST:PHIST + SEQ_S].rearrange("p (h b) t -> p h b t", h=2),
                                             sample(pair(t)), ACT.Copy).then_inc(psum_free[t % PAIRS], 1)
            named_hi(("out_ab", 1))
            for tap in range(TAPS):
                if tap >= DIAGS:
                    act.wait_ge(diag_used, tap - DIAGS + 1)
                nc.scalar.activation(diag[:, tap % DIAGS, :], ident[:, :], ACT.Copy, scale=w_dw_v[:, tap, 0:1])\
                  .then_inc(diag_ready, 1)
            t = tile_of["conv_pe"]
            full(act, t)
            nc.scalar.activation(prompt(acc[:, 0]), prompt(pair(t)), ACT.Identity, bias=b_dw_v[:, 0:1])\
              .then_inc(psum_free[t % PAIRS], 1)
            for g in range(AT):
                freed(act, tile_of[("pool", g)])
            nc.scalar.activation(new_s[:, 1].rearrange("p j (b t) -> p j b t", t=SEQ_S), p_ext_s[:, :, :, PHIST:PHIST + SEQ_S],
                                 ACT.Copy).then_inc(new_s_ready, 1)
            freed(act, tile_of[("value", AT - 1)])
            nc.scalar.activation(new_s[:, 0].rearrange("p j (b t) -> p j b t", t=SEQ_S), a_ext_s[:, :, :, HIST:HIST + SEQ_S],
                                 ACT.Copy).then_inc(new_s_ready, 1)
            for g in range(AT):
                t = tile_of[("pool_mix", g)]
                full(act, t)
                if g >= 2:
                    act.wait_ge(piece_ready, U_MIX_OUT + g - 1)
                nc.scalar.activation(work[:, g % 2], pair(t)[:, :, 0:HALF], ACT.Copy, scale=s_pool_v[:, g:g + 1])\
                  .then_inc(psum_free[t % PAIRS], 1)
                if g:
                    piece_to_hi(act_hi[:, AT + g - 1], U_MIX_OUT + g - 1)
            piece_to_hi(act_hi[:, KT - 1], U_MIX_OUT + AT - 1)
            for j in range(AT):
                t = tile_of["conv_mean"]
                square(acc[:, j], [(centred, j + 1)] if j < AT - 1 else [(psum_free[t % PAIRS], uses(t))])
            root(tile_of["conv_var"], 2)
            for i, name in enumerate(("conv_state", "pool_state")):
                t = tile_of[name]
                full(act, t)
                nc.scalar.activation(state_rows[:, 2 * i:2 * i + 2, :], pair(t)[0:NS], ACT.Copy).then_inc(psum_free[t % PAIRS], 1)
            for j in range(AT):
                act.wait_ge(norm_ready, j + 1)
                nc.scalar.activation(flat(sq[:, j % 2]), flat(work[:, j % 2]), ACT.Sigmoid, bias=b_cln_v[:, j:j + 1],
                                     scale=g_cln_v[:, j:j + 1]).then_inc(silu_ready, 1)
                piece_to_hi(act_hi[:, j], U_MIX_OUT + AT + j)

            def project(name, adds, following, split=1):
                for b in range(OUT_BLOCKS):
                    if b + 1 >= split:
                        named_hi((name, b + 1) if b + 1 < OUT_BLOCKS else following)
                    for m in range(2 * b - 2, 2 * b):
                        if m >= 0:
                            square_x(m, adds + m)
                for m in range(KT - 2, KT):
                    square_x(m, adds + m)

            project("out_ab", G_EVEN, ("ffn", 0, 0, 0), split=2)
            root(tile_of[("stat", 1)], 3)
            norm_pieces_hi(0, SH2, U_FFN_IN0, 1)
            ffn(0, U_FFN0, G_FFN0, ("in_u", 0))
            root(tile_of[("stat", 2)], 4)
            t = tile_of["ws"]
            full(act, t)
            nc.scalar.activation(ws_t.rearrange("p (a h) t -> p a (h t)", a=2), pair(t), ACT.Copy).then_inc(psum_free[t % PAIRS], 1)
            norm_pieces_hi(1, SH1, U_ODD_IN, 2)
            sequence = [("in_u", 0), *[("in_v", b) for b in range(OUT_BLOCKS)], *[("in_u", b) for b in range(1, OUT_BLOCKS)]]
            act.wait_ge(piece_lo, U_ODD_IN + KT)
            for dst, src in ((in_s_hi, act_hi), (in_s_lo, act_lo)):
                nc.scalar.activation(dst.rearrange("p k (h t) -> p k h t", h=2), src[:, :, :, HP:HALF].bitcast(F32),
                                     ACT.Copy).then_inc(in_s_ready, 1)
            for n, (name, b) in enumerate(sequence):
                named_hi(sequence[n + 1] if n + 1 < len(sequence) else ("out_c", 0))
                if name == "in_u":
                    for m in (2 * b, 2 * b + 1):
                        t = tile_of[("u", m)]
                        full(act, t)
                        nc.scalar.activation(u[:, m], pair(t)[:, :, 0:HALF], ACT.Copy).then_inc(psum_free[t % PAIRS], 1)
                else:
                    t = tile_of[("v", b)]
                    full(act, t)
                    nc.scalar.activation(v[:, :, b * BN:(b + 1) * BN].rearrange("p (a c) n -> p a c n", a=2),
                                         pair(t).rearrange("p a (c n) -> p a c n", n=BN), ACT.Copy).then_inc(psum_free[t % PAIRS], 1)
                    t = tile_of[("v_sample", b)]
                    full(act, t)
                    nc.scalar.activation(v_s[:, b * BN:(b + 1) * BN], pair(t)[0:NS, 0, 0:BN], ACT.Copy)\
                      .then_inc(psum_free[t % PAIRS], 1)
                for c in {4: (0,), 5: (1, 2), 6: (3, 4)}.get(n, ()):
                    act.wait_ge(v_centred, c + 1)
                    if c >= 2:
                        act.wait_ge(v_var, c - 1)
                    rows, src = (NS, v_s[:, :]) if c == CHUNKS else (P, v[:, c, :])
                    nc.scalar.activation((sq, work)[c % 2][0:rows].rearrange("p i h t -> p (i h t)")[:, 0:D], src,
                                         ACT.Square).then_inc(v_sq, 1)
                    act.wait_ge(v_var, c + 1)
                    nc.scalar.activation(lnst[0:rows, c, 2:3], lnst[0:rows, c, 1:2], ACT.Sqrt, bias=eps[0:rows, 0:1],
                                         scale=1.0 / D).then_inc(v_root, 1)
            for h in range(HEADS):
                piece_to_hi(act_hi[:, h], U_ODD_OUT + h)
            project("out_c", G_ODD, ("ffn", 1, 0, 0))
            root(tile_of[("stat", 3)], 5)
            norm_pieces_hi(1, SH2, U_FFN_IN1, 3)
            ffn(1, U_FFN1, G_FFN1)
            root(tile_of[("stat", 4)], 6)
            for k in range(KT):
                act.wait_ge(norm_ready, AT + k + 1)
                nc.scalar.activation(flat(y_t[:, k]), flat(work[:, k % 2]), ACT.Copy, scale=g_final_v[:, k:k + 1]).then_inc(y_ready, 1)
            for c in range(CHUNKS):
                t = tile_of[("y", c)]
                full(act, t)
                nc.scalar.activation(y_rows[:, c, :].rearrange("p (a n) -> p a n", a=2), pair(t), ACT.Copy)\
                  .then_inc(psum_free[t % PAIRS], 1)
            for h in range(2):
                t = tile_of[("y_sample", h)]
                full(act, t)
                nc.scalar.activation(ys_rows[:, h, :].rearrange("p (a n) -> p a n", a=2), pair(t)[0:HS], ACT.Copy)\
                  .then_inc(psum_free[t % PAIRS], 1)

        @block.vector
        def _(dve):
            own = Own(dve, dve_step)
            dv = nc.vector
            adds = [0]
            squares = [0]

            def weights_lo(b, i, per_b=None):
                dve.wait_ge(w_hi_ready, b + 1 if per_b is None else per_b + (b + 1))
                dv.tensor_tensor(w_lo[:, b % 2, :, :].rearrange("p k n -> p (k n)"), raw[:, i % RAW, :],
                                 w_hi[:, b % 2, :, :].rearrange("p k n -> p (k n)").bitcast(F32), ALU.subtract)\
                  .then_inc(w_lo_ready, 1)

            def named_lo(name):
                weights_lo(block_of[name], item_of[name])

            def piece_free(n, per=None):
                if per is not None or n >= 2:
                    dve.wait_ge(piece_lo, n - 1 if per is None else per + (n - 1))

            def piece_to_lo(dst_lo, dst_hi, n, per=None):
                dve.wait_ge(piece_hi, n + 1 if per is None else per + (n + 1))
                dv.tensor_tensor(flat(dst_lo), flat(piece[:, n % 2]), flat(dst_hi).bitcast(F32), ALU.subtract)\
                  .then_inc(piece_lo, 1)

            def sum_into_ss(src, first):
                n = adds[0]
                if n:
                    dve.wait_ge(ss_added, n)
                if first:
                    dv.tensor_copy(flat(ss), flat(src)).then_inc(ss_added, 1)
                else:
                    dv.tensor_tensor(flat(ss), flat(ss), flat(src), ALU.add).then_inc(ss_added, 1)
                adds[0] += 1

            def sum_square(first):
                n = squares[0]
                dve.wait_ge(sq_ready, n + 1)
                sum_into_ss(sq[:, n % 2], first)
                squares[0] += 1

            def inverse_root(t, n):
                dve.wait_ge(root_ready, n)
                dv.reciprocal(flat(rstd), flat(rstd)).then_inc(psum_free[t % PAIRS], 1)
                freed(dve, t)

            def modulation(layer, i):
                t = tile_of[("ada", layer, i)]
                full(dve, t)
                own.after(own.n)
                dv.transpose(mod_t.rearrange("p k c -> p (k c)"), pair(t)[:, 0, 0:2 * P]).then_inc(psum_free[t % PAIRS], 1)
                freed(dve, t)
                own.step(dv.tensor_tensor(mod[:, layer, i], mod_t[:, :, 0:NCOND],
                                          b_ada_v[:, layer, i, :].unsqueeze(2).broadcast_to([P, KT, NCOND]), ALU.add))

            def norm_pieces(layer, sc, gains, unit, nth):
                own.after(own.n)
                dv.scalar_tensor_tensor(scale[:, :, :], mod[:, layer, sc], 1.0,
                                        gains.unsqueeze(2).broadcast_to([P, KT, NCOND]), ALU.add, ALU.mult)\
                  .then_inc(scale_ready, 1)
                for k in range(KT):
                    if k >= 2:
                        dve.wait_ge(piece_hi, unit + k - 1)
                    dv.tensor_tensor(flat(work[:, k % 2]), flat(x[:, k]), flat(rstd), ALU.mult).then_inc(xr_ready, 1)
                    if k:
                        piece_to_lo(act_lo[:, k - 1], act_hi[:, k - 1], unit + k - 1)
                piece_to_lo(act_lo[:, KT - 1], act_hi[:, KT - 1], unit + KT - 1)

            def gated_add(a, m, t, layer, gate, per_a=None, per_t=None):
                def at(n):
                    return n if per_a is None else per_a + n
                gates = mod[:, layer, gate, m, :]
                full(dve, t, per_t)
                if a >= KT:
                    dve.wait_ge(x_prompt_done, at(a - KT + 1))
                    dve.wait_ge(x_sample_done, at(a - KT + 1))
                dv.scalar_tensor_tensor(prompt(x[:, m]), prompt(pair(t)), gates[:, 0:1], prompt(x[:, m]),
                                        ALU.mult, ALU.add).then_inc(x_prompt_done, 1)
                if a >= 2:
                    dve.wait_ge(x_sample_done, at(a - 1))
                tmp = gated_s[:, a % 2, :].rearrange("p (h b t) -> p h b t", h=2, t=SEQ_S)
                dve.wait_ge(x_prompt_done, at(a + 1))
                dv.tensor_tensor(tmp, sample(pair(t)), per_seq(gates), ALU.mult).then_inc(psum_free[t % PAIRS], 1)
                freed(dve, t, per_t)
                dv.tensor_tensor(sample(x[:, m]), sample(x[:, m]), tmp, ALU.add).then_inc(x_sample_done, 1)

            def quarter(layer, units, a0, q=0, per=None, last=False, following=None):
                b0, i0, t0 = (block_of[("ffn", layer, q, 0)], item_of[("ffn", layer, q, 1)] - 1, tile_of[("ffn", layer, q, 0)])
                per_b = None if per is None else per * FFN_BLOCKS
                per_t = None if per is None else per * (2 * FFN_BLOCKS // PAIRS)
                per_u = None if per is None else per * KT
                for j in range(FFN_BLOCKS):
                    if j < FFN_BLOCKS - 1 or not last:
                        weights_lo(b0 + j + 1, i0 + j + 1, per_b)
                    elif following:
                        named_lo(following)
                    for m in range(2 * j, 2 * j + 2):
                        if j < OUT_BLOCKS:
                            n = units + m
                            piece_free(n, per_u)
                            freed(dve, t0 + m, per_t)
                            dv.tensor_tensor(flat(piece[:, n % 2]), flat(work[:, n % 2]), flat(work[:, n % 2]), ALU.mult)\
                              .then_inc(piece_ready, 1)
                            if m:
                                piece_to_lo(f_lo[:, m - 1], f_hi[:, m - 1], n - 1, per_u)
                        else:
                            if m == KT:
                                piece_to_lo(f_lo[:, KT - 1], f_hi[:, KT - 1], units + KT - 1, per_u)
                            gated_add(a0 + m - KT, m - KT, t0 + m, layer, GT2, per_u, per_t)
                            if last and m > KT:
                                sum_square(m == KT + 1)
                if last:
                    sum_square(False)

            def ffn(layer, units, a0, following=None):
                with dve.Fori(0, QUARTERS - 1) as q:
                    quarter(layer, units, a0, per=q)
                done = (QUARTERS - 1) * KT
                quarter(layer, units + done, a0 + done, q=QUARTERS - 1, last=True, following=following)

            def project(name, a0, layer, following, split=1):
                for b in range(OUT_BLOCKS):
                    if b + 1 >= split:
                        named_lo((name, b + 1) if b + 1 < OUT_BLOCKS else following)
                    for m in range(2 * b, 2 * b + 2):
                        gated_add(a0 + m, m, tile_of[(name, m)], layer, GT1)
                        if m:
                            sum_square(m == 1)
                sum_square(False)

            dve.wait_ge(c_sigmoid, 1)
            c_sig = sq[0:32].rearrange("p i h t -> p (i h t)")[:, 0:D]
            dv.tensor_tensor(c_rows[:, :], c_rows[:, :], c_sig, ALU.mult).then_inc(c_silu, 1)
            for k in range(KT):
                sum_square(k == 0)
            freed(dve, tile_of["vec"])
            inverse_root(tile_of[("stat", 0)], 1)
            modulation(0, SH1)
            named_lo(("in_ab", 0))
            modulation(0, SC1)
            norm_pieces(0, SC1, g_mix_v[:, 0, :], U_MIX_IN, 0)
            dve.wait_ge(pads_ready, 2)
            conv_ops = [(j, tap) for j in range(1, AT) for tap in range(TAPS + 1)]
            at_op = [0]

            def convolve(count):
                for _ in range(count):
                    if at_op[0] == len(conv_ops):
                        return
                    j, tap = conv_ops[at_op[0]]
                    n = at_op[0]
                    at_op[0] += 1
                    even = prompt(acc[:, j])
                    odd = acc_odd[:, j % 2, :].rearrange("p (h t) -> p h t", h=2)
                    if n >= 2:
                        dve.wait_ge(conv_step, n - 1 if tap < TAPS else n)
                    if tap == TAPS:
                        dv.tensor_tensor(even, even, odd, ALU.add).then_inc(conv_step, 1)
                        continue
                    src = a_ext[:, j, tap:tap + SEQ].rearrange("p (h t) -> p h t", h=2)
                    w = w_dw_v[:, tap, j:j + 1]
                    dst = odd if tap % 2 else even
                    if tap == 0:
                        dv.tensor_scalar(dst, src, w, b_dw_v[:, j:j + 1], ALU.mult, ALU.add).then_inc(conv_step, 1)
                    elif tap == 1:
                        dv.tensor_scalar(dst, src, w, None, ALU.mult).then_inc(conv_step, 1)
                    else:
                        dv.scalar_tensor_tensor(dst, src, w, dst, ALU.mult, ALU.add).then_inc(conv_step, 1)

            def convolve_samples(j):
                own.after(own.n)
                for t in range(SEQ_S):
                    own.step(dv.tensor_tensor(prod[:, t], a_ext_s[:, j, :, t:t + TAPS],
                                              w_dw_v[:, :, j].unsqueeze(1).broadcast_to([P, BATCH_S, TAPS]), ALU.mult))
                own.after(own.n)
                own.step(dv.reduce_sum(gated_s[:, 0, :].rearrange("p (t b) -> p t b", t=SEQ_S), prod[:, :, :, :], AX_X))
                own.after(own.n)
                own.step(dv.tensor_scalar(sample(acc[:, j]),
                                          gated_s[:, 0, :].rearrange("p (t h b) -> p h b t", t=SEQ_S, h=2),
                                          b_dw_v[:, j:j + 1], None, ALU.add))

            def pool_input(g):
                w = WINDOWS[g]
                dve.wait_ge(win_ready, g + 1)
                own.after(own.n)
                head = own.step(dv.tensor_tensor(gated_s[:, 1, 0:16], win[:, g, 0, 0:16], inv_count[:, g, :], ALU.mult))
                own.after(head)
                body = own.step(dv.scalar_tensor_tensor(
                    prompt(win[:, g]), prompt(win[:, g]), 1.0 / w,
                    p_ext[:, g, PHIST:PHIST + SEQ].rearrange("p (h t) -> p h t", h=2), ALU.mult, ALU.subtract))
                own.step(dv.scalar_tensor_tensor(
                    sample(win[:, g]), sample(win[:, g]), 1.0 / w,
                    p_ext_s[:, g, :, PHIST:PHIST + SEQ_S].rearrange("p (h b) t -> p h b t", h=2), ALU.mult, ALU.subtract))
                own.after(own.n)
                dv.tensor_tensor(win[:, g, 0, 0:16], gated_s[:, 1, 0:16], p_ext[:, g, PHIST:PHIST + 16], ALU.subtract)\
                  .then_inc(pool_in_ready, 1)

            for b in range(MIX_BLOCKS_IN):
                named_lo(("in_ab", b + 1) if b + 1 < MIX_BLOCKS_IN else ("out_ab", 0))
                kind, first = IN_AB[b]
                for m in range(first, first + 2) if kind == "gate" else ():
                    t_a, t_g = tile_of[("value", m)], tile_of[("gate", m)]
                    full(dve, t_a)
                    freed(dve, t_g)
                    dv.tensor_tensor(a_ext[:, m, HIST:HIST + SEQ].rearrange("p (h t) -> p h t", h=2), prompt(pair(t_a)),
                                     prompt(work[:, m % 2]), ALU.mult).then_inc(a_ready, 1)
                    dve.wait_ge(a_ready, m + 1)
                    dv.tensor_tensor(a_ext_s[:, m, :, HIST:HIST + SEQ_S].rearrange("p (h b) t -> p h b t", h=2),
                                     sample(pair(t_a)), sample(work[:, m % 2]), ALU.mult).then_inc(psum_free[t_a % PAIRS], 1)
                    freed(dve, t_a)
                if b >= 1:
                    convolve(15)
                if b in MOD_AFTER:
                    modulation(0, MOD_AFTER[b])
            for g in range(AT):
                convolve(5)
                pool_input(g)
                if g == 1:
                    named_lo(("out_ab", 1))
            convolve(len(conv_ops))
            for j in range(AT):
                convolve_samples(j)
            own.after(own.n)
            dve.wait_ge(conv_step, len(conv_ops))
            freed(dve, tile_of["conv_pe"])
            for j in range(AT):
                sum_into_ss(acc[:, j], j == 0)
            for g in range(AT):
                n = U_MIX_OUT + g
                freed(dve, tile_of[("pool_mix", g)])
                piece_free(n)
                dv.tensor_copy(flat(piece[:, n % 2]), flat(work[:, g % 2])).then_inc(piece_ready, 1)
                if g:
                    piece_to_lo(act_lo[:, AT + g - 1], act_hi[:, AT + g - 1], n - 1)
            piece_to_lo(act_lo[:, KT - 1], act_hi[:, KT - 1], U_MIX_OUT + AT - 1)
            t = tile_of["conv_mean"]
            full(dve, t)
            for j in range(AT):
                dv.tensor_tensor(acc[:, j], acc[:, j], pair(t)[:, :, 0:HALF], ALU.subtract)\
                  .then_inc(centred if j < AT - 1 else psum_free[t % PAIRS], 1)
            for j in range(AT):
                sum_square(j == 0)
            modulation(0, GT2)
            modulation(1, SH1)
            inverse_root(tile_of["conv_var"], 2)
            dve.wait_ge(centred, AT - 1)
            freed(dve, t)
            for j in range(AT + 1):
                if j < AT:
                    if j >= 2:
                        own.after(own.n)
                    dv.tensor_tensor(flat(work[:, j % 2]), flat(acc[:, j]), flat(rstd), ALU.mult).then_inc(norm_ready, 1)
                    dve.wait_ge(norm_ready, j + 1)
                    own.step(dv.tensor_scalar(flat(acc[:, j]), flat(work[:, j % 2]), g_cln_v[:, j:j + 1],
                                              b_cln_v[:, j:j + 1], ALU.mult, ALU.add))
                    n = U_MIX_OUT + AT + j
                    dve.wait_ge(silu_ready, j + 1)
                    own.after(own.n)
                    piece_free(n)
                    dv.tensor_tensor(flat(piece[:, n % 2]), flat(acc[:, j]), flat(sq[:, j % 2]), ALU.mult).then_inc(piece_ready, 1)
                    piece_to_lo(act_lo[:, j], act_hi[:, j], n)
            modulation(1, SC1)
            modulation(1, SH2)
            project("out_ab", G_EVEN, 0, ("ffn", 0, 0, 0), split=2)
            modulation(1, SC2)
            inverse_root(tile_of[("stat", 1)], 3)
            norm_pieces(0, SC2, g_ffn_v[:, 0, :], U_FFN_IN0, 1)
            ffn(0, U_FFN0, G_FFN0, ("in_u", 0))
            modulation(1, GT1)
            inverse_root(tile_of[("stat", 2)], 4)
            norm_pieces(1, SC1, g_mix_v[:, 1, :], U_ODD_IN, 2)

            def v_norm(c):
                rows, src = (NS, v_s[:, :]) if c == CHUNKS else (P, v[:, c, :])
                own.after(own.n)
                own.step(dv.reduce_sum(lnst[0:rows, c, 0:1], src, AX_X))
                own.after(own.n)
                own.step(dv.tensor_scalar(lnst[0:rows, c, 0:1], lnst[0:rows, c, 0:1], 1.0 / D, None, ALU.mult))
                own.after(own.n)
                dv.tensor_scalar(src, src, lnst[0:rows, c, 0:1], None, ALU.subtract).then_inc(v_centred, 1)
                dve.wait_ge(v_sq, c + 1)
                own.step(dv.reduce_sum(lnst[0:rows, c, 1:2],
                                       (sq, work)[c % 2][0:rows].rearrange("p i h t -> p (i h t)")[:, 0:D], AX_X))
                own.after(own.n)
                dv.tensor_copy(lnst[0:rows, c, 3:4], lnst[0:rows, c, 1:2]).then_inc(v_var, 1)
                dve.wait_ge(v_root, c + 1)
                own.step(dv.reciprocal(lnst[0:rows, c, 2:3], lnst[0:rows, c, 2:3]))
                own.after(own.n)
                own.step(dv.scalar_tensor_tensor(src, src, lnst[0:rows, c, 2:3], g_v[0:rows, :], ALU.mult, ALU.mult))
                own.after(own.n)
                dv.tensor_tensor(src, src, b_v[0:rows, :], ALU.add).then_inc(v_ready, 1)

            dve.wait_ge(odd_loaded, 64)
            sequence = [("in_u", 0), *[("in_v", b) for b in range(OUT_BLOCKS)], *[("in_u", b) for b in range(1, OUT_BLOCKS)]]
            for n, (name, b) in enumerate(sequence):
                named_lo(sequence[n + 1] if n + 1 < len(sequence) else ("out_c", 0))
                if n == 4:
                    freed(dve, tile_of[("v", OUT_BLOCKS - 1)])
                    freed(dve, tile_of[("v_sample", OUT_BLOCKS - 1)])
                for c in {4: (0,), 5: (1, 2), 6: (3, 4)}.get(n, ()):
                    v_norm(c)
            t = tile_of["rep"]
            full(dve, t)
            for h in range(HEADS):
                mm = dv.tensor_tensor(
                    ws_seq[:, h],
                    pair(t)[0:NS, 0, h * SEQ_S:(h + 1) * SEQ_S].unsqueeze(1).broadcast_to([NS, BATCH_S, SEQ_S]),
                    same_seq[:, :].unsqueeze(2).broadcast_to([NS, BATCH_S, SEQ_S]), ALU.mult)
                if h < HEADS - 1:
                    own.step(mm)
                else:
                    mm.then_inc(psum_free[t % PAIRS], 1)
            freed(dve, tile_of[("u", KT - 1)])
            own.after(own.n)
            for h in range(HEADS):
                t = tile_of[("spatial", h)]
                n = U_ODD_OUT + h
                full(dve, t)
                bias = b_s[:, h, :]
                part = own.step(dv.tensor_tensor(
                    prompt(work[:, h % 2]).rearrange("p h (c t) -> p h c t", t=CHUNK),
                    prompt(pair(t)).rearrange("p h (c t) -> p h c t", t=CHUNK),
                    bias.unsqueeze(1).unsqueeze(1).broadcast_to([P, 2, 2, CHUNK]), ALU.add))
                own.after(part)
                dv.tensor_tensor(sample(work[:, h % 2]), sample(pair(t)),
                                 bias[:, 0:SEQ_S].unsqueeze(1).unsqueeze(1).broadcast_to([P, 2, HB, SEQ_S]), ALU.add)\
                  .then_inc(psum_free[t % PAIRS], 1)
                freed(dve, t)
                piece_free(n)
                dv.tensor_tensor(flat(piece[:, n % 2]), flat(work[:, h % 2]), flat(u[:, h]), ALU.mult).then_inc(piece_ready, 1)
                dve.wait_ge(piece_ready, n + 1)
                if h:
                    piece_to_lo(act_lo[:, h - 1], act_hi[:, h - 1], n - 1)
            piece_to_lo(act_lo[:, KT - 1], act_hi[:, KT - 1], U_ODD_OUT + KT - 1)
            project("out_c", G_ODD, 1, ("ffn", 1, 0, 0))
            modulation(1, GT2)
            inverse_root(tile_of[("stat", 3)], 5)
            norm_pieces(1, SC2, g_ffn_v[:, 1, :], U_FFN_IN1, 3)
            ffn(1, U_FFN1, G_FFN1)
            inverse_root(tile_of[("stat", 4)], 6)
            for k in range(KT):
                if k >= 2:
                    dve.wait_ge(y_ready, k - 1)
                dv.tensor_tensor(flat(work[:, k % 2]), flat(x[:, k]), flat(rstd), ALU.mult).then_inc(norm_ready, 1)


_INS = ["x_prompt", "x_sample", "c_prompt", "c_sample", "state_conv", "state_pool", "w_ada", "b_ada", "g_mix", "g_ffn",
        "w_in_ab", "w_dw", "b_dw", "g_conv_ln", "b_conv_ln", "w_pool", "s_pool", "w_out_ab", "w_in_c", "g_v_ln", "b_v_ln",
        "w_spatial", "b_spatial", "w_out_c", "w_ffn1", "w_ffn2", "g_final"]
_OUTS = [("y_prompt", (1, 512, 1024)), ("y_sample", (8, 4, 1024)), ("new_conv_prompt", (1, 1, 30, 512)),
         ("new_pool_prompt", (1, 1, 15, 512)), ("new_conv_sample", (1, 8, 30, 512)), ("new_pool_sample", (1, 8, 15, 512)),
         ("new_v_sample", (1, 8, 4, 1024))]


def kernel(**inputs):
    import numpy as _np
    import concourse.bacc as _bacc
    from concourse import mybir as _mybir
    from concourse.bass_utils import run_bass_kernel_spmd as _run

    nc = _bacc.Bacc("TRN2", target_bir_lowering=False, num_devices=1)
    arrays, ins, outs = {}, {}, {}
    for name in _INS:
        a = _np.ascontiguousarray(inputs[name])
        arrays[f"in_{name}_dram"] = a
        ins[name] = nc.dram_tensor(f"in_{name}_dram", a.shape, _mybir.dt.from_np(a.dtype), kind="ExternalInput").ap()
    for name, shape in _OUTS:
        outs[name] = nc.dram_tensor(f"out_{name}_dram", shape, _mybir.dt.float32, kind="ExternalOutput").ap()
    hybrid_decoder_step(nc, ins, outs)
    r = _run(nc, [arrays], core_ids=[0])
    return tuple(r.results[0][f"out_{name}_dram"] for name, _ in _OUTS)
```

```python
from contextlib import ExitStack

import concourse.bass as bass
from concourse import mybir

ALU = mybir.AluOpType
ACT = mybir.ActivationFunctionType
F32 = mybir.dt.float32
F32R = mybir.dt.float32r
AX_X = mybir.AxisListType.X

P = 128
D = 1024
KT = D // P
SEQ, BATCH_S, SEQ_S = 512, 8, 4
HP, HB = SEQ // 2, BATCH_S // 2
HS = HB * SEQ_S
HALF = HP + HS
TOK = 2 * HALF
NS = BATCH_S * SEQ_S
DA = D // 2
AT = DA // P
TAPS = 31
HIST = TAPS - 1
PHIST = 15
WINDOWS = (2, 4, 8, 16)
FF = 4 * D
QUARTERS = FF // D
HEADS = 8
CHUNK = 128
CHUNKS = SEQ // CHUNK
NCOND = 1 + BATCH_S
NMOD = 6
EPS = 1e-6
BN = 256
RAW = 4
PAIRS = 4
PE_TAPS = 22
CONV_STEPS = (AT - 1) * (TAPS + 1) + TAPS - PE_TAPS + 2
IN_AB = (("value", 0), ("gate", 0), ("value", 2), ("gate", 2), ("pool", 0), ("pool", 2))
MIX_BLOCKS_IN = len(IN_AB)
DIAGS = 8
OUT_BLOCKS = D // BN
FFN_BLOCKS = 2 * OUT_BLOCKS
CPM = 4
SH1, SC1, GT1, SH2, SC2, GT2 = range(NMOD)


MOD_AFTER = {1: GT1, 3: SH2, 4: SC2}
MOD_IN_OUT = {1: SH1, 2: SC1, 3: GT1}


class Own:

    def __init__(self, eng, sem):
        self.eng, self.sem, self.n = eng, sem, 0

    def step(self, instruction):
        instruction.then_inc(self.sem, 1)
        self.n += 1
        return self.n

    def after(self, n):
        self.eng.wait_ge(self.sem, n)


def plan():
    tile, item, block = {}, {}, {}
    blocks = chunks = 0
    order = []

    def tiles(*names):
        for n in names:
            assert n not in tile
            tile[n] = len(tile_list)
            tile_list.append(n)

    tile_list = []

    def load(name, is_block):
        nonlocal blocks, chunks
        item[name] = len(order)
        if is_block:
            block[name] = blocks
            blocks += 1
            order.append(("block", blocks))
        elif name[3] < CPM - 1:
            chunks += 1
            order.append(("ada", chunks))
        else:
            order.append(("tile", tile[name[:3]]))

    def load_ada(layer, i):
        for c in range(CPM):
            load(("ada", layer, i, c), False)

    tiles("vec", "cT")
    tiles(*[("x", k) for k in range(KT)])
    tiles(("stat", 0), ("ada", 0, SH1), ("ada", 0, SC1))
    tiles(*[("conv_hist", j) for j in range(AT)], "pool_hist")
    for b, (kind, m) in enumerate(IN_AB):
        tiles((kind, m), (kind, m + 1))
        if b in MOD_AFTER:
            tiles(("ada", 0, MOD_AFTER[b]))
    tiles("conv_pe", *[("pool_mix", g) for g in range(AT)], "conv_state", "pool_state")
    tiles("conv_mean", ("ada", 0, GT2), "conv_var")
    for b in range(OUT_BLOCKS):
        tiles(("out_ab", 2 * b), ("out_ab", 2 * b + 1))
        if b in MOD_IN_OUT:
            tiles(("ada", 1, MOD_IN_OUT[b]))
    tiles(("stat", 1))
    tiles(*[("ffn", 0, q, m) for q in range(QUARTERS) for m in range(2 * KT)])
    tiles(("ada", 1, SH2), ("stat", 2), "ws", ("u", 0), ("u", 1))
    for b in range(OUT_BLOCKS):
        tiles(("v", b), ("v_sample", b))
    tiles(*[("u", m) for m in range(2, KT)], ("ada", 1, SC2), "rep", *[("spatial", h) for h in range(HEADS)])
    tiles(*[("out_c", m) for m in range(KT)], ("ada", 1, GT2), ("stat", 3))
    tiles(*[("ffn", 1, q, m) for q in range(QUARTERS) for m in range(2 * KT)])
    tiles(("stat", 4), *[("y", c) for c in range(CHUNKS)], ("y_sample", 0), ("y_sample", 1))

    load_ada(0, SH1)
    load(("in_ab", 0), True)
    load_ada(0, SC1)
    load(("in_ab", 1), True)
    for b in range(2, MIX_BLOCKS_IN):
        load(("in_ab", b), True)
        if b - 1 in MOD_AFTER:
            load_ada(0, MOD_AFTER[b - 1])
    load(("out_ab", 0), True)
    load(("out_ab", 1), True)
    load_ada(0, GT2)
    for b in range(2, OUT_BLOCKS):
        load(("out_ab", b), True)
        load_ada(1, MOD_IN_OUT[b - 1])
    for layer, gate in ((0, GT1), (1, GT2)):
        for q in range(QUARTERS):
            for j in range(FFN_BLOCKS):
                load(("ffn", layer, q, j), True)
                if q == 0 and j == 0:
                    load_ada(1, gate)
        if layer == 0:
            load(("in_u", 0), True)
            load_ada(1, SH2)
            for b in range(OUT_BLOCKS):
                load(("in_v", b), True)
            for b in range(1, OUT_BLOCKS):
                load(("in_u", b), True)
            load(("out_c", 0), True)
            load_ada(1, SC2)
            for b in range(1, OUT_BLOCKS):
                load(("out_c", b), True)
    last = {("in_ab", b): tile[(kind, m + 1)] for b, (kind, m) in enumerate(IN_AB)}
    for b in range(OUT_BLOCKS):
        last[("in_v", b)] = tile[("v_sample", b)]
        for name, t in (("out_ab", "out_ab"), ("out_c", "out_c"), ("in_u", "u")):
            last[(name, b)] = tile[(t, 2 * b + 1)]
    last_tile = {n: last[name] if name in last else tile[(*name[:3], 2 * name[3] + 1)] for name, n in block.items()}
    return tile, item, block, last_tile, order


def hybrid_decoder_step(nc, I, O):
    tile_of, item_of, block_of, last_tile_of, order = plan()
    ctx = ExitStack()
    with ctx:
        def sb(name, shape, dt=F32, where=ctx):
            return where.enter_context(nc.sbuf_tensor(name, shape, dt))

        def sem(name):
            return ctx.enter_context(nc.semaphore(name))

        x = sb("x", [P, KT, 2, HALF])
        act_hi = sb("act_hi", [P, KT, 2, HALF], F32R)
        act_lo = sb("act_lo", [P, KT, 2, HALF], F32R)
        in_s_hi = sb("in_s_hi", [P, KT, NS], F32R)
        in_s_lo = sb("in_s_lo", [P, KT, NS], F32R)
        w_hi = sb("w_hi", [P, 2, KT, BN], F32R)
        w_lo = sb("w_lo", [P, 2, KT, BN], F32R)
        raw = sb("raw", [P, RAW, KT * BN])
        work = sb("work", [P, 2, 2, HALF])
        piece = sb("piece", [P, 2, 2, HALF])
        sq = sb("sq", [P, 2, 2, HALF])
        ss = sb("ss", [P, 2, HALF])
        rstd = sb("rstd", [P, 2, HALF])
        gated_s = sb("gated_s", [P, 2, HS * 2])
        scaled_s = sb("scaled_s", [P, 2, NS])
        ident = sb("ident", [P, P])
        ones_d = sb("ones_d", [P, P])
        ones_a = sb("ones_a", [P, P])
        eps = sb("eps", [P, 1])
        NVEC = 4 * KT + KT + 4 * AT
        NB_ADA = 2 * NMOD * KT
        NTAP = TAPS * AT
        vec = sb("vec", [P, NVEC + NB_ADA + NTAP])
        cT = sb("cT", [P, KT, 32])
        mod_t = sb("mod_t", [P, KT, 32])
        mod = sb("mod", [P, 2, NMOD, KT, NCOND])
        scale = sb("scale", [P, KT, NCOND])
        inv_count = sb("inv_count", [P, AT, 16])
        w_pool_sb = sb("w_pool_sb", [P, AT, P])
        replicate = sb("replicate", [P, BATCH_S, SEQ_S])
        same_seq = sb("same_seq", [NS, BATCH_S])
        lnst = sb("lnst", [P, CHUNKS + 1, 4])

        g_mix_v = vec[:, 0:2 * KT].rearrange("p (l k) -> p l k", l=2)
        g_ffn_v = vec[:, 2 * KT:4 * KT].rearrange("p (l k) -> p l k", l=2)
        g_final_v = vec[:, 4 * KT:5 * KT]
        b_dw_v, g_cln_v, b_cln_v, s_pool_v = [vec[:, 5 * KT + i * AT:5 * KT + (i + 1) * AT] for i in range(4)]
        b_ada_v = vec[:, NVEC:NVEC + NB_ADA].rearrange("p (l i k) -> p l i k", l=2, i=NMOD)
        w_dw_v = vec[:, NVEC + NB_ADA:].rearrange("p (t j) -> p t j", j=AT)

        with ExitStack() as zone:
            a_ext = sb("a_ext", [P, AT, HIST + SEQ], where=zone)
            a_ext_s = sb("a_ext_s", [P, AT, BATCH_S, HIST + SEQ_S], where=zone)
            p_ext = sb("p_ext", [P, AT, PHIST + SEQ], where=zone)
            p_ext_s = sb("p_ext_s", [P, AT, BATCH_S, PHIST + SEQ_S], where=zone)
            with ExitStack() as early:
                x_rows = sb("x_rows", [P, CHUNKS, D], where=early)
                xs_rows = sb("xs_rows", [HS, 2, D], where=early)
                c_rows = sb("c_rows", [32, D], where=early)
                vec_rows = sb("vec_rows", [P, 3, P], where=early)
                conv_rows = sb("conv_rows", [4 * HIST, 2, DA], where=early)
                pool_rows = sb("pool_rows", [BATCH_S * PHIST, DA], where=early)
            with ExitStack() as late:
                acc = sb("acc", [P, AT, 2, HALF], where=late)
                diag = sb("diag", [P, DIAGS, P], where=late)
                acc_odd = sb("acc_odd", [P, 2, SEQ], where=late)
                win = sb("win", [P, AT, 2, HALF], where=late)
                sum_p = sb("sum_p", [P, 2, PHIST + SEQ], where=late)
                sum_s = sb("sum_s", [P, 2, BATCH_S, PHIST + SEQ_S], where=late)
                new_s = sb("new_s", [P, 2, AT, NS], where=late)
                conv_part = sb("conv_part", [P, 2, HP], where=late)
                prod = sb("prod", [P, SEQ_S, BATCH_S, TAPS], where=late)
        with ExitStack() as zone:
            f_hi = sb("f_hi", [P, KT, 2, HALF], F32R, where=zone)
            f_lo = sb("f_lo", [P, KT, 2, HALF], F32R, where=zone)
        with ExitStack() as zone:
            u = sb("u", [P, KT, 2, HALF], where=zone)
            v = sb("v", [P, CHUNKS, D], where=zone)
            v_s = sb("v_s", [NS, D], where=zone)
            ws_t = sb("ws_t", [P, HEADS, CHUNK], where=zone)
            b_s = sb("b_s", [P, HEADS, CHUNK], where=zone)
            g_v = sb("g_v", [P, D], where=zone)
            b_v = sb("b_v", [P, D], where=zone)
            ws_seq = sb("ws_seq", [NS, HEADS, BATCH_S, SEQ_S], where=zone)
        ws_rows = v[:, 0, :].rearrange("p (h s) -> p h s", h=HEADS)
        with ExitStack() as zone:
            y_t = sb("y_t", [P, KT, 2, HALF], where=zone)
            y_rows = sb("y_rows", [P, CHUNKS, D], where=zone)
            ys_rows = sb("ys_rows", [HS, 2, D], where=zone)
        head = gated_s[:, 1, 0:16]
        channel_squares = win[:, :, :, :]
        conv_state_rows = diag[0:NS].rearrange("p d c -> p (d c)")[:, 0:2 * DA].rearrange("p (i c) -> p i c", i=2)
        pool_state_rows = sum_p[0:NS].rearrange("p l t -> p (l t)")[:, 0:2 * DA].rearrange("p (i c) -> p i c", i=2)

        psum = ctx.enter_context(nc.psum_tensor("psum", [P, 2 * PAIRS, 512], F32))

        def pair(t):
            return psum[:, 2 * (t % PAIRS):2 * (t % PAIRS) + 2, :]

        def uses(t):
            return t // PAIRS + 1

        def full(eng, t, per=None):
            eng.wait_ge(psum_full[t % PAIRS], uses(t) if per is None else per + uses(t))

        def freed(eng, t, per=None):
            eng.wait_ge(psum_free[t % PAIRS], uses(t) if per is None else per + uses(t))

        def prompt(ap):
            return ap[:, :, 0:HP]

        def sample(ap):
            return ap[:, :, HP:HALF].rearrange("p h (b t) -> p h b t", t=SEQ_S)

        def per_seq(ap9):
            return ap9[:, 1:NCOND].rearrange("p (h b) -> p h b", h=2).unsqueeze(3).broadcast_to([P, 2, HB, SEQ_S])

        def flat(ap):
            return ap.rearrange("p h t -> p (h t)")

        psum_full = [sem(f"psum_full{i}") for i in range(PAIRS)]
        psum_free = [sem(f"psum_free{i}") for i in range(PAIRS)]
        raw_full = [sem(f"raw_full{i}") for i in range(RAW)]
        w_hi_ready, w_lo_ready, ada_used = sem("w_hi_ready"), sem("w_lo_ready"), sem("ada_used")
        vec_loaded, c_loaded, x_loaded, hist_loaded, pool_w_loaded = (
            sem("vec_loaded"), sem("c_loaded"), sem("x_loaded"), sem("hist_loaded"), sem("pool_w_loaded"))
        odd_loaded = sem("odd_loaded")
        pool_step, act_step, dve_step = sem("pool_step"), sem("act_step"), sem("dve_step")
        consts_ready, c_zeroed, pads_ready = sem("consts_ready"), sem("c_zeroed"), sem("pads_ready")
        c_sigmoid, c_silu = sem("c_sigmoid"), sem("c_silu")
        sq_ready, ss_added, root_ready = sem("sq_ready"), sem("ss_added"), sem("root_ready")
        piece_ready, piece_hi, piece_lo = sem("piece_ready"), sem("piece_hi"), sem("piece_lo")
        x_prompt_done, x_sample_done = sem("x_prompt_done"), sem("x_sample_done")
        a_ready, conv_step = sem("a_ready"), sem("conv_step")
        p_ready, win_ready, pool_in_ready = sem("p_ready"), sem("win_ready"), sem("pool_in_ready")
        conv_s_ready, channel_sq = sem("conv_s_ready"), sem("channel_sq")
        centred, norm_ready, silu_ready, affine_ready = sem("centred"), sem("norm_ready"), sem("silu_ready"), sem("affine_ready")
        diag_ready, diag_used, xr_ready, scale_ready = sem("diag_ready"), sem("diag_used"), sem("xr_ready"), sem("scale_ready")
        new_s_ready, in_s_ready = sem("new_s_ready"), sem("in_s_ready")
        out_stored, rows_stored, y_ready, ws_masked = sem("out_stored"), sem("rows_stored"), sem("y_ready"), sem("ws_masked")
        v_centred, v_sq, v_var, v_root, v_ready = (
            sem("v_centred"), sem("v_sq"), sem("v_var"), sem("v_root"), sem("v_ready"))

        U_MIX_IN, U_MIX_OUT, U_FFN_IN0, U_FFN0 = 0, KT, 2 * KT, 3 * KT
        U_ODD_IN = U_FFN0 + QUARTERS * KT
        U_ODD_OUT = U_ODD_IN + KT
        U_FFN_IN1 = U_ODD_OUT + KT
        U_FFN1 = U_FFN_IN1 + KT
        G_EVEN = 0
        G_FFN0 = KT
        G_ODD = G_FFN0 + QUARTERS * KT
        G_FFN1 = G_ODD + KT
        G_END = G_FFN1 + QUARTERS * KT
        STATE_STORES = 16 * (4 + 2)

        block = ctx.enter_context(nc.Block())

        @block.sync
        def _(sp):
            def buffer_free(i):
                if i >= RAW:
                    kind, n = order[i - RAW]
                    if kind == "tile":
                        sp.wait_ge(psum_full[n % PAIRS], uses(n))
                    else:
                        sp.wait_ge(w_lo_ready if kind == "block" else ada_used, n)

            def load(name, src, shape):
                i = item_of[name]
                buffer_free(i)
                dst = raw[:, i % RAW, :].rearrange(shape[0], **shape[1])
                sp.dma_start(dst, src).then_inc(raw_full[i % RAW], 16)

            def load_block(name, w, rows, cols):
                load(name, w[rows:rows + D, cols:cols + BN].rearrange("(k p) n -> p k n", p=P),
                     ("p (k n) -> p k n", {"k": KT}))

            def load_ada(layer, i):
                for c in range(CPM):
                    load(("ada", layer, i, c),
                         I["w_ada"][layer, 2 * P * c:2 * P * (c + 1), i * D:(i + 1) * D].rearrange("(k p) n -> p k n", p=P),
                         ("p (k n) -> p k n", {"k": 2}))

            def load_ffn(layer, modulation):
                w1, w2 = I["w_ffn1"][layer], I["w_ffn2"][layer]
                first = item_of[("ffn", layer, 0, 1)] - 1
                blocks = block_of[("ffn", layer, 0, 0)]
                load_block(("ffn", layer, 0, 0), w1, 0, 0)
                load_ada(1, modulation)
                for j in range(1, OUT_BLOCKS):
                    load_block(("ffn", layer, 0, j), w1, 0, j * BN)
                full(sp, tile_of[("ada", 1, modulation)])
                with sp.Fori(0, QUARTERS - 1) as q:
                    for j in range(FFN_BLOCKS):
                        i = first + OUT_BLOCKS + j
                        sp.wait_ge(w_lo_ready, q * FFN_BLOCKS + (blocks + j + 1))
                        if j < OUT_BLOCKS:
                            src = w2[bass.ds(q * D, D), j * BN:(j + 1) * BN]
                        else:
                            src = w1[:, bass.ds(q * D + (D + (j - OUT_BLOCKS) * BN), BN)]
                        sp.dma_start(raw[:, i % RAW, :].rearrange("p (k n) -> p k n", k=KT),
                                     src.rearrange("(k p) n -> p k n", p=P)).then_inc(raw_full[i % RAW], 16)
                for j in range(OUT_BLOCKS):
                    load_block(("ffn", layer, QUARTERS - 1, OUT_BLOCKS + j), w2, (QUARTERS - 1) * D, j * BN)

            sp.wait_ge(c_zeroed, 1)
            sp.dma_start(c_rows[0:1, :], I["c_prompt"]).then_inc(c_loaded, 16)
            sp.dma_start(c_rows[1:NCOND, :], I["c_sample"]).then_inc(c_loaded, 16)
            sp.dma_start(x_rows[:, :, :], I["x_prompt"][0].rearrange("(c p) d -> p c d", p=P)).then_inc(x_loaded, 16)
            sp.dma_start(xs_rows[:, :, :], I["x_sample"].rearrange("(h b) t d -> (b t) h d", h=2)).then_inc(x_loaded, 16)
            w_in = I["w_in_ab"][0]

            def load_in(b):
                kind, m = IN_AB[b]
                load_block(("in_ab", b), w_in, 0, {"value": 0, "gate": DA, "pool": 2 * DA}[kind] + m * P)

            load_ada(0, SH1)
            load_in(0)
            load_ada(0, SC1)
            load_in(1)
            for b in range(2, MIX_BLOCKS_IN):
                load_in(b)
                if b - 1 in MOD_AFTER:
                    load_ada(0, MOD_AFTER[b - 1])
            keep = HIST - SEQ_S
            sp.dma_start(O["new_conv_sample"][0, :, 0:keep, :], I["state_conv"][0, :, SEQ_S:HIST, :]).then_inc(out_stored, 16)
            keep_p = PHIST - SEQ_S
            sp.dma_start(O["new_pool_sample"][0, :, 0:keep_p, :], I["state_pool"][0, :, SEQ_S:PHIST, :]).then_inc(out_stored, 16)
            for b in range(2):
                load_block(("out_ab", b), I["w_out_ab"][0], 0, b * BN)
            load_ada(0, GT2)
            for b in range(2, OUT_BLOCKS):
                load_block(("out_ab", b), I["w_out_ab"][0], 0, b * BN)
                load_ada(1, MOD_IN_OUT[b - 1])
            freed(sp, tile_of["conv_state"])
            freed(sp, tile_of["pool_state"])
            sp.dma_start(O["new_conv_prompt"][0, 0], conv_state_rows[NS - HIST:NS, 0, :]).then_inc(out_stored, 16)
            sp.dma_start(O["new_conv_sample"][0, :, keep:HIST, :], conv_state_rows[:, 1, :]).then_inc(out_stored, 16)
            sp.dma_start(O["new_pool_prompt"][0, 0], pool_state_rows[NS - PHIST:NS, 0, :]).then_inc(out_stored, 16)
            sp.dma_start(O["new_pool_sample"][0, :, keep_p:PHIST, :], pool_state_rows[:, 1, :]).then_inc(out_stored, 16)
            load_ffn(0, GT1)
            load_block(("in_u", 0), I["w_in_c"][0], 0, 0)
            load_ada(1, SH2)
            sp.wait_ge(x_sample_done, G_ODD)
            sp.dma_start(ws_rows, I["w_spatial"][0].rearrange("h t s -> t h s")).then_inc(odd_loaded, 16)
            sp.dma_start(b_s[:, :, :], I["b_spatial"][0].partition_broadcast(P)).then_inc(odd_loaded, 16)
            sp.dma_start(g_v[:, :], I["g_v_ln"][0].partition_broadcast(P)).then_inc(odd_loaded, 16)
            sp.dma_start(b_v[:, :], I["b_v_ln"][0].partition_broadcast(P)).then_inc(odd_loaded, 16)
            for b in range(OUT_BLOCKS):
                load_block(("in_v", b), I["w_in_c"][0], 0, D + b * BN)
            for b in range(1, OUT_BLOCKS):
                load_block(("in_u", b), I["w_in_c"][0], 0, b * BN)
            load_block(("out_c", 0), I["w_out_c"][0], 0, 0)
            load_ada(1, SC2)
            for b in range(1, OUT_BLOCKS):
                load_block(("out_c", b), I["w_out_c"][0], 0, b * BN)
            sp.wait_ge(v_ready, CHUNKS + 1)
            sp.dma_start(O["new_v_sample"][0].rearrange("b t d -> (b t) d"), v_s[:, :]).then_inc(out_stored, 16)
            load_ffn(1, GT2)
            for c in range(CHUNKS):
                freed(sp, tile_of[("y", c)])
                sp.dma_start(O["y_prompt"][0, c * CHUNK:(c + 1) * CHUNK, :], y_rows[:, c, :]).then_inc(rows_stored, 16)
            for h in range(2):
                freed(sp, tile_of[("y_sample", h)])
            sp.dma_start(O["y_sample"].rearrange("(h b) t d -> (b t) h d", h=2), ys_rows[:, :, :]).then_inc(rows_stored, 16)
            sp.wait_ge(out_stored, STATE_STORES + 16)
            sp.wait_ge(rows_stored, 16 * (CHUNKS + 1))

        @block.gpsimd
        def _(pool):
            own = Own(pool, pool_step)
            g = nc.gpsimd
            g.memset(c_rows[:, :], 0.0).then_inc(c_zeroed, 1)
            zero = own.step(g.memset(ident[:, :], 0.0))
            own.after(zero)
            g.affine_select(out=ident[:, :], in_=ident[:, :], compare_op=ALU.not_equal, fill=1.0, base=0,
                            pattern=[[-1, P]], channel_multiplier=1).then_inc(consts_ready, 1)
            g.memset(ones_d[:, :], 1.0 / D).then_inc(consts_ready, 1)
            g.memset(ones_a[:, :], 1.0 / DA).then_inc(consts_ready, 1)
            g.memset(eps[:, :], EPS).then_inc(consts_ready, 1)
            g.memset(a_ext[:, :, 0:HIST], 0.0).then_inc(pads_ready, 1)
            g.memset(p_ext[:, :, 0:PHIST], 0.0).then_inc(pads_ready, 1)
            for i, w in enumerate(WINDOWS):
                full = own.step(g.memset(inv_count[:, i, :], 1.0 / w))
                own.after(full)
                for t in range(w - 1):
                    last = own.step(g.memset(inv_count[:, i, t:t + 1], 1.0 / (t + 1)))
            own.after(last)
            m = own.step(g.memset(replicate[:, :, :], 0.0))
            own.after(m)
            m = own.step(g.affine_select(out=replicate[:, :, :], in_=replicate[:, :, :], compare_op=ALU.not_equal, fill=1.0,
                                         base=0, pattern=[[0, BATCH_S], [-1, SEQ_S]], channel_multiplier=1))
            m = own.step(g.memset(same_seq[:, :], 1.0))
            own.after(m)
            m = own.step(g.affine_select(out=same_seq[:, :], in_=same_seq[:, :], compare_op=ALU.is_ge, fill=0.0,
                                         base=0, pattern=[[-SEQ_S, BATCH_S]], channel_multiplier=1))
            own.after(m)
            g.affine_select(out=same_seq[:, :], in_=same_seq[:, :], compare_op=ALU.is_ge, fill=0.0,
                            base=SEQ_S - 1, pattern=[[SEQ_S, BATCH_S]], channel_multiplier=-1).then_inc(consts_ready, 1)
            def norm_pieces_samples(layer, sh, unit, nth):
                pool.wait_ge(scale_ready, nth + 1)
                for k in range(KT):
                    n = unit + k
                    pool.wait_ge(xr_ready, nth * KT + k + 1)
                    tmp = scaled_s[:, k % 2, :].rearrange("p (h b t) -> p h b t", h=2, t=SEQ_S)
                    done = own.step(g.tensor_tensor(tmp, sample(work[:, k % 2]), per_seq(scale[:, k, :]), ALU.mult))
                    own.after(done)
                    if n >= 2:
                        pool.wait_ge(piece_lo, n - 1)
                    g.tensor_tensor(sample(piece[:, n % 2]), tmp, per_seq(mod[:, layer, sh, k, :]), ALU.add)\
                     .then_inc(piece_ready, 1)

            def convolve_samples(j):
                freed(pool, tile_of[("conv_hist", j)])
                freed(pool, tile_of[("value", j)])
                own.after(own.n)
                for t in range(SEQ_S):
                    own.step(g.tensor_tensor(prod[:, t], a_ext_s[:, j, :, t:t + TAPS],
                                             w_dw_v[:, :, j].unsqueeze(1).broadcast_to([P, BATCH_S, TAPS]), ALU.mult))
                have, half = TAPS, 16
                while half:
                    own.after(own.n)
                    own.step(g.tensor_tensor(prod[:, :, :, 0:have - half], prod[:, :, :, 0:have - half],
                                             prod[:, :, :, half:have], ALU.add))
                    have, half = half, half // 2
                own.after(own.n)
                g.tensor_scalar(sample(acc[:, j]), prod[:, :, :, 0].rearrange("p t (h b) -> p h b t", h=2),
                                b_dw_v[:, j:j + 1], None, ALU.add).then_inc(conv_s_ready, 1)
                pool.wait_ge(conv_s_ready, j + 1)

            def pool_input(i):
                w = WINDOWS[i]
                own.step(g.tensor_tensor(head, win[:, i, 0, 0:16], inv_count[:, i, :], ALU.mult))
                own.after(own.n)
                own.step(g.tensor_scalar(flat(win[:, i]), flat(win[:, i]), 1.0 / w, None, ALU.mult))
                own.after(own.n)
                own.step(g.tensor_tensor(prompt(win[:, i]), prompt(win[:, i]),
                                         p_ext[:, i, PHIST:PHIST + SEQ].rearrange("p (h t) -> p h t", h=2), ALU.subtract))
                own.step(g.tensor_tensor(
                    sample(win[:, i]), sample(win[:, i]),
                    p_ext_s[:, i, :, PHIST:PHIST + SEQ_S].rearrange("p (h b) t -> p h b t", h=2), ALU.subtract))
                own.after(own.n)
                g.tensor_tensor(win[:, i, 0, 0:16], head, p_ext[:, i, PHIST:PHIST + 16], ALU.subtract)\
                 .then_inc(pool_in_ready, 1)
                pool.wait_ge(pool_in_ready, i + 1)

            norm_pieces_samples(0, SH1, U_MIX_IN, 0)
            for j in range(AT):
                convolve_samples(j)
            pool.wait_ge(pads_ready, 2)
            freed(pool, tile_of["pool_hist"])
            for i in range(AT):
                pool.wait_ge(p_ready, i + 1)
                freed(pool, tile_of[("pool", i)])
                src_p, src_s = p_ext[:, i, :], p_ext_s[:, i, :, :]
                shift = 1
                for level in range(i + 1):
                    lo = 2 * shift - 1
                    dst_p, dst_s = sum_p[:, level % 2, :], sum_s[:, level % 2, :, :]
                    if level == i:
                        own.step(g.tensor_tensor(
                            prompt(win[:, i]), src_p[:, PHIST:PHIST + SEQ].rearrange("p (h t) -> p h t", h=2),
                            src_p[:, PHIST - shift:PHIST + SEQ - shift].rearrange("p (h t) -> p h t", h=2), ALU.add))
                        own.after(own.n)
                        g.tensor_tensor(
                            sample(win[:, i]),
                            src_s[:, :, PHIST:PHIST + SEQ_S].rearrange("p (h b) t -> p h b t", h=2),
                            src_s[:, :, PHIST - shift:PHIST + SEQ_S - shift].rearrange("p (h b) t -> p h b t", h=2),
                            ALU.add).then_inc(win_ready, 1)
                        pool.wait_ge(win_ready, i + 1)
                    else:
                        own.step(g.tensor_tensor(dst_p[:, lo:], src_p[:, lo:], src_p[:, lo - shift:PHIST + SEQ - shift],
                                                 ALU.add))
                        own.step(g.tensor_tensor(dst_s[:, :, lo:], src_s[:, :, lo:],
                                                 src_s[:, :, lo - shift:PHIST + SEQ_S - shift], ALU.add))
                        own.after(own.n)
                    src_p, src_s = dst_p, dst_s
                    shift *= 2
                pool_input(i)
            norm_pieces_samples(0, SH2, U_FFN_IN0, 1)
            norm_pieces_samples(1, SH1, U_ODD_IN, 2)
            freed(pool, tile_of["ws"])
            g.affine_select(out=ws_t[:, :, :], in_=ws_t[:, :, :], compare_op=ALU.is_ge, fill=0.0, base=0,
                            pattern=[[0, HEADS], [1, CHUNK]], channel_multiplier=-1).then_inc(ws_masked, 1)
            norm_pieces_samples(1, SH2, U_FFN_IN1, 3)

        @block.tensor
        def _(pe):
            def take(t):
                if t >= PAIRS:
                    pe.wait_ge(psum_free[t % PAIRS], t // PAIRS)
                return pair(t)

            def give(t, mm):
                mm.then_inc(psum_full[t % PAIRS], 1)

            def product(out, left, right, start, stop):
                for n, (a, b) in enumerate(((0, 0), (0, 1), (1, 0))):
                    mm = nc.tensor.matmul(out, left[a], right[b], start=start and n == 0, stop=stop and n == 2,
                                          skip_group_check=True)
                return mm

            def block_product(b, t, hi, lo, units, k_order=range(KT), first=True, last=True, per_b=None, per_t=None,
                              per_u=None):
                slot = b % 2

                def at(n, per):
                    return n if per is None else per + n

                pe.wait_ge(w_lo_ready, at(b + 1, per_b))
                for m in range(2):
                    if first and t + m >= PAIRS:
                        pe.wait_ge(psum_free[(t + m) % PAIRS], at((t + m) // PAIRS, per_t))
                for n, k in enumerate(k_order):
                    if units is not None:
                        pe.wait_ge(piece_lo, at(units + n + 1, per_u))
                    for m in range(2):
                        out = pair(t + m)
                        cols = slice(m * P, (m + 1) * P)
                        for i, (a, c) in enumerate(((w_hi, hi), (w_hi, lo), (w_lo, hi))):
                            for h in range(2):
                                mm = nc.tensor.matmul(out[:, h, 0:HALF], a[:, slot, k, cols], c[:, k, h, :],
                                                      start=(first and n == 0 and i == 0),
                                                      stop=(last and n == len(k_order) - 1 and i == 2),
                                                      skip_group_check=True)
                        if last and n == len(k_order) - 1:
                            if m == 0:
                                mm.then_inc(psum_full[t % PAIRS], 1)
                            else:
                                mm.then_inc(psum_full[(t + 1) % PAIRS], 1)

            def named_block(name, t_name, hi, lo, units, k_order=range(KT), first=True, last=True):
                block_product(block_of[name], tile_of[t_name], hi, lo, units, k_order, first, last)

            def ada(layer, i):
                t = tile_of[("ada", layer, i)]
                out = take(t)
                for c in range(CPM):
                    it = item_of[("ada", layer, i, c)]
                    pe.wait_ge(raw_full[it % RAW], 16 * (it // RAW + 1))
                    chunk = raw[:, it % RAW, :].rearrange("p (k j g f) -> p k g j f", k=2, g=4, f=32)
                    for kk in range(2):
                        k = 2 * c + kk
                        for grp in range(4):
                            mm = nc.tensor.matmul(out[32 * grp:32 * grp + 32, 0, 0:2 * P], cT[:, k, :], chunk[:, kk, grp],
                                                  start=(k == 0), stop=(k == KT - 1), skip_group_check=True)
                    if c < CPM - 1:
                        mm.then_inc(ada_used, 1)
                give(t, mm)

            def stat(t, ones, count):
                out = take(t)
                pe.wait_ge(ss_added, count)
                for h in range(2):
                    mm = nc.tensor.matmul(out[:, h, 0:HALF], ones[:, :], ss[:, h, :], start=True, stop=True)
                give(t, mm)

            def ffn(layer, units_in, units):
                b0, t0 = block_of[("ffn", layer, 0, 0)], tile_of[("ffn", layer, 0, 0)]
                with pe.Fori(0, QUARTERS) as q:
                    per_b, per_t, per_u = q * FFN_BLOCKS, q * (2 * FFN_BLOCKS // PAIRS), q * KT
                    for j in range(OUT_BLOCKS):
                        block_product(b0 + j, t0 + 2 * j, act_hi, act_lo, None if j else units_in, per_b=per_b,
                                      per_t=per_t, per_u=q * 0)
                    for j in range(OUT_BLOCKS, FFN_BLOCKS):
                        block_product(b0 + j, t0 + 2 * j, f_hi, f_lo, None if j > OUT_BLOCKS else units, per_b=per_b,
                                      per_t=per_t, per_u=per_u)

            pe.wait_ge(consts_ready, 5)
            pe.wait_ge(vec_loaded, 16 * 9)
            out = take(tile_of["vec"])
            at = 0
            for i, n in enumerate((NVEC, NB_ADA, NTAP)):
                mm = nc.tensor.transpose(out[:, 0, at:at + n], vec_rows[0:n, i, :], ident[0:n, 0:n])
                at += n
            give(tile_of["vec"], mm)
            pe.wait_ge(c_silu, 1)
            out = take(tile_of["cT"])
            for k in range(KT):
                mm = nc.tensor.transpose(out[:, 0, 32 * k:32 * k + 32], c_rows[:, k * P:(k + 1) * P], ident[0:32, 0:32])
            give(tile_of["cT"], mm)
            pe.wait_ge(x_loaded, 32)
            for k in range(KT):
                out = take(tile_of[("x", k)])
                for c in range(CHUNKS):
                    nc.tensor.transpose(out[:, c // 2, (c % 2) * CHUNK:(c % 2 + 1) * CHUNK], x_rows[:, c, k * P:(k + 1) * P],
                                        ident[:, :])
                for h in range(2):
                    mm = nc.tensor.transpose(out[:, h, HP:HALF], xs_rows[:, h, k * P:(k + 1) * P], ident[0:HS, 0:HS])
                give(tile_of[("x", k)], mm)
            stat(tile_of[("stat", 0)], ones_d, KT)
            freed(pe, tile_of["cT"])
            ada(0, SH1)
            ada(0, SC1)
            pe.wait_ge(hist_loaded, 48)
            for j in range(AT):
                out = take(tile_of[("conv_hist", j)])
                for h in range(2):
                    mm = nc.tensor.transpose(out[:, h, 0:HB * HIST], conv_rows[:, h, j * P:(j + 1) * P],
                                             ident[0:HB * HIST, 0:HB * HIST])
                give(tile_of[("conv_hist", j)], mm)
            out = take(tile_of["pool_hist"])
            n = BATCH_S * PHIST
            for j in range(AT):
                mm = nc.tensor.transpose(out[:, 0, j * n:(j + 1) * n], pool_rows[:, j * P:(j + 1) * P], ident[0:n, 0:n])
            give(tile_of["pool_hist"], mm)
            for b, name in enumerate(IN_AB):
                named_block(("in_ab", b), name, act_hi, act_lo, None if b else U_MIX_IN)
                if b in MOD_AFTER:
                    ada(0, MOD_AFTER[b])
            conv = take(tile_of["conv_pe"])
            pe.wait_ge(a_ready, 1)
            freed(pe, tile_of[("value", 0)])
            for tap in range(PE_TAPS):
                pe.wait_ge(diag_ready, tap + 1)
                for h in range(2):
                    mm = nc.tensor.matmul(conv[:, h, 0:HP], diag[:, tap % DIAGS, :],
                                          a_ext[:, 0, tap + h * HP:tap + (h + 1) * HP], start=(tap == 0),
                                          stop=(tap == PE_TAPS - 1), skip_group_check=True)
                mm.then_inc(diag_used if tap < PE_TAPS - 1 else psum_full[tile_of["conv_pe"] % PAIRS], 1)
            pe.wait_ge(pool_w_loaded, 16)
            for i in range(AT):
                out = take(tile_of[("pool_mix", i)])
                pe.wait_ge(pool_in_ready, i + 1)
                for h in range(2):
                    mm = nc.tensor.matmul(out[:, h, 0:HALF], w_pool_sb[:, i, :], win[:, i, h, :], start=True, stop=True)
                give(tile_of[("pool_mix", i)], mm)
            out = take(tile_of["conv_state"])
            pe.wait_ge(new_s_ready, 2)
            for j in range(AT):
                nc.tensor.transpose(out[0:NS, 0, j * P:(j + 1) * P], a_ext[:, j, SEQ + HIST - NS:SEQ + HIST], ident[:, :])
                mm = nc.tensor.transpose(out[0:NS, 1, j * P:(j + 1) * P], new_s[:, 0, j, :], ident[:, :])
            give(tile_of["conv_state"], mm)
            out = take(tile_of["pool_state"])
            for j in range(AT):
                nc.tensor.transpose(out[0:NS, 0, j * P:(j + 1) * P], p_ext[:, j, SEQ + PHIST - NS:SEQ + PHIST], ident[:, :])
                mm = nc.tensor.transpose(out[0:NS, 1, j * P:(j + 1) * P], new_s[:, 1, j, :], ident[:, :])
            give(tile_of["pool_state"], mm)
            out = take(tile_of["conv_mean"])
            pe.wait_ge(conv_s_ready, AT)
            for n, j in enumerate((*range(1, AT), 0)):
                pe.wait_ge(conv_step, j * (TAPS + 1) if j else CONV_STEPS)
                for h in range(2):
                    mm = nc.tensor.matmul(out[:, h, 0:HALF], ones_a[:, :], acc[:, j, h, :], start=(n == 0), stop=(n == AT - 1),
                                          skip_group_check=True)
            give(tile_of["conv_mean"], mm)
            ada(0, GT2)
            out = take(tile_of["conv_var"])
            for j in range(AT):
                pe.wait_ge(channel_sq, j + 1)
                for h in range(2):
                    mm = nc.tensor.matmul(out[:, h, 0:HALF], ones_a[:, :], channel_squares[:, j, h, :], start=(j == 0),
                                          stop=(j == AT - 1), skip_group_check=True)
            give(tile_of["conv_var"], mm)
            pooled, convolved = range(AT, KT), range(AT)
            for b in range(2):
                named_block(("out_ab", b), ("out_ab", 2 * b), act_hi, act_lo, None if b else U_MIX_OUT, pooled, last=False)
            for b in range(2):
                named_block(("out_ab", b), ("out_ab", 2 * b), act_hi, act_lo, None if b else U_MIX_OUT + AT, convolved,
                            first=False)
            ada(1, MOD_IN_OUT[1])
            for b in range(2, OUT_BLOCKS):
                named_block(("out_ab", b), ("out_ab", 2 * b), act_hi, act_lo, None)
                ada(1, MOD_IN_OUT[b])
            stat(tile_of[("stat", 1)], ones_d, 2 * KT)
            ffn(0, U_FFN_IN0, U_FFN0)
            ada(1, SH2)
            stat(tile_of[("stat", 2)], ones_d, 3 * KT)
            pe.wait_ge(odd_loaded, 64)
            out = take(tile_of["ws"])
            for h in range(HEADS):
                mm = nc.tensor.transpose(out[:, h // 4, (h % 4) * P:(h % 4 + 1) * P], ws_rows[:, h, :], ident[:, :])
            give(tile_of["ws"], mm)
            named_block(("in_u", 0), ("u", 0), act_hi, act_lo, U_ODD_IN)
            for b in range(OUT_BLOCKS):
                blk = block_of[("in_v", b)]
                pe.wait_ge(w_lo_ready, blk + 1)
                t = tile_of[("v", b)]
                out = take(t)
                for c in range(CHUNKS):
                    rows = slice((c % 2) * CHUNK, (c % 2 + 1) * CHUNK)
                    for k in range(KT):
                        mm = product(out[:, c // 2, (c % 2) * BN:(c % 2 + 1) * BN],
                                     (act_hi[:, k, c // 2, rows], act_lo[:, k, c // 2, rows]),
                                     (w_hi[:, blk % 2, k, :], w_lo[:, blk % 2, k, :]), k == 0, k == KT - 1)
                give(t, mm)
                t = tile_of[("v_sample", b)]
                out = take(t)
                pe.wait_ge(in_s_ready, 2)
                for k in range(KT):
                    mm = product(out[0:NS, 0, 0:BN], (in_s_hi[:, k, :], in_s_lo[:, k, :]),
                                 (w_hi[:, blk % 2, k, :], w_lo[:, blk % 2, k, :]), k == 0, k == KT - 1)
                give(t, mm)
            for b in range(1, OUT_BLOCKS):
                named_block(("in_u", b), ("u", 2 * b), act_hi, act_lo, None)
            ada(1, SC2)
            out = take(tile_of["rep"])
            pe.wait_ge(ws_masked, 1)
            mm = nc.tensor.matmul(out[0:NS, 0, 0:HEADS * SEQ_S], replicate[:, :, :], ws_t[:, :, 0:SEQ_S], start=True, stop=True)
            give(tile_of["rep"], mm)
            pe.wait_ge(v_ready, CHUNKS + 1)
            freed(pe, tile_of["rep"])
            for h in range(HEADS):
                out = take(tile_of[("spatial", h)])
                cols = slice(h * P, (h + 1) * P)
                for c in range(CHUNKS):
                    nc.tensor.matmul(out[:, c // 2, (c % 2) * CHUNK:(c % 2 + 1) * CHUNK], v[:, c, cols], ws_t[:, h, :],
                                     start=True, stop=True, skip_group_check=True)
                for s in range(2):
                    mm = nc.tensor.matmul(out[:, s, HP:HALF], v_s[:, cols], ws_seq[:, h, s * HB:(s + 1) * HB, :],
                                          start=True, stop=True, skip_group_check=True)
                give(tile_of[("spatial", h)], mm)
            for b in range(OUT_BLOCKS):
                named_block(("out_c", b), ("out_c", 2 * b), act_hi, act_lo, None if b else U_ODD_OUT)
            ada(1, GT2)
            stat(tile_of[("stat", 3)], ones_d, 4 * KT)
            ffn(1, U_FFN_IN1, U_FFN1)
            stat(tile_of[("stat", 4)], ones_d, 5 * KT)
            pe.wait_ge(y_ready, KT)
            for c in range(CHUNKS):
                out = take(tile_of[("y", c)])
                for k in range(KT):
                    mm = nc.tensor.transpose(out[:, k // 4, (k % 4) * P:(k % 4 + 1) * P],
                                             y_t[:, k, c // 2, (c % 2) * CHUNK:(c % 2 + 1) * CHUNK], ident[:, :])
                give(tile_of[("y", c)], mm)
            for h in range(2):
                t = tile_of[("y_sample", h)]
                out = take(t)
                for k in range(KT):
                    mm = nc.tensor.transpose(out[0:HS, k // 4, (k % 4) * P:(k % 4 + 1) * P], y_t[:, k, h, HP:HALF],
                                             ident[:, :])
                give(t, mm)

        @block.scalar
        def _(act):
            own = Own(act, act_step)
            squares = [0]

            def weights_hi(b, i, t_used=None, per_b=None, per_i=None, per_t=None):
                def at(n, per):
                    return n if per is None else per + n
                act.wait_ge(raw_full[i % RAW], at(16 * (i // RAW + 1), per_i))
                if per_b is not None:
                    full(act, t_used, per_t)
                elif b >= 2:
                    full(act, last_tile_of[b - 2])
                nc.scalar.activation(w_hi[:, b % 2, :, :].rearrange("p k n -> p (k n)"), raw[:, i % RAW, :],
                                     ACT.Copy).then_inc(w_hi_ready, 1)

            def named_hi(name):
                weights_hi(block_of[name], item_of[name])

            def piece_to_hi(dst, n, per=None):
                act.wait_ge(piece_ready, n + 1 if per is None else per + (n + 1))
                nc.scalar.activation(flat(dst), flat(piece[:, n % 2]), ACT.Copy).then_inc(piece_hi, 1)

            def square(src, waits):
                n = squares[0]
                for s, c in waits:
                    act.wait_ge(s, c)
                if n >= 2:
                    act.wait_ge(ss_added, n - 1)
                nc.scalar.activation(flat(sq[:, n % 2]), flat(src), ACT.Square).then_inc(sq_ready, 1)
                squares[0] += 1

            def square_x(m, adds):
                square(x[:, m], [(x_prompt_done, adds + 1), (x_sample_done, adds + 1)])

            def norm_pieces_hi(layer, sh, unit, nth):
                act.wait_ge(scale_ready, nth + 1)
                for k in range(KT):
                    n = unit + k
                    act.wait_ge(xr_ready, nth * KT + k + 1)
                    if n >= 2:
                        act.wait_ge(piece_lo, n - 1)
                    done = own.step(nc.scalar.activation(prompt(piece[:, n % 2]), prompt(work[:, k % 2]), ACT.Identity,
                                                         bias=mod[:, layer, sh, k, 0:1], scale=scale[:, k, 0:1]))
                    own.after(done)
                    piece_to_hi(act_hi[:, k], n)

            def root(t, n):
                full(act, t)
                nc.scalar.activation(rstd[:, :, :], pair(t)[:, :, 0:HALF], ACT.Sqrt, bias=eps[:, 0:1]).then_inc(root_ready, 1)

            def relu(t, n, per_t=None, per_u=None):
                full(act, t, per_t)
                act.wait_ge(piece_ready, n - 1 if per_u is None else per_u + (n - 1))
                nc.scalar.activation(work[:, n % 2], pair(t)[:, :, 0:HALF], ACT.Relu).then_inc(psum_free[t % PAIRS], 1)

            def quarter(layer, q, units, adds=None, per=None, last=False, following=None):
                b0, i0, t0 = (block_of[("ffn", layer, q, 0)], item_of[("ffn", layer, q, 1)] - 1, tile_of[("ffn", layer, q, 0)])
                per_b = None if per is None else per * FFN_BLOCKS
                per_i = None if per is None else per * (16 * FFN_BLOCKS // RAW)
                per_t = None if per is None else per * (2 * FFN_BLOCKS // PAIRS)
                per_u = None if per is None else per * KT
                for j in range(FFN_BLOCKS):
                    if j < FFN_BLOCKS - 1 or not last:
                        weights_hi(b0 + j + 1, i0 + j + 1, t0 + 2 * j - 1, per_b, per_i, per_t)
                    elif following:
                        named_hi(following)
                    if last and j > OUT_BLOCKS:
                        for m in range(2 * (j - 1) - KT, 2 * j - KT):
                            square_x(m, adds + m)
                    if j < OUT_BLOCKS:
                        for m in range(2 * j, 2 * j + 2):
                            relu(t0 + m, units + m, per_t, per_u)
                            if m:
                                piece_to_hi(f_hi[:, m - 1], units + m - 1, per_u)
                    elif j == OUT_BLOCKS:
                        piece_to_hi(f_hi[:, KT - 1], units + KT - 1, per_u)

            def ffn(layer, units, adds, following=None):
                with act.Fori(0, QUARTERS - 1) as q:
                    quarter(layer, 0, units, per=q)
                done = (QUARTERS - 1) * KT
                quarter(layer, QUARTERS - 1, units + done, adds + done, last=True, following=following)
                for m in range(KT - 2, KT):
                    square_x(m, adds + done + m)

            def diagonals(lo, hi):
                for tap in range(lo, hi):
                    if tap >= DIAGS:
                        act.wait_ge(diag_used, tap - DIAGS + 1)
                    nc.scalar.activation(diag[:, tap % DIAGS, :], ident[:, :], ACT.Copy, scale=w_dw_v[:, tap, 0:1])\
                      .then_inc(diag_ready, 1)

            act.dma_start(vec_rows[0:16, 0, :], I["g_mix"].rearrange("l (k p) -> (l k) p", p=P)).then_inc(vec_loaded, 16)
            act.dma_start(vec_rows[16:32, 0, :], I["g_ffn"].rearrange("l (k p) -> (l k) p", p=P)).then_inc(vec_loaded, 16)
            act.dma_start(vec_rows[32:40, 0, :], I["g_final"].rearrange("(k p) -> k p", p=P)).then_inc(vec_loaded, 16)
            for i, name in enumerate(("b_dw", "g_conv_ln", "b_conv_ln", "s_pool")):
                act.dma_start(vec_rows[40 + 4 * i:44 + 4 * i, 0, :],
                              I[name][0].rearrange("(k p) -> k p", p=P)).then_inc(vec_loaded, 16)
            act.dma_start(vec_rows[0:NB_ADA, 1, :], I["b_ada"].rearrange("l (k p) -> (l k) p", p=P)).then_inc(vec_loaded, 16)
            act.dma_start(vec_rows[0:NTAP, 2, :], I["w_dw"][0].rearrange("t (j p) -> (t j) p", p=P)).then_inc(vec_loaded, 16)
            act.dma_start(w_pool_sb[:, :, :], I["w_pool"][0].rearrange("g i o -> i g o")).then_inc(pool_w_loaded, 16)
            for h in range(2):
                act.dma_start(conv_rows[:, h, :], I["state_conv"][0, h * HB:(h + 1) * HB].rearrange("b r c -> (b r) c"))\
                   .then_inc(hist_loaded, 16)
            act.dma_start(pool_rows[:, :], I["state_pool"][0].rearrange("b r c -> (b r) c")).then_inc(hist_loaded, 16)

            act.wait_ge(c_loaded, 32)
            c_sig = sq[0:32].rearrange("p i h t -> p (i h t)")[:, 0:D]
            nc.scalar.activation(c_sig, c_rows[:, :], ACT.Sigmoid).then_inc(c_sigmoid, 1)
            full(act, tile_of["vec"])
            nc.scalar.activation(vec[:, :], pair(tile_of["vec"])[:, 0, 0:NVEC + NB_ADA + NTAP], ACT.Copy)\
              .then_inc(psum_free[tile_of["vec"] % PAIRS], 1)
            full(act, tile_of["cT"])
            nc.scalar.activation(cT.rearrange("p k c -> p (k c)"), pair(tile_of["cT"])[:, 0, 0:32 * KT], ACT.Copy)\
              .then_inc(psum_free[tile_of["cT"] % PAIRS], 1)
            for k in range(KT + 1):
                if k < KT:
                    t = tile_of[("x", k)]
                    full(act, t)
                    nc.scalar.activation(x[:, k], pair(t)[:, :, 0:HALF], ACT.Copy).then_inc(psum_free[t % PAIRS], 1)
                if k:
                    t = tile_of[("x", k - 1)]
                    square(x[:, k - 1], [(psum_free[t % PAIRS], uses(t))])
            act.wait_ge(consts_ready, 5)
            root(tile_of[("stat", 0)], 1)
            named_hi(("in_ab", 0))
            for j in range(AT):
                t = tile_of[("conv_hist", j)]
                full(act, t)
                nc.scalar.activation(a_ext_s[:, j, :, 0:HIST].rearrange("p (h b) r -> p h b r", h=2),
                                     pair(t)[:, :, 0:HB * HIST].rearrange("p h (b r) -> p h b r", r=HIST),
                                     ACT.Copy).then_inc(psum_free[t % PAIRS], 1)
            t = tile_of["pool_hist"]
            full(act, t)
            nc.scalar.activation(p_ext_s[:, :, :, 0:PHIST],
                                 pair(t)[:, 0, 0:AT * BATCH_S * PHIST].rearrange("p (j b r) -> p j b r", j=AT, r=PHIST),
                                 ACT.Copy).then_inc(psum_free[t % PAIRS], 1)
            norm_pieces_hi(0, SH1, U_MIX_IN, 0)
            for b in range(MIX_BLOCKS_IN):
                named_hi(("in_ab", b + 1) if b + 1 < MIX_BLOCKS_IN else ("out_ab", 0))
                kind, first = IN_AB[b]
                for m in range(first, first + 2):
                    t = tile_of[(kind, m)]
                    if kind == "gate":
                        full(act, t)
                        if m >= 2:
                            act.wait_ge(a_ready, m - 1)
                            freed(act, tile_of[("value", m - 2)])
                        nc.scalar.activation(work[:, m % 2], pair(t)[:, :, 0:HALF], ACT.Sigmoid).then_inc(psum_free[t % PAIRS], 1)
                    elif kind == "pool":
                        full(act, t)
                        nc.scalar.activation(p_ext[:, m, PHIST:PHIST + SEQ].rearrange("p (h t) -> p h t", h=2),
                                             prompt(pair(t)), ACT.Copy).then_inc(p_ready, 1)
                        nc.scalar.activation(p_ext_s[:, m, :, PHIST:PHIST + SEQ_S].rearrange("p (h b) t -> p h b t", h=2),
                                             sample(pair(t)), ACT.Copy).then_inc(psum_free[t % PAIRS], 1)
                if b == MIX_BLOCKS_IN - 2:
                    diagonals(0, DIAGS)
            named_hi(("out_ab", 1))
            for g in range(AT):
                freed(act, tile_of[("pool", g)])
            nc.scalar.activation(new_s[:, 1].rearrange("p j (b t) -> p j b t", t=SEQ_S), p_ext_s[:, :, :, PHIST:PHIST + SEQ_S],
                                 ACT.Copy).then_inc(new_s_ready, 1)
            freed(act, tile_of[("value", AT - 1)])
            nc.scalar.activation(new_s[:, 0].rearrange("p j (b t) -> p j b t", t=SEQ_S), a_ext_s[:, :, :, HIST:HIST + SEQ_S],
                                 ACT.Copy).then_inc(new_s_ready, 1)
            diagonals(DIAGS, PE_TAPS)
            t = tile_of["conv_pe"]
            full(act, t)
            nc.scalar.activation(conv_part[:, :, :], prompt(pair(t)), ACT.Copy).then_inc(psum_free[t % PAIRS], 1)
            for g in range(AT):
                t, n = tile_of[("pool_mix", g)], U_MIX_OUT + g
                full(act, t)
                act.wait_ge(piece_lo, n - 1)
                nc.scalar.activation(sample(piece[:, n % 2]), sample(pair(t)), ACT.Copy, scale=s_pool_v[:, g:g + 1])\
                  .then_inc(piece_ready, 1)
                nc.scalar.activation(prompt(piece[:, n % 2]), prompt(pair(t)), ACT.Copy, scale=s_pool_v[:, g:g + 1])\
                  .then_inc(psum_free[t % PAIRS], 1)
                freed(act, t)
                piece_to_hi(act_hi[:, AT + g], n)
            for name, rows in (("conv_state", conv_state_rows), ("pool_state", pool_state_rows)):
                t = tile_of[name]
                full(act, t)
                nc.scalar.activation(rows, pair(t)[0:NS], ACT.Copy).then_inc(psum_free[t % PAIRS], 1)
            for j in range(AT):
                if j < AT - 1:
                    act.wait_ge(centred, j + 1)
                else:
                    freed(act, tile_of["conv_mean"])
                nc.scalar.activation(flat(channel_squares[:, j]), flat(acc[:, j]), ACT.Square).then_inc(channel_sq, 1)
            root(tile_of["conv_var"], 2)
            for j in range(AT + 1):
                if j < AT:
                    act.wait_ge(norm_ready, j + 1)
                    nc.scalar.activation(flat(acc[:, j]), flat(work[:, j % 2]), ACT.Identity, bias=b_cln_v[:, j:j + 1],
                                         scale=g_cln_v[:, j:j + 1]).then_inc(affine_ready, 1)
                    if j >= 2:
                        act.wait_ge(piece_ready, U_MIX_OUT + AT + j - 1)
                    nc.scalar.activation(flat(sq[:, j % 2]), flat(work[:, j % 2]), ACT.Sigmoid, bias=b_cln_v[:, j:j + 1],
                                         scale=g_cln_v[:, j:j + 1]).then_inc(silu_ready, 1)
                if j:
                    piece_to_hi(act_hi[:, j - 1], U_MIX_OUT + AT + j - 1)

            def project(name, adds, following, split=1):
                for b in range(OUT_BLOCKS):
                    if b + 1 >= split:
                        named_hi((name, b + 1) if b + 1 < OUT_BLOCKS else following)
                    for m in range(2 * b - 2, 2 * b):
                        if m >= 0:
                            square_x(m, adds + m)
                for m in range(KT - 2, KT):
                    square_x(m, adds + m)

            project("out_ab", G_EVEN, ("ffn", 0, 0, 0), split=2)
            root(tile_of[("stat", 1)], 3)
            norm_pieces_hi(0, SH2, U_FFN_IN0, 1)
            ffn(0, U_FFN0, G_FFN0, ("in_u", 0))
            root(tile_of[("stat", 2)], 4)
            t = tile_of["ws"]
            full(act, t)
            nc.scalar.activation(ws_t.rearrange("p (a h) t -> p a (h t)", a=2), pair(t), ACT.Copy).then_inc(psum_free[t % PAIRS], 1)
            norm_pieces_hi(1, SH1, U_ODD_IN, 2)
            sequence = [("in_u", 0), *[("in_v", b) for b in range(OUT_BLOCKS)], *[("in_u", b) for b in range(1, OUT_BLOCKS)]]
            act.wait_ge(piece_lo, U_ODD_IN + KT)
            for dst, src in ((in_s_hi, act_hi), (in_s_lo, act_lo)):
                nc.scalar.activation(dst.rearrange("p k (h t) -> p k h t", h=2), src[:, :, :, HP:HALF].bitcast(F32),
                                     ACT.Copy).then_inc(in_s_ready, 1)
            for n, (name, b) in enumerate(sequence):
                named_hi(sequence[n + 1] if n + 1 < len(sequence) else ("out_c", 0))
                if name == "in_u":
                    for m in (2 * b, 2 * b + 1):
                        t = tile_of[("u", m)]
                        full(act, t)
                        nc.scalar.activation(u[:, m], pair(t)[:, :, 0:HALF], ACT.Copy).then_inc(psum_free[t % PAIRS], 1)
                else:
                    t = tile_of[("v", b)]
                    full(act, t)
                    nc.scalar.activation(v[:, :, b * BN:(b + 1) * BN].rearrange("p (a c) n -> p a c n", a=2),
                                         pair(t).rearrange("p a (c n) -> p a c n", n=BN), ACT.Copy).then_inc(psum_free[t % PAIRS], 1)
                    t = tile_of[("v_sample", b)]
                    full(act, t)
                    nc.scalar.activation(v_s[:, b * BN:(b + 1) * BN], pair(t)[0:NS, 0, 0:BN], ACT.Copy)\
                      .then_inc(psum_free[t % PAIRS], 1)
                for c in {4: (0,), 5: (1, 2), 6: (3, 4)}.get(n, ()):
                    act.wait_ge(v_centred, c + 1)
                    if c >= 2:
                        act.wait_ge(v_var, c - 1)
                    rows, src = (NS, v_s[:, :]) if c == CHUNKS else (P, v[:, c, :])
                    nc.scalar.activation((sq, work)[c % 2][0:rows].rearrange("p i h t -> p (i h t)")[:, 0:D], src,
                                         ACT.Square).then_inc(v_sq, 1)
                    act.wait_ge(v_var, c + 1)
                    nc.scalar.activation(lnst[0:rows, c, 2:3], lnst[0:rows, c, 1:2], ACT.Sqrt, bias=eps[0:rows, 0:1],
                                         scale=1.0 / D).then_inc(v_root, 1)
            for h in range(HEADS):
                piece_to_hi(act_hi[:, h], U_ODD_OUT + h)
            project("out_c", G_ODD, ("ffn", 1, 0, 0))
            root(tile_of[("stat", 3)], 5)
            norm_pieces_hi(1, SH2, U_FFN_IN1, 3)
            ffn(1, U_FFN1, G_FFN1)
            root(tile_of[("stat", 4)], 6)
            for k in range(KT):
                act.wait_ge(norm_ready, AT + k + 1)
                nc.scalar.activation(flat(y_t[:, k]), flat(work[:, k % 2]), ACT.Copy, scale=g_final_v[:, k:k + 1]).then_inc(y_ready, 1)
            for c in range(CHUNKS):
                t = tile_of[("y", c)]
                full(act, t)
                nc.scalar.activation(y_rows[:, c, :].rearrange("p (a n) -> p a n", a=2), pair(t), ACT.Copy)\
                  .then_inc(psum_free[t % PAIRS], 1)
            for h in range(2):
                t = tile_of[("y_sample", h)]
                full(act, t)
                nc.scalar.activation(ys_rows[:, h, :].rearrange("p (a n) -> p a n", a=2), pair(t)[0:HS], ACT.Copy)\
                  .then_inc(psum_free[t % PAIRS], 1)

        @block.vector
        def _(dve):
            own = Own(dve, dve_step)
            dv = nc.vector
            adds = [0]
            squares = [0]

            def weights_lo(b, i, per_b=None):
                dve.wait_ge(w_hi_ready, b + 1 if per_b is None else per_b + (b + 1))
                dv.tensor_tensor(w_lo[:, b % 2, :, :].rearrange("p k n -> p (k n)"), raw[:, i % RAW, :],
                                 w_hi[:, b % 2, :, :].rearrange("p k n -> p (k n)").bitcast(F32), ALU.subtract)\
                  .then_inc(w_lo_ready, 1)

            def named_lo(name):
                weights_lo(block_of[name], item_of[name])

            def piece_free(n, per=None):
                if per is not None or n >= 2:
                    dve.wait_ge(piece_lo, n - 1 if per is None else per + (n - 1))

            def piece_to_lo(dst_lo, dst_hi, n, per=None):
                dve.wait_ge(piece_hi, n + 1 if per is None else per + (n + 1))
                dv.tensor_tensor(flat(dst_lo), flat(piece[:, n % 2]), flat(dst_hi).bitcast(F32), ALU.subtract)\
                  .then_inc(piece_lo, 1)

            def sum_into_ss(src, first):
                n = adds[0]
                if n:
                    dve.wait_ge(ss_added, n)
                if first:
                    dv.tensor_copy(flat(ss), flat(src)).then_inc(ss_added, 1)
                else:
                    dv.tensor_tensor(flat(ss), flat(ss), flat(src), ALU.add).then_inc(ss_added, 1)
                adds[0] += 1

            def sum_square(first):
                n = squares[0]
                dve.wait_ge(sq_ready, n + 1)
                sum_into_ss(sq[:, n % 2], first)
                squares[0] += 1

            def inverse_root(t, n):
                dve.wait_ge(root_ready, n)
                dv.reciprocal(flat(rstd), flat(rstd)).then_inc(psum_free[t % PAIRS], 1)
                freed(dve, t)

            def modulation(layer, i):
                t = tile_of[("ada", layer, i)]
                full(dve, t)
                own.after(own.n)
                dv.transpose(mod_t.rearrange("p k c -> p (k c)"), pair(t)[:, 0, 0:2 * P]).then_inc(psum_free[t % PAIRS], 1)
                freed(dve, t)
                own.step(dv.tensor_tensor(mod[:, layer, i], mod_t[:, :, 0:NCOND],
                                          b_ada_v[:, layer, i, :].unsqueeze(2).broadcast_to([P, KT, NCOND]), ALU.add))

            def norm_pieces(layer, sc, gains, unit, nth):
                own.after(own.n)
                dv.scalar_tensor_tensor(scale[:, :, :], mod[:, layer, sc], 1.0,
                                        gains.unsqueeze(2).broadcast_to([P, KT, NCOND]), ALU.add, ALU.mult)\
                  .then_inc(scale_ready, 1)
                for k in range(KT):
                    if k >= 2:
                        dve.wait_ge(piece_hi, unit + k - 1)
                    dv.tensor_tensor(flat(work[:, k % 2]), flat(x[:, k]), flat(rstd), ALU.mult).then_inc(xr_ready, 1)
                    if k:
                        piece_to_lo(act_lo[:, k - 1], act_hi[:, k - 1], unit + k - 1)
                piece_to_lo(act_lo[:, KT - 1], act_hi[:, KT - 1], unit + KT - 1)

            def gated_add(a, m, t, layer, gate, per_a=None, per_t=None):
                def at(n):
                    return n if per_a is None else per_a + n
                gates = mod[:, layer, gate, m, :]
                full(dve, t, per_t)
                if a >= KT:
                    dve.wait_ge(x_prompt_done, at(a - KT + 1))
                    dve.wait_ge(x_sample_done, at(a - KT + 1))
                dv.scalar_tensor_tensor(prompt(x[:, m]), prompt(pair(t)), gates[:, 0:1], prompt(x[:, m]),
                                        ALU.mult, ALU.add).then_inc(x_prompt_done, 1)
                if a >= 2:
                    dve.wait_ge(x_sample_done, at(a - 1))
                tmp = gated_s[:, a % 2, :].rearrange("p (h b t) -> p h b t", h=2, t=SEQ_S)
                dve.wait_ge(x_prompt_done, at(a + 1))
                dv.tensor_tensor(tmp, sample(pair(t)), per_seq(gates), ALU.mult).then_inc(psum_free[t % PAIRS], 1)
                freed(dve, t, per_t)
                dv.tensor_tensor(sample(x[:, m]), sample(x[:, m]), tmp, ALU.add).then_inc(x_sample_done, 1)

            def quarter(layer, units, a0, q=0, per=None, last=False, following=None):
                b0, i0, t0 = (block_of[("ffn", layer, q, 0)], item_of[("ffn", layer, q, 1)] - 1, tile_of[("ffn", layer, q, 0)])
                per_b = None if per is None else per * FFN_BLOCKS
                per_t = None if per is None else per * (2 * FFN_BLOCKS // PAIRS)
                per_u = None if per is None else per * KT
                for j in range(FFN_BLOCKS):
                    if j < FFN_BLOCKS - 1 or not last:
                        weights_lo(b0 + j + 1, i0 + j + 1, per_b)
                    elif following:
                        named_lo(following)
                    for m in range(2 * j, 2 * j + 2):
                        if j < OUT_BLOCKS:
                            n = units + m
                            piece_free(n, per_u)
                            freed(dve, t0 + m, per_t)
                            dv.tensor_tensor(flat(piece[:, n % 2]), flat(work[:, n % 2]), flat(work[:, n % 2]), ALU.mult)\
                              .then_inc(piece_ready, 1)
                            if m:
                                piece_to_lo(f_lo[:, m - 1], f_hi[:, m - 1], n - 1, per_u)
                        else:
                            if m == KT:
                                piece_to_lo(f_lo[:, KT - 1], f_hi[:, KT - 1], units + KT - 1, per_u)
                            gated_add(a0 + m - KT, m - KT, t0 + m, layer, GT2, per_u, per_t)
                            if last and m > KT:
                                sum_square(m == KT + 1)
                if last:
                    sum_square(False)

            def ffn(layer, units, a0, following=None):
                with dve.Fori(0, QUARTERS - 1) as q:
                    quarter(layer, units, a0, per=q)
                done = (QUARTERS - 1) * KT
                quarter(layer, units + done, a0 + done, q=QUARTERS - 1, last=True, following=following)

            def project(name, a0, layer, following, split=1):
                for b in range(OUT_BLOCKS):
                    if b + 1 >= split:
                        named_lo((name, b + 1) if b + 1 < OUT_BLOCKS else following)
                    for m in range(2 * b, 2 * b + 2):
                        gated_add(a0 + m, m, tile_of[(name, m)], layer, GT1)
                        if m:
                            sum_square(m == 1)
                    if name == "out_ab" and b in MOD_IN_OUT:
                        modulation(1, MOD_IN_OUT[b])
                sum_square(False)

            dve.wait_ge(c_sigmoid, 1)
            c_sig = sq[0:32].rearrange("p i h t -> p (i h t)")[:, 0:D]
            dv.tensor_tensor(c_rows[:, :], c_rows[:, :], c_sig, ALU.mult).then_inc(c_silu, 1)
            for k in range(KT):
                sum_square(k == 0)
            freed(dve, tile_of["vec"])
            inverse_root(tile_of[("stat", 0)], 1)
            modulation(0, SH1)
            named_lo(("in_ab", 0))
            modulation(0, SC1)
            norm_pieces(0, SC1, g_mix_v[:, 0, :], U_MIX_IN, 0)
            dve.wait_ge(pads_ready, 2)
            conv_ops = [(j, tap) for j in range(1, AT) for tap in range(TAPS + 1)]
            conv_ops += [(0, tap) for tap in range(PE_TAPS, TAPS + 2)]
            at_op = [0]

            def convolve(count):
                for _ in range(count):
                    if at_op[0] == len(conv_ops):
                        return
                    j, tap = conv_ops[at_op[0]]
                    n = at_op[0]
                    at_op[0] += 1
                    even = prompt(acc[:, j])
                    odd = acc_odd[:, j % 2, :].rearrange("p (h t) -> p h t", h=2)
                    if n >= 2:
                        dve.wait_ge(conv_step, n - 1 if tap < TAPS else n)
                    if tap == TAPS + 1:
                        freed(dve, tile_of["conv_pe"])
                        dv.tensor_tensor(even, even, conv_part[:, :, :], ALU.add).then_inc(conv_step, 1)
                        continue
                    if tap == TAPS:
                        dv.tensor_tensor(even, even, odd, ALU.add).then_inc(conv_step, 1)
                        continue
                    src = a_ext[:, j, tap:tap + SEQ].rearrange("p (h t) -> p h t", h=2)
                    w = w_dw_v[:, tap, j:j + 1]
                    nth = tap if j else tap - PE_TAPS
                    dst = odd if nth % 2 else even
                    if nth == 0:
                        dv.tensor_scalar(dst, src, w, b_dw_v[:, j:j + 1], ALU.mult, ALU.add).then_inc(conv_step, 1)
                    elif nth == 1:
                        dv.tensor_scalar(dst, src, w, None, ALU.mult).then_inc(conv_step, 1)
                    else:
                        dv.scalar_tensor_tensor(dst, src, w, dst, ALU.mult, ALU.add).then_inc(conv_step, 1)

            for b in range(MIX_BLOCKS_IN):
                named_lo(("in_ab", b + 1) if b + 1 < MIX_BLOCKS_IN else ("out_ab", 0))
                kind, first = IN_AB[b]
                for m in range(first, first + 2) if kind == "gate" else ():
                    t_a, t_g = tile_of[("value", m)], tile_of[("gate", m)]
                    full(dve, t_a)
                    freed(dve, t_g)
                    dv.tensor_tensor(a_ext[:, m, HIST:HIST + SEQ].rearrange("p (h t) -> p h t", h=2), prompt(pair(t_a)),
                                     prompt(work[:, m % 2]), ALU.mult).then_inc(a_ready, 1)
                    dve.wait_ge(a_ready, m + 1)
                    dv.tensor_tensor(a_ext_s[:, m, :, HIST:HIST + SEQ_S].rearrange("p (h b) t -> p h b t", h=2),
                                     sample(pair(t_a)), sample(work[:, m % 2]), ALU.mult).then_inc(psum_free[t_a % PAIRS], 1)
                    freed(dve, t_a)
                if b >= 1:
                    convolve(15)
                if b in MOD_AFTER:
                    modulation(0, MOD_AFTER[b])
            named_lo(("out_ab", 1))
            convolve(len(conv_ops) - at_op[0] - 2 * AT)
            for g in range(AT):
                piece_to_lo(act_lo[:, AT + g], act_hi[:, AT + g], U_MIX_OUT + g)
                convolve(2)
            dve.wait_ge(conv_step, CONV_STEPS)
            t = tile_of["conv_mean"]
            full(dve, t)
            for j in range(AT):
                dv.tensor_tensor(acc[:, j], acc[:, j], pair(t)[:, :, 0:HALF], ALU.subtract)\
                  .then_inc(centred if j < AT - 1 else psum_free[t % PAIRS], 1)
            modulation(0, GT2)
            inverse_root(tile_of["conv_var"], 2)
            dve.wait_ge(centred, AT - 1)
            freed(dve, t)
            for j in range(AT + 2):
                if j < AT:
                    if j >= 2:
                        dve.wait_ge(silu_ready, j - 1)
                    dv.tensor_tensor(flat(work[:, j % 2]), flat(acc[:, j]), flat(rstd), ALU.mult).then_inc(norm_ready, 1)
                if 0 < j <= AT:
                    n = U_MIX_OUT + AT + j - 1
                    dve.wait_ge(affine_ready, j)
                    dve.wait_ge(silu_ready, j)
                    piece_free(n)
                    dv.tensor_tensor(flat(piece[:, n % 2]), flat(acc[:, j - 1]), flat(sq[:, (j - 1) % 2]), ALU.mult)\
                      .then_inc(piece_ready, 1)
                if j > 1:
                    piece_to_lo(act_lo[:, j - 2], act_hi[:, j - 2], U_MIX_OUT + AT + j - 2)
            project("out_ab", G_EVEN, 0, ("ffn", 0, 0, 0), split=2)
            inverse_root(tile_of[("stat", 1)], 3)
            norm_pieces(0, SC2, g_ffn_v[:, 0, :], U_FFN_IN0, 1)
            ffn(0, U_FFN0, G_FFN0, ("in_u", 0))
            modulation(1, SH2)
            inverse_root(tile_of[("stat", 2)], 4)
            norm_pieces(1, SC1, g_mix_v[:, 1, :], U_ODD_IN, 2)

            def v_norm(c):
                rows, src = (NS, v_s[:, :]) if c == CHUNKS else (P, v[:, c, :])
                own.after(own.n)
                own.step(dv.reduce_sum(lnst[0:rows, c, 0:1], src, AX_X))
                own.after(own.n)
                own.step(dv.tensor_scalar(lnst[0:rows, c, 0:1], lnst[0:rows, c, 0:1], 1.0 / D, None, ALU.mult))
                own.after(own.n)
                dv.tensor_scalar(src, src, lnst[0:rows, c, 0:1], None, ALU.subtract).then_inc(v_centred, 1)
                dve.wait_ge(v_sq, c + 1)
                own.step(dv.reduce_sum(lnst[0:rows, c, 1:2],
                                       (sq, work)[c % 2][0:rows].rearrange("p i h t -> p (i h t)")[:, 0:D], AX_X))
                own.after(own.n)
                dv.tensor_copy(lnst[0:rows, c, 3:4], lnst[0:rows, c, 1:2]).then_inc(v_var, 1)
                dve.wait_ge(v_root, c + 1)
                own.step(dv.reciprocal(lnst[0:rows, c, 2:3], lnst[0:rows, c, 2:3]))
                own.after(own.n)
                own.step(dv.scalar_tensor_tensor(src, src, lnst[0:rows, c, 2:3], g_v[0:rows, :], ALU.mult, ALU.mult))
                own.after(own.n)
                dv.tensor_tensor(src, src, b_v[0:rows, :], ALU.add).then_inc(v_ready, 1)

            dve.wait_ge(odd_loaded, 64)
            sequence = [("in_u", 0), *[("in_v", b) for b in range(OUT_BLOCKS)], *[("in_u", b) for b in range(1, OUT_BLOCKS)]]
            for n, (name, b) in enumerate(sequence):
                named_lo(sequence[n + 1] if n + 1 < len(sequence) else ("out_c", 0))
                if n == 4:
                    freed(dve, tile_of[("v", OUT_BLOCKS - 1)])
                    freed(dve, tile_of[("v_sample", OUT_BLOCKS - 1)])
                for c in {4: (0,), 5: (1, 2), 6: (3, 4)}.get(n, ()):
                    v_norm(c)
            modulation(1, SC2)
            t = tile_of["rep"]
            full(dve, t)
            for h in range(HEADS):
                mm = dv.tensor_tensor(
                    ws_seq[:, h],
                    pair(t)[0:NS, 0, h * SEQ_S:(h + 1) * SEQ_S].unsqueeze(1).broadcast_to([NS, BATCH_S, SEQ_S]),
                    same_seq[:, :].unsqueeze(2).broadcast_to([NS, BATCH_S, SEQ_S]), ALU.mult)
                if h < HEADS - 1:
                    own.step(mm)
                else:
                    mm.then_inc(psum_free[t % PAIRS], 1)
            freed(dve, tile_of[("u", KT - 1)])
            own.after(own.n)
            for h in range(HEADS):
                t = tile_of[("spatial", h)]
                n = U_ODD_OUT + h
                full(dve, t)
                bias = b_s[:, h, :]
                part = own.step(dv.tensor_tensor(
                    prompt(work[:, h % 2]).rearrange("p h (c t) -> p h c t", t=CHUNK),
                    prompt(pair(t)).rearrange("p h (c t) -> p h c t", t=CHUNK),
                    bias.unsqueeze(1).unsqueeze(1).broadcast_to([P, 2, 2, CHUNK]), ALU.add))
                own.after(part)
                dv.tensor_tensor(sample(work[:, h % 2]), sample(pair(t)),
                                 bias[:, 0:SEQ_S].unsqueeze(1).unsqueeze(1).broadcast_to([P, 2, HB, SEQ_S]), ALU.add)\
                  .then_inc(psum_free[t % PAIRS], 1)
                freed(dve, t)
                piece_free(n)
                dv.tensor_tensor(flat(piece[:, n % 2]), flat(work[:, h % 2]), flat(u[:, h]), ALU.mult).then_inc(piece_ready, 1)
                dve.wait_ge(piece_ready, n + 1)
                if h:
                    piece_to_lo(act_lo[:, h - 1], act_hi[:, h - 1], n - 1)
            piece_to_lo(act_lo[:, KT - 1], act_hi[:, KT - 1], U_ODD_OUT + KT - 1)
            project("out_c", G_ODD, 1, ("ffn", 1, 0, 0))
            modulation(1, GT2)
            inverse_root(tile_of[("stat", 3)], 5)
            norm_pieces(1, SC2, g_ffn_v[:, 1, :], U_FFN_IN1, 3)
            ffn(1, U_FFN1, G_FFN1)
            inverse_root(tile_of[("stat", 4)], 6)
            for k in range(KT):
                if k >= 2:
                    dve.wait_ge(y_ready, k - 1)
                dv.tensor_tensor(flat(work[:, k % 2]), flat(x[:, k]), flat(rstd), ALU.mult).then_inc(norm_ready, 1)


_INS = ["x_prompt", "x_sample", "c_prompt", "c_sample", "state_conv", "state_pool", "w_ada", "b_ada", "g_mix", "g_ffn",
        "w_in_ab", "w_dw", "b_dw", "g_conv_ln", "b_conv_ln", "w_pool", "s_pool", "w_out_ab", "w_in_c", "g_v_ln", "b_v_ln",
        "w_spatial", "b_spatial", "w_out_c", "w_ffn1", "w_ffn2", "g_final"]
_OUTS = [("y_prompt", (1, 512, 1024)), ("y_sample", (8, 4, 1024)), ("new_conv_prompt", (1, 1, 30, 512)),
         ("new_pool_prompt", (1, 1, 15, 512)), ("new_conv_sample", (1, 8, 30, 512)), ("new_pool_sample", (1, 8, 15, 512)),
         ("new_v_sample", (1, 8, 4, 1024))]


def kernel(**inputs):
    import numpy as _np
    import concourse.bacc as _bacc
    from concourse import mybir as _mybir
    from concourse.bass_utils import run_bass_kernel_spmd as _run

    nc = _bacc.Bacc("TRN2", target_bir_lowering=False, num_devices=1)
    arrays, ins, outs = {}, {}, {}
    for name in _INS:
        a = _np.ascontiguousarray(inputs[name])
        arrays[f"in_{name}_dram"] = a
        ins[name] = nc.dram_tensor(f"in_{name}_dram", a.shape, _mybir.dt.from_np(a.dtype), kind="ExternalInput").ap()
    for name, shape in _OUTS:
        outs[name] = nc.dram_tensor(f"out_{name}_dram", shape, _mybir.dt.float32, kind="ExternalOutput").ap()
    hybrid_decoder_step(nc, ins, outs)
    r = _run(nc, [arrays], core_ids=[0])
    return tuple(r.results[0][f"out_{name}_dram"] for name, _ in _OUTS)
```

```python
from contextlib import ExitStack

import concourse.bass as bass
from concourse import mybir

ALU = mybir.AluOpType
ACT = mybir.ActivationFunctionType
F32 = mybir.dt.float32
F32R = mybir.dt.float32r
AX_X = mybir.AxisListType.X

P = 128
D = 1024
KT = D // P
SEQ, BATCH_S, SEQ_S = 512, 8, 4
HP, HB = SEQ // 2, BATCH_S // 2
HS = HB * SEQ_S
HALF = HP + HS
NS = BATCH_S * SEQ_S
DA = D // 2
AT = DA // P
TAPS = 31
HIST = TAPS - 1
PHIST = 15
WINDOWS = (2, 4, 8, 16)
FF = 4 * D
QUARTERS = FF // D
HEADS = 8
CHUNK = 128
CHUNKS = SEQ // CHUNK
NCOND = 1 + BATCH_S
NMOD = 6
EPS = 1e-6
BN = 256
RAW = 4
PAIRS = 4
PE_TAPS = 22
CONV_STEPS = (AT - 1) * (TAPS + 1) + TAPS - PE_TAPS + 2
IN_AB = (("value", 0), ("gate", 0), ("value", 2), ("gate", 2), ("pool", 0), ("pool", 2))
MIX_BLOCKS_IN = len(IN_AB)
ADDS_AT, SQUARES_AT, ROOT_AT = 2, 3, 6
SECOND_HI_AT, SECOND_LO_AT = 6, 10
DIAGS = 8
OUT_BLOCKS = D // BN
FFN_BLOCKS = 2 * OUT_BLOCKS
CPM = 4
SH1, SC1, GT1, SH2, SC2, GT2 = range(NMOD)


MOD_AFTER = {1: GT1, 3: SH2, 4: SC2}
MOD_IN_OUT = {1: SH1, 2: SC1, 3: GT1}
IN_C = (*(("in_v", b) for b in range(4)), *(("in_u", b) for b in range(4)))
MOD_IN_C = {5: SH2, 7: SC2}
MOD_OUT_C = {3: GT2}
REPLICATE_AT = 5


class Own:

    def __init__(self, eng, sem):
        self.eng, self.sem, self.n = eng, sem, 0

    def step(self, instruction):
        instruction.then_inc(self.sem, 1)
        self.n += 1
        return self.n

    def after(self, n):
        self.eng.wait_ge(self.sem, n)


def plan():
    tile, item, block = {}, {}, {}
    blocks = chunks = 0
    order = []

    def tiles(*names):
        for n in names:
            assert n not in tile
            tile[n] = len(tile_list)
            tile_list.append(n)

    tile_list = []

    def load(name, is_block):
        nonlocal blocks, chunks
        item[name] = len(order)
        if is_block:
            block[name] = blocks
            blocks += 1
            order.append(("block", blocks))
        elif name[3] < CPM - 1:
            chunks += 1
            order.append(("ada", chunks))
        else:
            order.append(("tile", tile[name[:3]]))

    def load_ada(layer, i):
        for c in range(CPM):
            load(("ada", layer, i, c), False)

    tiles("vec", "cT")
    tiles(*[("x", k) for k in range(KT)])
    tiles(("ada", 0, SH1), ("stat", 0))
    tiles(*[("conv_hist", j) for j in range(AT)], "pool_hist", ("ada", 0, SC1))
    for b, (kind, m) in enumerate(IN_AB):
        tiles((kind, m), (kind, m + 1))
        if b in MOD_AFTER:
            tiles(("ada", 0, MOD_AFTER[b]))
    tiles("conv_pe", *[("pool_mix", g) for g in range(AT)], "conv_state", "pool_state")
    tiles("conv_mean", ("ada", 0, GT2), "conv_var")
    for b in range(OUT_BLOCKS):
        tiles(("out_ab", 2 * b), ("out_ab", 2 * b + 1))
        if b == OUT_BLOCKS - 1:
            tiles(("stat", 1))
        if b in MOD_IN_OUT:
            tiles(("ada", 1, MOD_IN_OUT[b]))
    tiles(*[("ffn", 0, q, m) for q in range(QUARTERS) for m in range(2 * KT)])
    tiles(("stat", 2), ("v", 0), "ws", ("v", 1), ("v_sample", 0), ("v_sample", 1))
    for n, (name, b) in enumerate(IN_C):
        if n >= 2:
            tiles(*((("v", b), ("v_sample", b)) if name == "in_v" else (("u", 2 * b), ("u", 2 * b + 1))))
        if n in MOD_IN_C:
            tiles(("ada", 1, MOD_IN_C[n]))
        if n == REPLICATE_AT:
            tiles("rep")
    tiles(*[("spatial", h) for h in range(HEADS)])
    for b in range(OUT_BLOCKS):
        tiles(("out_c", 2 * b), ("out_c", 2 * b + 1))
        if b == OUT_BLOCKS - 1:
            tiles(("stat", 3))
        if b in MOD_OUT_C:
            tiles(("ada", 1, MOD_OUT_C[b]))
    tiles(*[("ffn", 1, q, m) for q in range(QUARTERS) for m in range(2 * KT)])
    tiles(("stat", 4), *[("y", c) for c in range(CHUNKS)], ("y_sample", 0), ("y_sample", 1))

    load_ada(0, SH1)
    load(("in_ab", 0), True)
    load_ada(0, SC1)
    load(("in_ab", 1), True)
    for b in range(2, MIX_BLOCKS_IN):
        load(("in_ab", b), True)
        if b - 1 in MOD_AFTER:
            load_ada(0, MOD_AFTER[b - 1])
    load(("out_ab", 0), True)
    load(("out_ab", 1), True)
    load_ada(0, GT2)
    for b in range(2, OUT_BLOCKS):
        load(("out_ab", b), True)
        load_ada(1, MOD_IN_OUT[b - 1])
    for layer, gate in ((0, GT1), (1, GT2)):
        for q in range(QUARTERS):
            for j in range(FFN_BLOCKS):
                load(("ffn", layer, q, j), True)
                if q == 0 and j == 0:
                    load_ada(1, gate)
        if layer == 0:
            for n, name in enumerate(IN_C):
                load(name, True)
                if n - 1 in MOD_IN_C:
                    load_ada(1, MOD_IN_C[n - 1])
            load(("out_c", 0), True)
            load_ada(1, SC2)
            for b in range(1, OUT_BLOCKS):
                load(("out_c", b), True)
    last = {("in_ab", b): tile[(kind, m + 1)] for b, (kind, m) in enumerate(IN_AB)}
    for b in range(OUT_BLOCKS):
        last[("in_v", b)] = tile[("v_sample", b)]
        for name, t in (("out_ab", "out_ab"), ("out_c", "out_c"), ("in_u", "u")):
            last[(name, b)] = tile[(t, 2 * b + 1)]
    last_tile = {n: last[name] if name in last else tile[(*name[:3], 2 * name[3] + 1)] for name, n in block.items()}
    return tile, item, block, last_tile, order


def hybrid_decoder_step(nc, I, O):
    tile_of, item_of, block_of, last_tile_of, order = plan()
    ctx = ExitStack()
    with ctx:
        def sb(name, shape, dt=F32, where=ctx):
            return where.enter_context(nc.sbuf_tensor(name, shape, dt))

        def sem(name):
            return ctx.enter_context(nc.semaphore(name))

        x = sb("x", [P, KT, 2, HALF])
        act_hi = sb("act_hi", [P, KT, 2, HALF], F32R)
        act_lo = sb("act_lo", [P, KT, 2, HALF], F32R)
        in_s_hi = sb("in_s_hi", [P, KT, NS], F32R)
        in_s_lo = sb("in_s_lo", [P, KT, NS], F32R)
        w_hi = sb("w_hi", [P, 2, KT, BN], F32R)
        w_lo = sb("w_lo", [P, 2, KT, BN], F32R)
        raw = sb("raw", [P, RAW, KT * BN])
        work = sb("work", [P, 2, 2, HALF])
        piece = sb("piece", [P, 2, 2, HALF])
        sq = sb("sq", [P, 2, 2, HALF])
        ss = sb("ss", [P, 2, HALF])
        rstd = sb("rstd", [P, 2, HALF])
        gated_s = sb("gated_s", [P, 2, HS * 2])
        scaled_s = sb("scaled_s", [P, 2, NS])
        ident = sb("ident", [P, P])
        ones_d = sb("ones_d", [P, P])
        ones_a = sb("ones_a", [P, P])
        eps = sb("eps", [P, 1])
        NVEC = 4 * KT + KT + 4 * AT
        NB_ADA = 2 * NMOD * KT
        NTAP = TAPS * AT
        vec = sb("vec", [P, NVEC + NB_ADA + NTAP])
        cT = sb("cT", [P, KT, 32])
        mod_t = sb("mod_t", [P, KT, 32])
        mod = sb("mod", [P, 2, NMOD, KT, NCOND])
        scale = sb("scale", [P, KT, NCOND])
        inv_count = sb("inv_count", [P, AT, 16])
        w_pool_sb = sb("w_pool_sb", [P, AT, P])
        replicate = sb("replicate", [P, BATCH_S, SEQ_S])
        same_seq = sb("same_seq", [NS, BATCH_S])
        lnst = sb("lnst", [P, CHUNKS + 1, 4])

        g_mix_v = vec[:, 0:2 * KT].rearrange("p (l k) -> p l k", l=2)
        g_ffn_v = vec[:, 2 * KT:4 * KT].rearrange("p (l k) -> p l k", l=2)
        g_final_v = vec[:, 4 * KT:5 * KT]
        b_dw_v, g_cln_v, b_cln_v, s_pool_v = [vec[:, 5 * KT + i * AT:5 * KT + (i + 1) * AT] for i in range(4)]
        b_ada_v = vec[:, NVEC:NVEC + NB_ADA].rearrange("p (l i k) -> p l i k", l=2, i=NMOD)
        w_dw_v = vec[:, NVEC + NB_ADA:].rearrange("p (t j) -> p t j", j=AT)

        with ExitStack() as zone:
            a_ext = sb("a_ext", [P, AT, HIST + SEQ], where=zone)
            a_ext_s = sb("a_ext_s", [P, AT, BATCH_S, HIST + SEQ_S], where=zone)
            p_ext = sb("p_ext", [P, AT, PHIST + SEQ], where=zone)
            p_ext_s = sb("p_ext_s", [P, AT, BATCH_S, PHIST + SEQ_S], where=zone)
            with ExitStack() as early:
                x_rows = sb("x_rows", [P, CHUNKS, D], where=early)
                xs_rows = sb("xs_rows", [HS, 2, D], where=early)
                c_rows = sb("c_rows", [32, D], where=early)
                vec_rows = sb("vec_rows", [P, 3, P], where=early)
                conv_rows = sb("conv_rows", [4 * HIST, 2, DA], where=early)
                pool_rows = sb("pool_rows", [BATCH_S * PHIST, DA], where=early)
            with ExitStack() as late:
                acc = sb("acc", [P, AT, 2, HALF], where=late)
                diag = sb("diag", [P, DIAGS, P], where=late)
                acc_odd = sb("acc_odd", [P, 2, SEQ], where=late)
                win = sb("win", [P, AT, 2, HALF], where=late)
                sum_p = sb("sum_p", [P, 2, PHIST + SEQ], where=late)
                sum_s = sb("sum_s", [P, 2, BATCH_S, PHIST + SEQ_S], where=late)
                new_s = sb("new_s", [P, 2, AT, NS], where=late)
                conv_part = sb("conv_part", [P, 2, HP], where=late)
                prod = sb("prod", [P, SEQ_S, BATCH_S, TAPS], where=late)
        with ExitStack() as zone:
            f_hi = sb("f_hi", [P, KT, 2, HALF], F32R, where=zone)
            f_lo = sb("f_lo", [P, KT, 2, HALF], F32R, where=zone)
        with ExitStack() as zone:
            u = sb("u", [P, KT, 2, HALF], where=zone)
            v = sb("v", [P, CHUNKS, D], where=zone)
            v_s = sb("v_s", [NS, D], where=zone)
            ws_t = sb("ws_t", [P, HEADS, CHUNK], where=zone)
            b_s = sb("b_s", [P, HEADS, CHUNK], where=zone)
            g_v = sb("g_v", [P, D], where=zone)
            b_v = sb("b_v", [P, D], where=zone)
            ws_seq = sb("ws_seq", [NS, HEADS, BATCH_S, SEQ_S], where=zone)
        ws_rows = v[:, 0, :].rearrange("p (h s) -> p h s", h=HEADS)
        with ExitStack() as zone:
            y_t = sb("y_t", [P, KT, 2, HALF], where=zone)
            y_rows = sb("y_rows", [P, CHUNKS, D], where=zone)
            ys_rows = sb("ys_rows", [HS, 2, D], where=zone)
        head = gated_s[:, 1, 0:16]
        channel_squares = win[:, :, :, :]
        conv_state_rows = diag[0:NS].rearrange("p d c -> p (d c)")[:, 0:2 * DA].rearrange("p (i c) -> p i c", i=2)
        pool_state_rows = sum_p[0:NS].rearrange("p l t -> p (l t)")[:, 0:2 * DA].rearrange("p (i c) -> p i c", i=2)

        psum = ctx.enter_context(nc.psum_tensor("psum", [P, 2 * PAIRS, 512], F32))

        def pair(t):
            return psum[:, 2 * (t % PAIRS):2 * (t % PAIRS) + 2, :]

        def uses(t):
            return t // PAIRS + 1

        def full(eng, t, per=None):
            eng.wait_ge(psum_full[t % PAIRS], uses(t) if per is None else per + uses(t))

        def freed(eng, t, per=None):
            eng.wait_ge(psum_free[t % PAIRS], uses(t) if per is None else per + uses(t))

        def prompt(ap):
            return ap[:, :, 0:HP]

        def sample(ap):
            return ap[:, :, HP:HALF].rearrange("p h (b t) -> p h b t", t=SEQ_S)

        def per_seq(ap9):
            return ap9[:, 1:NCOND].rearrange("p (h b) -> p h b", h=2).unsqueeze(3).broadcast_to([P, 2, HB, SEQ_S])

        def half_slot(buffer, n):
            return buffer[:, n % 4 // 2, n % 2, :]

        def sample_of(ap):
            return ap[:, HP:HALF].rearrange("p (b t) -> p b t", t=SEQ_S)

        def sample_half(ap, h):
            return ap[:, h, HP:HALF].rearrange("p (b t) -> p b t", t=SEQ_S)

        def per_seq_half(ap9, h):
            return ap9[:, 1 + h * HB:1 + (h + 1) * HB].unsqueeze(2).broadcast_to([P, HB, SEQ_S])

        def flat(ap):
            return ap.rearrange("p h t -> p (h t)")

        psum_full = [sem(f"psum_full{i}") for i in range(PAIRS)]
        psum_free = [sem(f"psum_free{i}") for i in range(PAIRS)]
        raw_full = [sem(f"raw_full{i}") for i in range(RAW)]
        w_hi_ready, w_lo_ready, ada_used = sem("w_hi_ready"), sem("w_lo_ready"), sem("ada_used")
        vec_loaded, c_loaded, x_loaded, hist_loaded, pool_w_loaded = (
            sem("vec_loaded"), sem("c_loaded"), sem("x_loaded"), sem("hist_loaded"), sem("pool_w_loaded"))
        odd_loaded = sem("odd_loaded")
        pool_step, act_step, dve_step = sem("pool_step"), sem("act_step"), sem("dve_step")
        consts_ready, c_zeroed, pads_ready = sem("consts_ready"), sem("c_zeroed"), sem("pads_ready")
        c_sigmoid, c_silu = sem("c_sigmoid"), sem("c_silu")
        half_full, stat_half = sem("half_full"), sem("stat_half")
        sq_ready, ss_added, root_ready = sem("sq_ready"), sem("ss_added"), sem("root_ready")
        piece_ready, piece_hi, piece_lo = sem("piece_ready"), sem("piece_hi"), sem("piece_lo")
        x_prompt_done, x_sample_done = sem("x_prompt_done"), sem("x_sample_done")
        a_ready, conv_step = sem("a_ready"), sem("conv_step")
        p_ready, win_ready, pool_in_ready = sem("p_ready"), sem("win_ready"), sem("pool_in_ready")
        conv_s_ready, channel_sq = sem("conv_s_ready"), sem("channel_sq")
        centred, norm_ready, silu_ready, affine_ready = sem("centred"), sem("norm_ready"), sem("silu_ready"), sem("affine_ready")
        diag_ready, diag_used, xr_ready, scale_ready = sem("diag_ready"), sem("diag_used"), sem("xr_ready"), sem("scale_ready")
        new_s_ready, in_s_ready = sem("new_s_ready"), sem("in_s_ready")
        out_stored, rows_stored, y_ready, ws_masked = sem("out_stored"), sem("rows_stored"), sem("y_ready"), sem("ws_masked")
        v_centred, v_sq, v_var, v_root, v_ready = (
            sem("v_centred"), sem("v_sq"), sem("v_var"), sem("v_root"), sem("v_ready"))

        NORM_UNITS = 2 * KT
        U_MIX_IN = 0
        U_MIX_OUT = NORM_UNITS
        U_FFN_IN0 = U_MIX_OUT + KT
        U_FFN0 = U_FFN_IN0 + NORM_UNITS
        U_ODD_IN = U_FFN0 + QUARTERS * KT
        U_ODD_OUT = U_ODD_IN + NORM_UNITS
        U_FFN_IN1 = U_ODD_OUT + KT
        U_FFN1 = U_FFN_IN1 + NORM_UNITS
        LAST = KT - 2
        HALF_ADDS = [(LAST, 0), (LAST + 1, 0), (LAST, 1), (LAST + 1, 1)]
        ADDS = LAST + len(HALF_ADDS)
        G_EVEN = 0
        G_FFN0 = ADDS
        G_ODD = G_FFN0 + (QUARTERS - 1) * KT + ADDS
        G_FFN1 = G_ODD + ADDS

        def sums_of_norm(nth):
            return KT + nth * LAST

        def squares_before(nth):
            return KT + (nth - 1) * ADDS

        STATE_STORES = 16 * (4 + 2)

        block = ctx.enter_context(nc.Block())

        @block.sync
        def _(sp):
            def buffer_free(i):
                if i >= RAW:
                    kind, n = order[i - RAW]
                    if kind == "tile":
                        sp.wait_ge(psum_full[n % PAIRS], uses(n))
                    else:
                        sp.wait_ge(w_lo_ready if kind == "block" else ada_used, n)

            def load(name, src, shape):
                i = item_of[name]
                buffer_free(i)
                dst = raw[:, i % RAW, :].rearrange(shape[0], **shape[1])
                sp.dma_start(dst, src).then_inc(raw_full[i % RAW], 16)

            def load_block(name, w, rows, cols):
                load(name, w[rows:rows + D, cols:cols + BN].rearrange("(k p) n -> p k n", p=P),
                     ("p (k n) -> p k n", {"k": KT}))

            def load_ada(layer, i):
                for c in range(CPM):
                    load(("ada", layer, i, c),
                         I["w_ada"][layer, 2 * P * c:2 * P * (c + 1), i * D:(i + 1) * D].rearrange("(k p) n -> p k n", p=P),
                         ("p (k n) -> p k n", {"k": 2}))

            def load_ffn(layer, modulation):
                w1, w2 = I["w_ffn1"][layer], I["w_ffn2"][layer]
                first = item_of[("ffn", layer, 0, 1)] - 1
                blocks = block_of[("ffn", layer, 0, 0)]
                load_block(("ffn", layer, 0, 0), w1, 0, 0)
                load_ada(1, modulation)
                for j in range(1, OUT_BLOCKS):
                    load_block(("ffn", layer, 0, j), w1, 0, j * BN)
                full(sp, tile_of[("ada", 1, modulation)])
                with sp.Fori(0, QUARTERS - 1) as q:
                    for j in range(FFN_BLOCKS):
                        i = first + OUT_BLOCKS + j
                        sp.wait_ge(w_lo_ready, q * FFN_BLOCKS + (blocks + j + 1))
                        if j < OUT_BLOCKS:
                            src = w2[bass.ds(q * D, D), j * BN:(j + 1) * BN]
                        else:
                            src = w1[:, bass.ds(q * D + (D + (j - OUT_BLOCKS) * BN), BN)]
                        sp.dma_start(raw[:, i % RAW, :].rearrange("p (k n) -> p k n", k=KT),
                                     src.rearrange("(k p) n -> p k n", p=P)).then_inc(raw_full[i % RAW], 16)
                for j in range(OUT_BLOCKS):
                    load_block(("ffn", layer, QUARTERS - 1, OUT_BLOCKS + j), w2, (QUARTERS - 1) * D, j * BN)

            sp.wait_ge(c_zeroed, 1)
            sp.dma_start(c_rows[0:1, :], I["c_prompt"]).then_inc(c_loaded, 16)
            sp.dma_start(c_rows[1:NCOND, :], I["c_sample"]).then_inc(c_loaded, 16)
            sp.dma_start(x_rows[:, :, :], I["x_prompt"][0].rearrange("(c p) d -> p c d", p=P)).then_inc(x_loaded, 16)
            sp.dma_start(xs_rows[:, :, :], I["x_sample"].rearrange("(h b) t d -> (b t) h d", h=2)).then_inc(x_loaded, 16)
            w_in = I["w_in_ab"][0]

            def load_in(b):
                kind, m = IN_AB[b]
                load_block(("in_ab", b), w_in, 0, {"value": 0, "gate": DA, "pool": 2 * DA}[kind] + m * P)

            sp.wait_ge(vec_loaded, 16 * 9)
            load_ada(0, SH1)
            load_in(0)
            load_ada(0, SC1)
            load_in(1)
            for b in range(2, MIX_BLOCKS_IN):
                load_in(b)
                if b - 1 in MOD_AFTER:
                    load_ada(0, MOD_AFTER[b - 1])
            keep = HIST - SEQ_S
            sp.dma_start(O["new_conv_sample"][0, :, 0:keep, :], I["state_conv"][0, :, SEQ_S:HIST, :]).then_inc(out_stored, 16)
            keep_p = PHIST - SEQ_S
            sp.dma_start(O["new_pool_sample"][0, :, 0:keep_p, :], I["state_pool"][0, :, SEQ_S:PHIST, :]).then_inc(out_stored, 16)
            for b in range(2):
                load_block(("out_ab", b), I["w_out_ab"][0], 0, b * BN)
            load_ada(0, GT2)
            for b in range(2, OUT_BLOCKS):
                load_block(("out_ab", b), I["w_out_ab"][0], 0, b * BN)
                load_ada(1, MOD_IN_OUT[b - 1])
            freed(sp, tile_of["conv_state"])
            freed(sp, tile_of["pool_state"])
            sp.dma_start(O["new_conv_prompt"][0, 0], conv_state_rows[NS - HIST:NS, 0, :]).then_inc(out_stored, 16)
            sp.dma_start(O["new_conv_sample"][0, :, keep:HIST, :], conv_state_rows[:, 1, :]).then_inc(out_stored, 16)
            sp.dma_start(O["new_pool_prompt"][0, 0], pool_state_rows[NS - PHIST:NS, 0, :]).then_inc(out_stored, 16)
            sp.dma_start(O["new_pool_sample"][0, :, keep_p:PHIST, :], pool_state_rows[:, 1, :]).then_inc(out_stored, 16)
            load_ffn(0, GT1)
            for b in range(2):
                load_block(("in_v", b), I["w_in_c"][0], 0, D + b * BN)
            sp.wait_ge(x_sample_done, G_ODD)
            sp.dma_start(ws_rows, I["w_spatial"][0].rearrange("h t s -> t h s")).then_inc(odd_loaded, 16)
            sp.dma_start(b_s[:, :, :], I["b_spatial"][0].partition_broadcast(P)).then_inc(odd_loaded, 16)
            sp.dma_start(g_v[:, :], I["g_v_ln"][0].partition_broadcast(P)).then_inc(odd_loaded, 16)
            sp.dma_start(b_v[:, :], I["b_v_ln"][0].partition_broadcast(P)).then_inc(odd_loaded, 16)
            for n, (name, b) in enumerate(IN_C):
                if n >= 2:
                    load_block((name, b), I["w_in_c"][0], 0, (D if name == "in_v" else 0) + b * BN)
                if n - 1 in MOD_IN_C:
                    load_ada(1, MOD_IN_C[n - 1])
            load_block(("out_c", 0), I["w_out_c"][0], 0, 0)
            load_ada(1, SC2)
            for b in range(1, OUT_BLOCKS):
                load_block(("out_c", b), I["w_out_c"][0], 0, b * BN)
            sp.wait_ge(v_ready, CHUNKS + 1)
            sp.dma_start(O["new_v_sample"][0].rearrange("b t d -> (b t) d"), v_s[:, :]).then_inc(out_stored, 16)
            load_ffn(1, GT2)
            for c in range(CHUNKS):
                freed(sp, tile_of[("y", c)])
                sp.dma_start(O["y_prompt"][0, c * CHUNK:(c + 1) * CHUNK, :], y_rows[:, c, :]).then_inc(rows_stored, 16)
            for h in range(2):
                freed(sp, tile_of[("y_sample", h)])
            sp.dma_start(O["y_sample"].rearrange("(h b) t d -> (b t) h d", h=2), ys_rows[:, :, :]).then_inc(rows_stored, 16)
            sp.wait_ge(out_stored, STATE_STORES + 16)
            sp.wait_ge(rows_stored, 16 * (CHUNKS + 1))

        @block.gpsimd
        def _(pool):
            own = Own(pool, pool_step)
            g = nc.gpsimd
            g.memset(c_rows[:, :], 0.0).then_inc(c_zeroed, 1)
            zero = own.step(g.memset(ident[:, :], 0.0))
            own.after(zero)
            g.affine_select(out=ident[:, :], in_=ident[:, :], compare_op=ALU.not_equal, fill=1.0, base=0,
                            pattern=[[-1, P]], channel_multiplier=1).then_inc(consts_ready, 1)
            g.memset(ones_d[:, :], 1.0 / D).then_inc(consts_ready, 1)
            g.memset(ones_a[:, :], 1.0 / DA).then_inc(consts_ready, 1)
            g.memset(eps[:, :], EPS).then_inc(consts_ready, 1)
            g.memset(a_ext[:, :, 0:HIST], 0.0).then_inc(pads_ready, 1)
            g.memset(p_ext[:, :, 0:PHIST], 0.0).then_inc(pads_ready, 1)
            for i, w in enumerate(WINDOWS):
                full = own.step(g.memset(inv_count[:, i, :], 1.0 / w))
                own.after(full)
                for t in range(w - 1):
                    last = own.step(g.memset(inv_count[:, i, t:t + 1], 1.0 / (t + 1)))
            own.after(last)
            m = own.step(g.memset(replicate[:, :, :], 0.0))
            own.after(m)
            m = own.step(g.affine_select(out=replicate[:, :, :], in_=replicate[:, :, :], compare_op=ALU.not_equal, fill=1.0,
                                         base=0, pattern=[[0, BATCH_S], [-1, SEQ_S]], channel_multiplier=1))
            m = own.step(g.memset(same_seq[:, :], 1.0))
            own.after(m)
            m = own.step(g.affine_select(out=same_seq[:, :], in_=same_seq[:, :], compare_op=ALU.is_ge, fill=0.0,
                                         base=0, pattern=[[-SEQ_S, BATCH_S]], channel_multiplier=1))
            own.after(m)
            g.affine_select(out=same_seq[:, :], in_=same_seq[:, :], compare_op=ALU.is_ge, fill=0.0,
                            base=SEQ_S - 1, pattern=[[SEQ_S, BATCH_S]], channel_multiplier=-1).then_inc(consts_ready, 1)
            def norm_pieces_samples(layer, sh, unit, nth):
                pool.wait_ge(scale_ready, nth + 1)
                for i in range(NORM_UNITS):
                    h, k = divmod(i, KT)
                    n = unit + i
                    pool.wait_ge(xr_ready, nth * NORM_UNITS + i + 1)
                    tmp = scaled_s[:, i % 2, 0:HS].rearrange("p (b t) -> p b t", t=SEQ_S)
                    done = own.step(g.tensor_tensor(tmp, sample_of(half_slot(work, i)), per_seq_half(scale[:, k, :], h),
                                                    ALU.mult))
                    own.after(done)
                    if n >= 4:
                        pool.wait_ge(piece_lo, max(n - 3, unit))
                    g.tensor_tensor(sample_of(half_slot(piece, n)), tmp, per_seq_half(mod[:, layer, sh, k, :], h), ALU.add)\
                     .then_inc(piece_ready, 1)

            def convolve_samples(j):
                freed(pool, tile_of[("conv_hist", j)])
                freed(pool, tile_of[("value", j)])
                own.after(own.n)
                for t in range(SEQ_S):
                    own.step(g.tensor_tensor(prod[:, t], a_ext_s[:, j, :, t:t + TAPS],
                                             w_dw_v[:, :, j].unsqueeze(1).broadcast_to([P, BATCH_S, TAPS]), ALU.mult))
                have, half = TAPS, 16
                while half:
                    own.after(own.n)
                    own.step(g.tensor_tensor(prod[:, :, :, 0:have - half], prod[:, :, :, 0:have - half],
                                             prod[:, :, :, half:have], ALU.add))
                    have, half = half, half // 2
                own.after(own.n)
                g.tensor_scalar(sample(acc[:, j]), prod[:, :, :, 0].rearrange("p t (h b) -> p h b t", h=2),
                                b_dw_v[:, j:j + 1], None, ALU.add).then_inc(conv_s_ready, 1)
                pool.wait_ge(conv_s_ready, j + 1)

            def pool_input(i):
                w = WINDOWS[i]
                own.step(g.tensor_tensor(head, win[:, i, 0, 0:16], inv_count[:, i, :], ALU.mult))
                own.after(own.n)
                own.step(g.tensor_scalar(flat(win[:, i]), flat(win[:, i]), 1.0 / w, None, ALU.mult))
                own.after(own.n)
                own.step(g.tensor_tensor(prompt(win[:, i]), prompt(win[:, i]),
                                         p_ext[:, i, PHIST:PHIST + SEQ].rearrange("p (h t) -> p h t", h=2), ALU.subtract))
                own.step(g.tensor_tensor(
                    sample(win[:, i]), sample(win[:, i]),
                    p_ext_s[:, i, :, PHIST:PHIST + SEQ_S].rearrange("p (h b) t -> p h b t", h=2), ALU.subtract))
                own.after(own.n)
                g.tensor_tensor(win[:, i, 0, 0:16], head, p_ext[:, i, PHIST:PHIST + 16], ALU.subtract)\
                 .then_inc(pool_in_ready, 1)
                pool.wait_ge(pool_in_ready, i + 1)

            norm_pieces_samples(0, SH1, U_MIX_IN, 0)
            for j in range(AT):
                convolve_samples(j)
            pool.wait_ge(pads_ready, 2)
            freed(pool, tile_of["pool_hist"])
            for i in range(AT):
                pool.wait_ge(p_ready, i + 1)
                freed(pool, tile_of[("pool", i)])
                src_p, src_s = p_ext[:, i, :], p_ext_s[:, i, :, :]
                shift = 1
                for level in range(i + 1):
                    lo = 2 * shift - 1
                    dst_p, dst_s = sum_p[:, level % 2, :], sum_s[:, level % 2, :, :]
                    if level == i:
                        own.step(g.tensor_tensor(
                            prompt(win[:, i]), src_p[:, PHIST:PHIST + SEQ].rearrange("p (h t) -> p h t", h=2),
                            src_p[:, PHIST - shift:PHIST + SEQ - shift].rearrange("p (h t) -> p h t", h=2), ALU.add))
                        own.after(own.n)
                        g.tensor_tensor(
                            sample(win[:, i]),
                            src_s[:, :, PHIST:PHIST + SEQ_S].rearrange("p (h b) t -> p h b t", h=2),
                            src_s[:, :, PHIST - shift:PHIST + SEQ_S - shift].rearrange("p (h b) t -> p h b t", h=2),
                            ALU.add).then_inc(win_ready, 1)
                        pool.wait_ge(win_ready, i + 1)
                    else:
                        own.step(g.tensor_tensor(dst_p[:, lo:], src_p[:, lo:], src_p[:, lo - shift:PHIST + SEQ - shift],
                                                 ALU.add))
                        own.step(g.tensor_tensor(dst_s[:, :, lo:], src_s[:, :, lo:],
                                                 src_s[:, :, lo - shift:PHIST + SEQ_S - shift], ALU.add))
                        own.after(own.n)
                    src_p, src_s = dst_p, dst_s
                    shift *= 2
                pool_input(i)
            norm_pieces_samples(0, SH2, U_FFN_IN0, 1)
            norm_pieces_samples(1, SH1, U_ODD_IN, 2)
            freed(pool, tile_of["ws"])
            g.affine_select(out=ws_t[:, :, :], in_=ws_t[:, :, :], compare_op=ALU.is_ge, fill=0.0, base=0,
                            pattern=[[0, HEADS], [1, CHUNK]], channel_multiplier=-1).then_inc(ws_masked, 1)
            norm_pieces_samples(1, SH2, U_FFN_IN1, 3)

        @block.tensor
        def _(pe):
            def take(t):
                if t >= PAIRS:
                    pe.wait_ge(psum_free[t % PAIRS], t // PAIRS)
                return pair(t)

            def give(t, mm):
                mm.then_inc(psum_full[t % PAIRS], 1)

            def product(out, left, right, start, stop):
                for n, (a, b) in enumerate(((0, 0), (0, 1), (1, 0))):
                    mm = nc.tensor.matmul(out, left[a], right[b], start=start and n == 0, stop=stop and n == 2,
                                          skip_group_check=True)
                return mm

            def block_product(b, t, hi, lo, units, k_order=range(KT), first=True, last=True, half=None, norm=None,
                              per_b=None, per_t=None, per_u=None):
                slot = b % 2

                def at(n, per):
                    return n if per is None else per + n

                pe.wait_ge(w_lo_ready, at(b + 1, per_b))
                for m in range(2):
                    if first and half != 1 and t + m >= PAIRS:
                        pe.wait_ge(psum_free[(t + m) % PAIRS], at((t + m) // PAIRS, per_t))
                for n, k in enumerate(k_order):
                    if norm and half == 1 and n == KT // 2:
                        stat_of_half(norm, 0)
                    if units is not None:
                        pe.wait_ge(piece_lo, at(units + (KT if half else 0) + n + 1, per_u))
                    for m in range(2):
                        out = pair(t + m)
                        cols = slice(m * P, (m + 1) * P)
                        for i, (a, c) in enumerate(((w_hi, hi), (w_hi, lo), (w_lo, hi))):
                            for h in (0, 1) if half is None else (half,):
                                mm = nc.tensor.matmul(out[:, h, 0:HALF], a[:, slot, k, cols], c[:, k, h, :],
                                                      start=(first and n == 0 and i == 0),
                                                      stop=(last and n == len(k_order) - 1 and i == 2),
                                                      skip_group_check=True)
                        if last and n == len(k_order) - 1:
                            if half != 0:
                                mm.then_inc(psum_full[(t + m) % PAIRS], 1)
                            elif norm:
                                mm.then_inc(half_full, 1)

            def named_block(name, t_name, hi, lo, units, k_order=range(KT), first=True, last=True, half=None, norm=None):
                block_product(block_of[name], tile_of[t_name], hi, lo, units, k_order, first, last, half, norm)

            def block_before_norm(name, t_name, norm):
                for half in range(2):
                    named_block(name, t_name, act_hi, act_lo, None, half=half, norm=norm)

            def stat_of_half(nth, h):
                t = tile_of[("stat", nth)]
                out = take(t)
                pe.wait_ge(ss_added, sums_of_norm(nth))
                nc.tensor.matmul(out[:, h, 0:HALF], ones_d[:, :], ss[:, h, :], start=True, stop=False)
                for i in range(2):
                    n = squares_before(nth) + LAST + 2 * h + i
                    pe.wait_ge(sq_ready, n + 1)
                    mm = nc.tensor.matmul(out[:, h, 0:HALF], ones_d[:, :], sq[:, n % 2, h, :], start=False, stop=(i == 1))
                mm.then_inc(psum_full[t % PAIRS] if h else stat_half, 1)

            def ada(layer, i):
                t = tile_of[("ada", layer, i)]
                out = take(t)
                for c in range(CPM):
                    it = item_of[("ada", layer, i, c)]
                    pe.wait_ge(raw_full[it % RAW], 16 * (it // RAW + 1))
                    chunk = raw[:, it % RAW, :].rearrange("p (k j g f) -> p k g j f", k=2, g=4, f=32)
                    for kk in range(2):
                        k = 2 * c + kk
                        for grp in range(4):
                            mm = nc.tensor.matmul(out[32 * grp:32 * grp + 32, 0, 0:2 * P], cT[:, k, :], chunk[:, kk, grp],
                                                  start=(k == 0), stop=(k == KT - 1), skip_group_check=True)
                    if c < CPM - 1:
                        mm.then_inc(ada_used, 1)
                give(t, mm)

            def stat(t, ones, count):
                out = take(t)
                pe.wait_ge(ss_added, count)
                for h in range(2):
                    mm = nc.tensor.matmul(out[:, h, 0:HALF], ones[:, :], ss[:, h, :], start=True, stop=True)
                give(t, mm)

            def quarter(layer, q, units_in, units, norm=None, per=None):
                b0, t0 = block_of[("ffn", layer, q, 0)], tile_of[("ffn", layer, q, 0)]
                per_b = None if per is None else per * FFN_BLOCKS
                per_t = None if per is None else per * (2 * FFN_BLOCKS // PAIRS)
                for half in range(2):
                    block_product(b0, t0, act_hi, act_lo, units_in, half=half, per_b=per_b, per_t=per_t)
                for j in range(1, OUT_BLOCKS):
                    block_product(b0 + j, t0 + 2 * j, act_hi, act_lo, None, per_b=per_b, per_t=per_t)
                for j in range(OUT_BLOCKS, FFN_BLOCKS):
                    for half in range(2) if norm and j == FFN_BLOCKS - 1 else (None,):
                        block_product(b0 + j, t0 + 2 * j, f_hi, f_lo, None if j > OUT_BLOCKS else units, half=half,
                                      norm=norm if half is not None else None, per_b=per_b, per_t=per_t,
                                      per_u=None if per is None else per * KT)

            def ffn(layer, units_in, units, norm):
                with pe.Fori(0, QUARTERS - 1) as q:
                    quarter(layer, 0, units_in, units, per=q)
                quarter(layer, QUARTERS - 1, units_in, units + (QUARTERS - 1) * KT, norm=norm)

            pe.wait_ge(consts_ready, 5)
            pe.wait_ge(vec_loaded, 16 * 9)
            out = take(tile_of["vec"])
            at = 0
            for i, n in enumerate((NVEC, NB_ADA, NTAP)):
                mm = nc.tensor.transpose(out[:, 0, at:at + n], vec_rows[0:n, i, :], ident[0:n, 0:n])
                at += n
            give(tile_of["vec"], mm)
            pe.wait_ge(c_silu, 1)
            out = take(tile_of["cT"])
            for k in range(KT):
                mm = nc.tensor.transpose(out[:, 0, 32 * k:32 * k + 32], c_rows[:, k * P:(k + 1) * P], ident[0:32, 0:32])
            give(tile_of["cT"], mm)
            pe.wait_ge(x_loaded, 32)
            for k in range(KT):
                out = take(tile_of[("x", k)])
                for c in range(CHUNKS):
                    nc.tensor.transpose(out[:, c // 2, (c % 2) * CHUNK:(c % 2 + 1) * CHUNK], x_rows[:, c, k * P:(k + 1) * P],
                                        ident[:, :])
                for h in range(2):
                    mm = nc.tensor.transpose(out[:, h, HP:HALF], xs_rows[:, h, k * P:(k + 1) * P], ident[0:HS, 0:HS])
                give(tile_of[("x", k)], mm)
            freed(pe, tile_of["cT"])
            ada(0, SH1)
            stat(tile_of[("stat", 0)], ones_d, KT)
            pe.wait_ge(hist_loaded, 48)
            for j in range(AT):
                out = take(tile_of[("conv_hist", j)])
                for h in range(2):
                    mm = nc.tensor.transpose(out[:, h, 0:HB * HIST], conv_rows[:, h, j * P:(j + 1) * P],
                                             ident[0:HB * HIST, 0:HB * HIST])
                give(tile_of[("conv_hist", j)], mm)
            out = take(tile_of["pool_hist"])
            n = BATCH_S * PHIST
            for j in range(AT):
                mm = nc.tensor.transpose(out[:, 0, j * n:(j + 1) * n], pool_rows[:, j * P:(j + 1) * P], ident[0:n, 0:n])
            give(tile_of["pool_hist"], mm)
            ada(0, SC1)
            for half in range(2):
                for b in range(2):
                    named_block(("in_ab", b), IN_AB[b], act_hi, act_lo, None if b else U_MIX_IN, half=half)
            for b, name in enumerate(IN_AB):
                if b >= 2:
                    named_block(("in_ab", b), name, act_hi, act_lo, None)
                if b in MOD_AFTER:
                    ada(0, MOD_AFTER[b])
            conv = take(tile_of["conv_pe"])
            pe.wait_ge(a_ready, 1)
            freed(pe, tile_of[("value", 0)])
            for tap in range(PE_TAPS):
                pe.wait_ge(diag_ready, tap + 1)
                for h in range(2):
                    mm = nc.tensor.matmul(conv[:, h, 0:HP], diag[:, tap % DIAGS, :],
                                          a_ext[:, 0, tap + h * HP:tap + (h + 1) * HP], start=(tap == 0),
                                          stop=(tap == PE_TAPS - 1), skip_group_check=True)
                mm.then_inc(diag_used if tap < PE_TAPS - 1 else psum_full[tile_of["conv_pe"] % PAIRS], 1)
            pe.wait_ge(pool_w_loaded, 16)
            for i in range(AT):
                out = take(tile_of[("pool_mix", i)])
                pe.wait_ge(pool_in_ready, i + 1)
                for h in range(2):
                    mm = nc.tensor.matmul(out[:, h, 0:HALF], w_pool_sb[:, i, :], win[:, i, h, :], start=True, stop=True)
                give(tile_of[("pool_mix", i)], mm)
            out = take(tile_of["conv_state"])
            pe.wait_ge(new_s_ready, 2)
            for j in range(AT):
                nc.tensor.transpose(out[0:NS, 0, j * P:(j + 1) * P], a_ext[:, j, SEQ + HIST - NS:SEQ + HIST], ident[:, :])
                mm = nc.tensor.transpose(out[0:NS, 1, j * P:(j + 1) * P], new_s[:, 0, j, :], ident[:, :])
            give(tile_of["conv_state"], mm)
            out = take(tile_of["pool_state"])
            for j in range(AT):
                nc.tensor.transpose(out[0:NS, 0, j * P:(j + 1) * P], p_ext[:, j, SEQ + PHIST - NS:SEQ + PHIST], ident[:, :])
                mm = nc.tensor.transpose(out[0:NS, 1, j * P:(j + 1) * P], new_s[:, 1, j, :], ident[:, :])
            give(tile_of["pool_state"], mm)
            out = take(tile_of["conv_mean"])
            pe.wait_ge(conv_s_ready, AT)
            for n, j in enumerate((*range(1, AT), 0)):
                pe.wait_ge(conv_step, j * (TAPS + 1) if j else CONV_STEPS)
                for h in range(2):
                    mm = nc.tensor.matmul(out[:, h, 0:HALF], ones_a[:, :], acc[:, j, h, :], start=(n == 0), stop=(n == AT - 1),
                                          skip_group_check=True)
            give(tile_of["conv_mean"], mm)
            ada(0, GT2)
            out = take(tile_of["conv_var"])
            for j in range(AT):
                pe.wait_ge(channel_sq, j + 1)
                for h in range(2):
                    mm = nc.tensor.matmul(out[:, h, 0:HALF], ones_a[:, :], channel_squares[:, j, h, :], start=(j == 0),
                                          stop=(j == AT - 1), skip_group_check=True)
            give(tile_of["conv_var"], mm)
            pooled, convolved = range(AT, KT), range(AT)
            for b in range(2):
                named_block(("out_ab", b), ("out_ab", 2 * b), act_hi, act_lo, None if b else U_MIX_OUT, pooled, last=False)
            for b in range(2):
                named_block(("out_ab", b), ("out_ab", 2 * b), act_hi, act_lo, None if b else U_MIX_OUT + AT, convolved,
                            first=False)
            ada(1, MOD_IN_OUT[1])
            for b in range(2, OUT_BLOCKS):
                if b < OUT_BLOCKS - 1:
                    named_block(("out_ab", b), ("out_ab", 2 * b), act_hi, act_lo, None)
                else:
                    block_before_norm(("out_ab", b), ("out_ab", 2 * b), 1)
                if b in MOD_IN_OUT:
                    ada(1, MOD_IN_OUT[b])
            stat_of_half(1, 1)
            ffn(0, U_FFN_IN0, U_FFN0, 2)

            def v_chunks(b, chunks, split=None, norm=None):
                blk, t = block_of[("in_v", b)], tile_of[("v", b)]
                pe.wait_ge(w_lo_ready, blk + 1)
                out = take(t) if chunks[0] == 0 else pair(t)
                for k, c in ((k, c) for first in chunks[::2] for k in range(KT) for c in (first, first + 1)):
                    if c % 2 == 0:
                        if norm and k == KT // 2:
                            stat_of_half(norm, 1)
                        if split is not None:
                            pe.wait_ge(piece_lo, split + k + 1)
                    rows = slice((c % 2) * CHUNK, (c % 2 + 1) * CHUNK)
                    mm = product(out[:, c % 2, c // 2 * BN:(c // 2 + 1) * BN],
                                 (act_hi[:, k, c // 2, rows], act_lo[:, k, c // 2, rows]),
                                 (w_hi[:, blk % 2, k, :], w_lo[:, blk % 2, k, :]), k == 0, k == KT - 1)
                if chunks[-1] == CHUNKS - 1:
                    give(t, mm)

            def v_samples(b):
                blk, t = block_of[("in_v", b)], tile_of[("v_sample", b)]
                out = take(t)
                pe.wait_ge(in_s_ready, 2)
                for k in range(KT):
                    mm = product(out[0:NS, 0, 0:BN], (in_s_hi[:, k, :], in_s_lo[:, k, :]),
                                 (w_hi[:, blk % 2, k, :], w_lo[:, blk % 2, k, :]), k == 0, k == KT - 1)
                give(t, mm)

            v_chunks(0, range(0, 2), split=U_ODD_IN, norm=2)
            v_chunks(1, range(0, 2))
            pe.wait_ge(odd_loaded, 64)
            out = take(tile_of["ws"])
            for h in range(HEADS):
                mm = nc.tensor.transpose(out[:, h // 4, (h % 4) * P:(h % 4 + 1) * P], ws_rows[:, h, :], ident[:, :])
            give(tile_of["ws"], mm)
            v_chunks(0, range(2, 4), split=U_ODD_IN + KT)
            v_chunks(1, range(2, 4))
            v_samples(0)
            v_samples(1)
            for n, (name, b) in enumerate(IN_C):
                if n < 2:
                    continue
                if name == "in_v":
                    v_chunks(b, range(CHUNKS))
                    v_samples(b)
                else:
                    named_block(("in_u", b), ("u", 2 * b), act_hi, act_lo, None)
                if n in MOD_IN_C:
                    ada(1, MOD_IN_C[n])
                if n == REPLICATE_AT:
                    out = take(tile_of["rep"])
                    pe.wait_ge(ws_masked, 1)
                    mm = nc.tensor.matmul(out[0:NS, 0, 0:HEADS * SEQ_S], replicate[:, :, :], ws_t[:, :, 0:SEQ_S], start=True, stop=True)
                    give(tile_of["rep"], mm)
            pe.wait_ge(v_ready, CHUNKS + 1)
            freed(pe, tile_of["rep"])
            for h in range(HEADS):
                out = take(tile_of[("spatial", h)])
                cols = slice(h * P, (h + 1) * P)
                for c in range(CHUNKS):
                    nc.tensor.matmul(out[:, c // 2, (c % 2) * CHUNK:(c % 2 + 1) * CHUNK], v[:, c, cols], ws_t[:, h, :],
                                     start=True, stop=True, skip_group_check=True)
                for s in range(2):
                    mm = nc.tensor.matmul(out[:, s, HP:HALF], v_s[:, cols], ws_seq[:, h, s * HB:(s + 1) * HB, :],
                                          start=True, stop=True, skip_group_check=True)
                give(tile_of[("spatial", h)], mm)
            for b in range(OUT_BLOCKS):
                if b < OUT_BLOCKS - 1:
                    named_block(("out_c", b), ("out_c", 2 * b), act_hi, act_lo, None if b else U_ODD_OUT)
                else:
                    block_before_norm(("out_c", b), ("out_c", 2 * b), 3)
                if b in MOD_OUT_C:
                    ada(1, MOD_OUT_C[b])
            stat_of_half(3, 1)
            ffn(1, U_FFN_IN1, U_FFN1, 4)
            stat_of_half(4, 1)
            for c in range(CHUNKS):
                pe.wait_ge(y_ready, KT * (1 + c // 2))
                out = take(tile_of[("y", c)])
                for k in range(KT):
                    mm = nc.tensor.transpose(out[:, k // 4, (k % 4) * P:(k % 4 + 1) * P],
                                             y_t[:, k, c // 2, (c % 2) * CHUNK:(c % 2 + 1) * CHUNK], ident[:, :])
                give(tile_of[("y", c)], mm)
            for h in range(2):
                t = tile_of[("y_sample", h)]
                out = take(t)
                for k in range(KT):
                    mm = nc.tensor.transpose(out[0:HS, k // 4, (k % 4) * P:(k % 4 + 1) * P], y_t[:, k, h, HP:HALF],
                                             ident[:, :])
                give(t, mm)

        @block.scalar
        def _(act):
            own = Own(act, act_step)
            squares = [0]

            def weights_hi(b, i, t_used=None, per_b=None, per_i=None, per_t=None):
                def at(n, per):
                    return n if per is None else per + n
                act.wait_ge(raw_full[i % RAW], at(16 * (i // RAW + 1), per_i))
                if per_b is not None:
                    full(act, t_used, per_t)
                elif b >= 2:
                    full(act, last_tile_of[b - 2])
                nc.scalar.activation(w_hi[:, b % 2, :, :].rearrange("p k n -> p (k n)"), raw[:, i % RAW, :],
                                     ACT.Copy).then_inc(w_hi_ready, 1)

            def named_hi(name):
                weights_hi(block_of[name], item_of[name])

            def piece_to_hi(dst, n, per=None):
                act.wait_ge(piece_ready, n + 1 if per is None else per + (n + 1))
                nc.scalar.activation(flat(dst), flat(piece[:, n % 2]), ACT.Copy).then_inc(piece_hi, 1)

            def square(src, waits):
                n = squares[0]
                for s, c in waits:
                    act.wait_ge(s, c)
                if n < KT:
                    if n >= 2:
                        act.wait_ge(ss_added, n - 1)
                else:
                    nth, m = divmod(n - KT, ADDS)
                    act.wait_ge(ss_added, sums_of_norm(nth) + max(m - 1, 0))
                nc.scalar.activation(flat(sq[:, n % 2]), flat(src), ACT.Square).then_inc(sq_ready, 1)
                squares[0] += 1

            def square_x(m, adds):
                square(x[:, m], [(x_prompt_done, adds + 1), (x_sample_done, adds + 1)])

            def square_halves(adds, h):
                for i in range(2 * h, 2 * h + 2):
                    m, n = HALF_ADDS[i][0], squares[0]
                    act.wait_ge(x_prompt_done, adds + LAST + i + 1)
                    act.wait_ge(x_sample_done, adds + LAST + i + 1)
                    act.wait_ge(ss_added, sums_of_norm((n - KT) // ADDS + 1))
                    nc.scalar.activation(sq[:, n % 2, h], x[:, m, h], ACT.Square).then_inc(sq_ready, 1)
                    squares[0] += 1

            def norm_pieces_hi(layer, sh, unit, nth, second, adds=None):
                act.wait_ge(scale_ready, nth + 1)
                for i in range(NORM_UNITS + 1):
                    h, k = divmod(i, KT)
                    n = unit + i
                    if adds is not None and i == SQUARES_AT:
                        square_halves(adds, 1)
                    if adds is not None and i == ROOT_AT:
                        root_of_half(nth, 1)
                    if i == SECOND_HI_AT:
                        named_hi(second)
                    if i < NORM_UNITS:
                        act.wait_ge(xr_ready, nth * NORM_UNITS + i + 1)
                        if n >= 4:
                            act.wait_ge(piece_lo, max(n - 3, unit))
                        own.step(nc.scalar.activation(half_slot(piece, n)[:, 0:HP], half_slot(work, i)[:, 0:HP], ACT.Identity,
                                                      bias=mod[:, layer, sh, k, 0:1], scale=scale[:, k, 0:1]))
                    if i:
                        own.after(own.n - 1 if i < NORM_UNITS else own.n)
                        act.wait_ge(piece_ready, n)
                        h, k = divmod(i - 1, KT)
                        nc.scalar.activation(act_hi[:, k, h], half_slot(piece, n - 1), ACT.Copy).then_inc(piece_hi, 1)

            def root(t):
                full(act, t)
                nc.scalar.activation(rstd[:, :, :], pair(t)[:, :, 0:HALF], ACT.Sqrt, bias=eps[:, 0:1]).then_inc(root_ready, 1)

            def root_of_half(nth, h):
                t = tile_of[("stat", nth)]
                if h:
                    full(act, t)
                else:
                    act.wait_ge(stat_half, nth)
                nc.scalar.activation(rstd[:, h], pair(t)[:, h, 0:HALF], ACT.Sqrt, bias=eps[:, 0:1]).then_inc(root_ready, 1)

            def relu(t, n, per_t=None, per_u=None):
                full(act, t, per_t)
                act.wait_ge(piece_ready, n - 1 if per_u is None else per_u + (n - 1))
                nc.scalar.activation(work[:, n % 2], pair(t)[:, :, 0:HALF], ACT.Relu).then_inc(psum_free[t % PAIRS], 1)

            def quarter(layer, q, units, adds=None, per=None, last=False, following=None):
                b0, i0, t0 = (block_of[("ffn", layer, q, 0)], item_of[("ffn", layer, q, 1)] - 1, tile_of[("ffn", layer, q, 0)])
                per_b = None if per is None else per * FFN_BLOCKS
                per_i = None if per is None else per * (16 * FFN_BLOCKS // RAW)
                per_t = None if per is None else per * (2 * FFN_BLOCKS // PAIRS)
                per_u = None if per is None else per * KT
                for j in range(FFN_BLOCKS):
                    if j < FFN_BLOCKS - 2 or not last:
                        weights_hi(b0 + j + 2, i0 + j + 2, t0 + 2 * j + 1, per_b, per_i, per_t)
                    elif following and j == FFN_BLOCKS - 2:
                        named_hi(following)
                    if last and OUT_BLOCKS <= j < FFN_BLOCKS - 1:
                        for m in range(2 * j - KT, 2 * j + 2 - KT):
                            square_x(m, adds + m)
                    if j < OUT_BLOCKS:
                        for m in range(2 * j, 2 * j + 2):
                            relu(t0 + m, units + m, per_t, per_u)
                            if m:
                                piece_to_hi(f_hi[:, m - 1], units + m - 1, per_u)
                    if j == OUT_BLOCKS - 1:
                        piece_to_hi(f_hi[:, KT - 1], units + KT - 1, per_u)

            def ffn(layer, units, adds, following=None):
                with act.Fori(0, QUARTERS - 1) as q:
                    quarter(layer, 0, units, per=q)
                done = (QUARTERS - 1) * KT
                quarter(layer, QUARTERS - 1, units + done, adds + done, last=True, following=following)
                square_halves(adds + done, 0)

            def diagonals(lo, hi):
                for tap in range(lo, hi):
                    if tap >= DIAGS:
                        act.wait_ge(diag_used, tap - DIAGS + 1)
                    nc.scalar.activation(diag[:, tap % DIAGS, :], ident[:, :], ACT.Copy, scale=w_dw_v[:, tap, 0:1])\
                      .then_inc(diag_ready, 1)

            act.dma_start(vec_rows[0:16, 0, :], I["g_mix"].rearrange("l (k p) -> (l k) p", p=P)).then_inc(vec_loaded, 16)
            act.dma_start(vec_rows[16:32, 0, :], I["g_ffn"].rearrange("l (k p) -> (l k) p", p=P)).then_inc(vec_loaded, 16)
            act.dma_start(vec_rows[32:40, 0, :], I["g_final"].rearrange("(k p) -> k p", p=P)).then_inc(vec_loaded, 16)
            for i, name in enumerate(("b_dw", "g_conv_ln", "b_conv_ln", "s_pool")):
                act.dma_start(vec_rows[40 + 4 * i:44 + 4 * i, 0, :],
                              I[name][0].rearrange("(k p) -> k p", p=P)).then_inc(vec_loaded, 16)
            act.dma_start(vec_rows[0:NB_ADA, 1, :], I["b_ada"].rearrange("l (k p) -> (l k) p", p=P)).then_inc(vec_loaded, 16)
            act.dma_start(vec_rows[0:NTAP, 2, :], I["w_dw"][0].rearrange("t (j p) -> (t j) p", p=P)).then_inc(vec_loaded, 16)
            act.dma_start(w_pool_sb[:, :, :], I["w_pool"][0].rearrange("g i o -> i g o")).then_inc(pool_w_loaded, 16)
            for h in range(2):
                act.dma_start(conv_rows[:, h, :], I["state_conv"][0, h * HB:(h + 1) * HB].rearrange("b r c -> (b r) c"))\
                   .then_inc(hist_loaded, 16)
            act.dma_start(pool_rows[:, :], I["state_pool"][0].rearrange("b r c -> (b r) c")).then_inc(hist_loaded, 16)

            act.wait_ge(c_loaded, 32)
            c_sig = sq[0:32].rearrange("p i h t -> p (i h t)")[:, 0:D]
            nc.scalar.activation(c_sig, c_rows[:, :], ACT.Sigmoid).then_inc(c_sigmoid, 1)
            full(act, tile_of["vec"])
            nc.scalar.activation(vec[:, :], pair(tile_of["vec"])[:, 0, 0:NVEC + NB_ADA + NTAP], ACT.Copy)\
              .then_inc(psum_free[tile_of["vec"] % PAIRS], 1)
            full(act, tile_of["cT"])
            nc.scalar.activation(cT.rearrange("p k c -> p (k c)"), pair(tile_of["cT"])[:, 0, 0:32 * KT], ACT.Copy)\
              .then_inc(psum_free[tile_of["cT"] % PAIRS], 1)
            for k in range(KT + 1):
                if k < KT:
                    t = tile_of[("x", k)]
                    full(act, t)
                    nc.scalar.activation(x[:, k], pair(t)[:, :, 0:HALF], ACT.Copy).then_inc(psum_free[t % PAIRS], 1)
                if k:
                    t = tile_of[("x", k - 1)]
                    square(x[:, k - 1], [(psum_free[t % PAIRS], uses(t))])
            act.wait_ge(consts_ready, 5)
            named_hi(("in_ab", 0))
            root(tile_of[("stat", 0)])
            for j in range(AT):
                t = tile_of[("conv_hist", j)]
                full(act, t)
                nc.scalar.activation(a_ext_s[:, j, :, 0:HIST].rearrange("p (h b) r -> p h b r", h=2),
                                     pair(t)[:, :, 0:HB * HIST].rearrange("p h (b r) -> p h b r", r=HIST),
                                     ACT.Copy).then_inc(psum_free[t % PAIRS], 1)
            t = tile_of["pool_hist"]
            full(act, t)
            nc.scalar.activation(p_ext_s[:, :, :, 0:PHIST],
                                 pair(t)[:, 0, 0:AT * BATCH_S * PHIST].rearrange("p (j b r) -> p j b r", j=AT, r=PHIST),
                                 ACT.Copy).then_inc(psum_free[t % PAIRS], 1)
            norm_pieces_hi(0, SH1, U_MIX_IN, 0, ("in_ab", 1))
            for b in range(MIX_BLOCKS_IN):
                if b:
                    named_hi(("in_ab", b + 1) if b + 1 < MIX_BLOCKS_IN else ("out_ab", 0))
                kind, first = IN_AB[b]
                for m in range(first, first + 2):
                    t = tile_of[(kind, m)]
                    if kind == "gate":
                        full(act, t)
                        if m >= 2:
                            act.wait_ge(a_ready, m - 1)
                            freed(act, tile_of[("value", m - 2)])
                        nc.scalar.activation(work[:, m % 2], pair(t)[:, :, 0:HALF], ACT.Sigmoid).then_inc(psum_free[t % PAIRS], 1)
                    elif kind == "pool":
                        full(act, t)
                        nc.scalar.activation(p_ext[:, m, PHIST:PHIST + SEQ].rearrange("p (h t) -> p h t", h=2),
                                             prompt(pair(t)), ACT.Copy).then_inc(p_ready, 1)
                        nc.scalar.activation(p_ext_s[:, m, :, PHIST:PHIST + SEQ_S].rearrange("p (h b) t -> p h b t", h=2),
                                             sample(pair(t)), ACT.Copy).then_inc(psum_free[t % PAIRS], 1)
                if b == MIX_BLOCKS_IN - 2:
                    diagonals(0, DIAGS)
            named_hi(("out_ab", 1))
            for g in range(AT):
                freed(act, tile_of[("pool", g)])
            nc.scalar.activation(new_s[:, 1].rearrange("p j (b t) -> p j b t", t=SEQ_S), p_ext_s[:, :, :, PHIST:PHIST + SEQ_S],
                                 ACT.Copy).then_inc(new_s_ready, 1)
            freed(act, tile_of[("value", AT - 1)])
            nc.scalar.activation(new_s[:, 0].rearrange("p j (b t) -> p j b t", t=SEQ_S), a_ext_s[:, :, :, HIST:HIST + SEQ_S],
                                 ACT.Copy).then_inc(new_s_ready, 1)
            diagonals(DIAGS, PE_TAPS)
            t = tile_of["conv_pe"]
            full(act, t)
            nc.scalar.activation(conv_part[:, :, :], prompt(pair(t)), ACT.Copy).then_inc(psum_free[t % PAIRS], 1)
            for g in range(AT):
                t, n = tile_of[("pool_mix", g)], U_MIX_OUT + g
                full(act, t)
                act.wait_ge(piece_lo, max(n - 1, U_MIX_OUT))
                nc.scalar.activation(sample(piece[:, n % 2]), sample(pair(t)), ACT.Copy, scale=s_pool_v[:, g:g + 1])\
                  .then_inc(piece_ready, 1)
                nc.scalar.activation(prompt(piece[:, n % 2]), prompt(pair(t)), ACT.Copy, scale=s_pool_v[:, g:g + 1])\
                  .then_inc(psum_free[t % PAIRS], 1)
                freed(act, t)
                piece_to_hi(act_hi[:, AT + g], n)
            for name, rows in (("conv_state", conv_state_rows), ("pool_state", pool_state_rows)):
                t = tile_of[name]
                full(act, t)
                nc.scalar.activation(rows, pair(t)[0:NS], ACT.Copy).then_inc(psum_free[t % PAIRS], 1)
            for j in range(AT):
                if j < AT - 1:
                    act.wait_ge(centred, j + 1)
                else:
                    freed(act, tile_of["conv_mean"])
                nc.scalar.activation(flat(channel_squares[:, j]), flat(acc[:, j]), ACT.Square).then_inc(channel_sq, 1)
            root(tile_of["conv_var"])
            for j in range(AT + 1):
                if j < AT:
                    act.wait_ge(norm_ready, j + 1)
                    nc.scalar.activation(flat(acc[:, j]), flat(work[:, j % 2]), ACT.Identity, bias=b_cln_v[:, j:j + 1],
                                         scale=g_cln_v[:, j:j + 1]).then_inc(affine_ready, 1)
                    if j >= 2:
                        act.wait_ge(piece_ready, U_MIX_OUT + AT + j - 1)
                    nc.scalar.activation(flat(sq[:, j % 2]), flat(work[:, j % 2]), ACT.Sigmoid, bias=b_cln_v[:, j:j + 1],
                                         scale=g_cln_v[:, j:j + 1]).then_inc(silu_ready, 1)
                if j:
                    piece_to_hi(act_hi[:, j - 1], U_MIX_OUT + AT + j - 1)

            def project(name, adds, following, split=1):
                for b in range(OUT_BLOCKS):
                    if b + 1 >= split:
                        named_hi((name, b + 1) if b + 1 < OUT_BLOCKS else following)
                    for m in range(2 * b - 2, 2 * b):
                        if m >= 0:
                            square_x(m, adds + m)
                square_halves(adds, 0)

            project("out_ab", G_EVEN, ("ffn", 0, 0, 0), split=2)
            root_of_half(1, 0)
            norm_pieces_hi(0, SH2, U_FFN_IN0, 1, ("ffn", 0, 0, 1), G_EVEN)
            ffn(0, U_FFN0, G_FFN0, ("in_v", 0))
            root_of_half(2, 0)
            norm_pieces_hi(1, SH1, U_ODD_IN, 2, ("in_v", 1), G_FFN0 + (QUARTERS - 1) * KT)

            def v_norm(c):
                act.wait_ge(v_centred, c + 1)
                if c >= 2:
                    act.wait_ge(v_var, c - 1)
                rows, src = (NS, v_s[:, :]) if c == CHUNKS else (P, v[:, c, :])
                nc.scalar.activation((sq, work)[c % 2][0:rows].rearrange("p i h t -> p (i h t)")[:, 0:D], src,
                                     ACT.Square).then_inc(v_sq, 1)
                act.wait_ge(v_var, c + 1)
                nc.scalar.activation(lnst[0:rows, c, 2:3], lnst[0:rows, c, 1:2], ACT.Sqrt, bias=eps[0:rows, 0:1],
                                     scale=1.0 / D).then_inc(v_root, 1)

            act.wait_ge(piece_lo, U_ODD_IN + NORM_UNITS)
            for dst, src in ((in_s_hi, act_hi), (in_s_lo, act_lo)):
                nc.scalar.activation(dst.rearrange("p k (h t) -> p k h t", h=2), src[:, :, :, HP:HALF].bitcast(F32),
                                     ACT.Copy).then_inc(in_s_ready, 1)
            for n, (name, b) in enumerate(IN_C):
                if n:
                    named_hi(IN_C[n + 1] if n + 1 < len(IN_C) else ("out_c", 0))
                if n >= OUT_BLOCKS:
                    v_norm(n - OUT_BLOCKS + 1)
                if name == "in_u":
                    for m in (2 * b, 2 * b + 1):
                        t = tile_of[("u", m)]
                        full(act, t)
                        nc.scalar.activation(u[:, m], pair(t)[:, :, 0:HALF], ACT.Copy).then_inc(psum_free[t % PAIRS], 1)
                else:
                    if b == 0:
                        t = tile_of["ws"]
                        full(act, t)
                        nc.scalar.activation(ws_t.rearrange("p (a h) t -> p a (h t)", a=2), pair(t), ACT.Copy)\
                          .then_inc(psum_free[t % PAIRS], 1)
                    t = tile_of[("v", b)]
                    full(act, t)
                    nc.scalar.activation(v[:, :, b * BN:(b + 1) * BN].rearrange("p (c a) n -> p a c n", a=2),
                                         pair(t).rearrange("p a (c n) -> p a c n", n=BN), ACT.Copy).then_inc(psum_free[t % PAIRS], 1)
                    t = tile_of[("v_sample", b)]
                    full(act, t)
                    nc.scalar.activation(v_s[:, b * BN:(b + 1) * BN], pair(t)[0:NS, 0, 0:BN], ACT.Copy)\
                      .then_inc(psum_free[t % PAIRS], 1)
                if n == OUT_BLOCKS - 1:
                    v_norm(0)
            for h in range(HEADS):
                piece_to_hi(act_hi[:, h], U_ODD_OUT + h)
            project("out_c", G_ODD, ("ffn", 1, 0, 0))
            root_of_half(3, 0)
            norm_pieces_hi(1, SH2, U_FFN_IN1, 3, ("ffn", 1, 0, 1), G_ODD)
            ffn(1, U_FFN1, G_FFN1)
            root_of_half(4, 0)
            for i in range(NORM_UNITS):
                h, k = divmod(i, KT)
                if i == SQUARES_AT:
                    square_halves(G_FFN1 + (QUARTERS - 1) * KT, 1)
                if i == ROOT_AT:
                    root_of_half(4, 1)
                act.wait_ge(norm_ready, AT + i + 1)
                nc.scalar.activation(y_t[:, k, h], half_slot(work, i), ACT.Copy, scale=g_final_v[:, k:k + 1]).then_inc(y_ready, 1)
            for c in range(0, CHUNKS, 2):
                t = tile_of[("y", c)]
                full(act, t)
                nc.scalar.activation(y_rows[:, c, :].rearrange("p (a n) -> p a n", a=2), pair(t), ACT.Copy)\
                  .then_inc(psum_free[t % PAIRS], 1)
            for h in range(2):
                t = tile_of[("y_sample", h)]
                full(act, t)
                nc.scalar.activation(ys_rows[:, h, :].rearrange("p (a n) -> p a n", a=2), pair(t)[0:HS], ACT.Copy)\
                  .then_inc(psum_free[t % PAIRS], 1)

        @block.vector
        def _(dve):
            own = Own(dve, dve_step)
            dv = nc.vector
            adds = [0]

            def weights_lo(b, i, per_b=None):
                dve.wait_ge(w_hi_ready, b + 1 if per_b is None else per_b + (b + 1))
                dv.tensor_tensor(w_lo[:, b % 2, :, :].rearrange("p k n -> p (k n)"), raw[:, i % RAW, :],
                                 w_hi[:, b % 2, :, :].rearrange("p k n -> p (k n)").bitcast(F32), ALU.subtract)\
                  .then_inc(w_lo_ready, 1)

            def named_lo(name):
                weights_lo(block_of[name], item_of[name])

            def piece_free(n, per=None):
                if per is not None or n >= 2:
                    dve.wait_ge(piece_lo, n - 1 if per is None else per + (n - 1))

            def piece_to_lo(dst_lo, dst_hi, n, per=None):
                dve.wait_ge(piece_hi, n + 1 if per is None else per + (n + 1))
                dv.tensor_tensor(flat(dst_lo), flat(piece[:, n % 2]), flat(dst_hi).bitcast(F32), ALU.subtract)\
                  .then_inc(piece_lo, 1)

            def sum_square(first):
                a = adds[0]
                n = a if a < KT else squares_before(1 + (a - KT) // LAST) + (a - KT) % LAST
                if a:
                    dve.wait_ge(ss_added, a)
                dve.wait_ge(sq_ready, n + 1)
                if first:
                    dv.tensor_copy(flat(ss), flat(sq[:, n % 2])).then_inc(ss_added, 1)
                else:
                    dv.tensor_tensor(flat(ss), flat(ss), flat(sq[:, n % 2]), ALU.add).then_inc(ss_added, 1)
                adds[0] += 1

            def inverse_root_of_half(nth, h):
                dve.wait_ge(root_ready, 2 * nth + 1 + h)
                own.after(own.step(dv.reciprocal(rstd[:, h], rstd[:, h])))
                if h:
                    dv.tensor_copy(lnst[:, 0, 3:4], eps[:, :]).then_inc(psum_free[tile_of[("stat", nth)] % PAIRS], 1)

            def inverse_root(t, n):
                dve.wait_ge(root_ready, n)
                dv.reciprocal(flat(rstd), flat(rstd)).then_inc(psum_free[t % PAIRS], 1)
                freed(dve, t)

            def modulation(layer, i):
                t = tile_of[("ada", layer, i)]
                full(dve, t)
                own.after(own.n)
                dv.transpose(mod_t.rearrange("p k c -> p (k c)"), pair(t)[:, 0, 0:2 * P]).then_inc(psum_free[t % PAIRS], 1)
                freed(dve, t)
                own.step(dv.tensor_tensor(mod[:, layer, i], mod_t[:, :, 0:NCOND],
                                          b_ada_v[:, layer, i, :].unsqueeze(2).broadcast_to([P, KT, NCOND]), ALU.add))

            def norm_pieces(layer, sc, gains, unit, nth, second, adds_halves=None, filler=None):
                own.after(own.n)
                dv.scalar_tensor_tensor(scale[:, :, :], mod[:, layer, sc], 1.0,
                                        gains.unsqueeze(2).broadcast_to([P, KT, NCOND]), ALU.add, ALU.mult)\
                  .then_inc(scale_ready, 1)
                for i in range(NORM_UNITS + 2):
                    h, k = divmod(i, KT)
                    if adds_halves and i == ADDS_AT:
                        adds_halves(1)
                    if adds_halves and i == ROOT_AT:
                        inverse_root_of_half(nth, 1)
                    if i == SECOND_LO_AT:
                        named_lo(second)
                    if filler and i == KT:
                        filler()
                    if i < NORM_UNITS:
                        if i >= 4:
                            dve.wait_ge(piece_hi, unit + i - 3)
                        dv.tensor_tensor(half_slot(work, i), x[:, k, h], rstd[:, h], ALU.mult).then_inc(xr_ready, 1)
                    if i >= 2:
                        norm_piece_lo(unit, i - 2)
                dve.wait_ge(piece_lo, unit + NORM_UNITS)

            def norm_piece_lo(unit, i):
                h, k = divmod(i, KT)
                n = unit + i
                dve.wait_ge(piece_hi, n + 1)
                dv.tensor_tensor(act_lo[:, k, h], half_slot(piece, n), act_hi[:, k, h].bitcast(F32), ALU.subtract)\
                  .then_inc(piece_lo, 1)

            def gated_add(a, m, t, layer, gate, per_a=None, per_t=None):
                def at(n):
                    return n if per_a is None else per_a + n
                gates = mod[:, layer, gate, m, :]
                full(dve, t, per_t)
                if a >= KT:
                    dve.wait_ge(x_prompt_done, at(a - KT + 1))
                    dve.wait_ge(x_sample_done, at(a - KT + 1))
                dv.scalar_tensor_tensor(prompt(x[:, m]), prompt(pair(t)), gates[:, 0:1], prompt(x[:, m]),
                                        ALU.mult, ALU.add).then_inc(x_prompt_done, 1)
                if a >= 2:
                    dve.wait_ge(x_sample_done, at(a - 1))
                tmp = gated_s[:, a % 2, :].rearrange("p (h b t) -> p h b t", h=2, t=SEQ_S)
                dve.wait_ge(x_prompt_done, at(a + 1))
                dv.tensor_tensor(tmp, sample(pair(t)), per_seq(gates), ALU.mult).then_inc(psum_free[t % PAIRS], 1)
                freed(dve, t, per_t)
                dv.tensor_tensor(sample(x[:, m]), sample(x[:, m]), tmp, ALU.add).then_inc(x_sample_done, 1)

            def gated_add_halves(a0, t0, layer, gate, number):
                def step(h):
                    for i in range(2 * h, 2 * h + 2):
                        m, a, t = HALF_ADDS[i][0], a0 + i, t0 + i % 2
                        gates = mod[:, layer, gate, m, :]
                        if h:
                            full(dve, t)
                        else:
                            dve.wait_ge(half_full, 2 * number + i + 1)
                        dve.wait_ge(x_prompt_done, a)
                        dve.wait_ge(x_sample_done, a)
                        dv.scalar_tensor_tensor(x[:, m, h, 0:HP], pair(t)[:, h, 0:HP], gates[:, 0:1], x[:, m, h, 0:HP],
                                                ALU.mult, ALU.add).then_inc(x_prompt_done, 1)
                        tmp = gated_s[:, a % 2, 0:HS].rearrange("p (b t) -> p b t", t=SEQ_S)
                        mult = dv.tensor_tensor(tmp, sample_half(pair(t), h), per_seq_half(gates, h), ALU.mult)
                        if h:
                            mult.then_inc(psum_free[t % PAIRS], 1)
                            freed(dve, t)
                        else:
                            own.after(own.step(mult))
                        dv.tensor_tensor(sample_half(x[:, m], h), sample_half(x[:, m], h), tmp, ALU.add)\
                          .then_inc(x_sample_done, 1)
                return step

            def quarter(layer, units, a0, q=0, per=None, last=False, following=None):
                b0, i0, t0 = (block_of[("ffn", layer, q, 0)], item_of[("ffn", layer, q, 1)] - 1, tile_of[("ffn", layer, q, 0)])
                per_b = None if per is None else per * FFN_BLOCKS
                per_t = None if per is None else per * (2 * FFN_BLOCKS // PAIRS)
                per_u = None if per is None else per * KT
                for j in range(FFN_BLOCKS):
                    if j < FFN_BLOCKS - 2 or not last:
                        weights_lo(b0 + j + 2, i0 + j + 2, per_b)
                    for m in range(2 * j, 2 * j + 2):
                        if j < OUT_BLOCKS:
                            n = units + m
                            piece_free(n, per_u)
                            freed(dve, t0 + m, per_t)
                            dv.tensor_tensor(flat(piece[:, n % 2]), flat(work[:, n % 2]), flat(work[:, n % 2]), ALU.mult)\
                              .then_inc(piece_ready, 1)
                            if m:
                                piece_to_lo(f_lo[:, m - 1], f_hi[:, m - 1], n - 1, per_u)
                            if m == KT - 1:
                                piece_to_lo(f_lo[:, m], f_hi[:, m], n, per_u)
                        else:
                            if last and m >= KT + LAST:
                                continue
                            gated_add(a0 + m - KT, m - KT, t0 + m, layer, GT2, per_u, per_t)
                            if last and m > KT:
                                sum_square(m == KT + 1)
                if last:
                    sum_square(False)

            def ffn(layer, units, a0, number, following=None):
                with dve.Fori(0, QUARTERS - 1) as q:
                    quarter(layer, units, a0, per=q)
                done = (QUARTERS - 1) * KT
                quarter(layer, units + done, a0 + done, q=QUARTERS - 1, last=True, following=following)
                step = gated_add_halves(a0 + done + LAST, tile_of[("ffn", layer, QUARTERS - 1, KT + LAST)], layer, GT2, number)
                step(0)
                if following:
                    named_lo(following)
                return step

            def project(name, a0, layer, number, following, split=1):
                for b in range(OUT_BLOCKS):
                    if split <= b + 1 < OUT_BLOCKS:
                        named_lo((name, b + 1))
                    if b == OUT_BLOCKS - 1:
                        sum_square(False)
                        break
                    for m in range(2 * b, 2 * b + 2):
                        gated_add(a0 + m, m, tile_of[(name, m)], layer, GT1)
                        if m:
                            sum_square(m == 1)
                    if name == "out_ab" and b in MOD_IN_OUT:
                        modulation(1, MOD_IN_OUT[b])
                step = gated_add_halves(a0 + LAST, tile_of[(name, LAST)], layer, GT1, number)
                step(0)
                if following:
                    named_lo(following)
                return step

            dve.wait_ge(c_sigmoid, 1)
            c_sig = sq[0:32].rearrange("p i h t -> p (i h t)")[:, 0:D]
            dv.tensor_tensor(c_rows[:, :], c_rows[:, :], c_sig, ALU.mult).then_inc(c_silu, 1)
            for k in range(KT):
                sum_square(k == 0)
            freed(dve, tile_of["vec"])
            modulation(0, SH1)
            named_lo(("in_ab", 0))
            inverse_root(tile_of[("stat", 0)], 1)
            modulation(0, SC1)
            norm_pieces(0, SC1, g_mix_v[:, 0, :], U_MIX_IN, 0, ("in_ab", 1))
            dve.wait_ge(pads_ready, 2)
            conv_ops = [(j, tap) for j in range(1, AT) for tap in range(TAPS + 1)]
            conv_ops += [(0, tap) for tap in range(PE_TAPS, TAPS + 2)]
            at_op = [0]

            def convolve(count):
                for _ in range(count):
                    if at_op[0] == len(conv_ops):
                        return
                    j, tap = conv_ops[at_op[0]]
                    n = at_op[0]
                    at_op[0] += 1
                    even = prompt(acc[:, j])
                    odd = acc_odd[:, j % 2, :].rearrange("p (h t) -> p h t", h=2)
                    if n >= 2:
                        dve.wait_ge(conv_step, n - 1 if tap < TAPS else n)
                    if tap == TAPS + 1:
                        freed(dve, tile_of["conv_pe"])
                        dv.tensor_tensor(even, even, conv_part[:, :, :], ALU.add).then_inc(conv_step, 1)
                        continue
                    if tap == TAPS:
                        dv.tensor_tensor(even, even, odd, ALU.add).then_inc(conv_step, 1)
                        continue
                    src = a_ext[:, j, tap:tap + SEQ].rearrange("p (h t) -> p h t", h=2)
                    w = w_dw_v[:, tap, j:j + 1]
                    nth = tap if j else tap - PE_TAPS
                    dst = odd if nth % 2 else even
                    if nth == 0:
                        dv.tensor_scalar(dst, src, w, b_dw_v[:, j:j + 1], ALU.mult, ALU.add).then_inc(conv_step, 1)
                    elif nth == 1:
                        dv.tensor_scalar(dst, src, w, None, ALU.mult).then_inc(conv_step, 1)
                    else:
                        dv.scalar_tensor_tensor(dst, src, w, dst, ALU.mult, ALU.add).then_inc(conv_step, 1)

            for b in range(MIX_BLOCKS_IN):
                if b:
                    named_lo(("in_ab", b + 1) if b + 1 < MIX_BLOCKS_IN else ("out_ab", 0))
                kind, first = IN_AB[b]
                for m in range(first, first + 2) if kind == "gate" else ():
                    t_a, t_g = tile_of[("value", m)], tile_of[("gate", m)]
                    full(dve, t_a)
                    freed(dve, t_g)
                    dv.tensor_tensor(a_ext[:, m, HIST:HIST + SEQ].rearrange("p (h t) -> p h t", h=2), prompt(pair(t_a)),
                                     prompt(work[:, m % 2]), ALU.mult).then_inc(a_ready, 1)
                    dve.wait_ge(a_ready, m + 1)
                    dv.tensor_tensor(a_ext_s[:, m, :, HIST:HIST + SEQ_S].rearrange("p (h b) t -> p h b t", h=2),
                                     sample(pair(t_a)), sample(work[:, m % 2]), ALU.mult).then_inc(psum_free[t_a % PAIRS], 1)
                    freed(dve, t_a)
                if b >= 1:
                    convolve(15)
                if b in MOD_AFTER:
                    modulation(0, MOD_AFTER[b])
            named_lo(("out_ab", 1))
            convolve(len(conv_ops) - at_op[0] - 2 * AT)
            for g in range(AT):
                piece_to_lo(act_lo[:, AT + g], act_hi[:, AT + g], U_MIX_OUT + g)
                convolve(2)
            dve.wait_ge(conv_step, CONV_STEPS)
            t = tile_of["conv_mean"]
            full(dve, t)
            for j in range(AT):
                dv.tensor_tensor(acc[:, j], acc[:, j], pair(t)[:, :, 0:HALF], ALU.subtract)\
                  .then_inc(centred if j < AT - 1 else psum_free[t % PAIRS], 1)
            modulation(0, GT2)
            inverse_root(tile_of["conv_var"], 2)
            dve.wait_ge(centred, AT - 1)
            freed(dve, t)
            for j in range(AT + 2):
                if j < AT:
                    if j >= 2:
                        dve.wait_ge(silu_ready, j - 1)
                    dv.tensor_tensor(flat(work[:, j % 2]), flat(acc[:, j]), flat(rstd), ALU.mult).then_inc(norm_ready, 1)
                if 0 < j <= AT:
                    n = U_MIX_OUT + AT + j - 1
                    dve.wait_ge(affine_ready, j)
                    dve.wait_ge(silu_ready, j)
                    piece_free(n)
                    dv.tensor_tensor(flat(piece[:, n % 2]), flat(acc[:, j - 1]), flat(sq[:, (j - 1) % 2]), ALU.mult)\
                      .then_inc(piece_ready, 1)
                if j > 1:
                    piece_to_lo(act_lo[:, j - 2], act_hi[:, j - 2], U_MIX_OUT + AT + j - 2)
            halves = project("out_ab", G_EVEN, 0, 0, ("ffn", 0, 0, 0), split=2)
            inverse_root_of_half(1, 0)
            norm_pieces(0, SC2, g_ffn_v[:, 0, :], U_FFN_IN0, 1, ("ffn", 0, 0, 1), halves, lambda: modulation(1, GT1))
            halves = ffn(0, U_FFN0, G_FFN0, 1, ("in_v", 0))
            inverse_root_of_half(2, 0)
            norm_pieces(1, SC1, g_mix_v[:, 1, :], U_ODD_IN, 2, ("in_v", 1), halves)

            def v_norm(c):
                rows, src = (NS, v_s[:, :]) if c == CHUNKS else (P, v[:, c, :])
                own.after(own.n)
                own.step(dv.reduce_sum(lnst[0:rows, c, 0:1], src, AX_X))
                own.after(own.n)
                own.step(dv.tensor_scalar(lnst[0:rows, c, 0:1], lnst[0:rows, c, 0:1], 1.0 / D, None, ALU.mult))
                own.after(own.n)
                dv.tensor_scalar(src, src, lnst[0:rows, c, 0:1], None, ALU.subtract).then_inc(v_centred, 1)
                dve.wait_ge(v_sq, c + 1)
                own.step(dv.reduce_sum(lnst[0:rows, c, 1:2],
                                       (sq, work)[c % 2][0:rows].rearrange("p i h t -> p (i h t)")[:, 0:D], AX_X))
                own.after(own.n)
                dv.tensor_copy(lnst[0:rows, c, 3:4], lnst[0:rows, c, 1:2]).then_inc(v_var, 1)
                dve.wait_ge(v_root, c + 1)
                own.step(dv.reciprocal(lnst[0:rows, c, 2:3], lnst[0:rows, c, 2:3]))
                own.after(own.n)
                own.step(dv.scalar_tensor_tensor(src, src, lnst[0:rows, c, 2:3], g_v[0:rows, :], ALU.mult, ALU.mult))
                own.after(own.n)
                dv.tensor_tensor(src, src, b_v[0:rows, :], ALU.add).then_inc(v_ready, 1)

            dve.wait_ge(odd_loaded, 64)
            for n in range(len(IN_C)):
                if n:
                    named_lo(IN_C[n + 1] if n + 1 < len(IN_C) else ("out_c", 0))
                if n == OUT_BLOCKS - 1:
                    freed(dve, tile_of[("v", OUT_BLOCKS - 1)])
                    freed(dve, tile_of[("v_sample", OUT_BLOCKS - 1)])
                if n >= OUT_BLOCKS - 1:
                    c = n - (OUT_BLOCKS - 1)
                    v_norm(c)
                if n in MOD_IN_C:
                    modulation(1, MOD_IN_C[n])
                if n == REPLICATE_AT:
                    t = tile_of["rep"]
                    full(dve, t)
                    for h in range(HEADS):
                        mm = dv.tensor_tensor(
                            ws_seq[:, h],
                            pair(t)[0:NS, 0, h * SEQ_S:(h + 1) * SEQ_S].unsqueeze(1).broadcast_to([NS, BATCH_S, SEQ_S]),
                            same_seq[:, :].unsqueeze(2).broadcast_to([NS, BATCH_S, SEQ_S]), ALU.mult)
                        if h < HEADS - 1:
                            own.step(mm)
                        else:
                            mm.then_inc(psum_free[t % PAIRS], 1)
            freed(dve, tile_of[("u", KT - 1)])
            own.after(own.n)
            for h in range(HEADS):
                t = tile_of[("spatial", h)]
                n = U_ODD_OUT + h
                full(dve, t)
                bias = b_s[:, h, :]
                part = own.step(dv.tensor_tensor(
                    prompt(work[:, h % 2]).rearrange("p h (c t) -> p h c t", t=CHUNK),
                    prompt(pair(t)).rearrange("p h (c t) -> p h c t", t=CHUNK),
                    bias.unsqueeze(1).unsqueeze(1).broadcast_to([P, 2, 2, CHUNK]), ALU.add))
                own.after(part)
                dv.tensor_tensor(sample(work[:, h % 2]), sample(pair(t)),
                                 bias[:, 0:SEQ_S].unsqueeze(1).unsqueeze(1).broadcast_to([P, 2, HB, SEQ_S]), ALU.add)\
                  .then_inc(psum_free[t % PAIRS], 1)
                freed(dve, t)
                piece_free(n)
                dv.tensor_tensor(flat(piece[:, n % 2]), flat(work[:, h % 2]), flat(u[:, h]), ALU.mult).then_inc(piece_ready, 1)
                dve.wait_ge(piece_ready, n + 1)
                if h:
                    piece_to_lo(act_lo[:, h - 1], act_hi[:, h - 1], n - 1)
            piece_to_lo(act_lo[:, KT - 1], act_hi[:, KT - 1], U_ODD_OUT + KT - 1)
            halves = project("out_c", G_ODD, 1, 2, ("ffn", 1, 0, 0))
            inverse_root_of_half(3, 0)
            norm_pieces(1, SC2, g_ffn_v[:, 1, :], U_FFN_IN1, 3, ("ffn", 1, 0, 1), halves, lambda: modulation(1, GT2))
            halves = ffn(1, U_FFN1, G_FFN1, 3)
            inverse_root_of_half(4, 0)
            for i in range(NORM_UNITS):
                h, k = divmod(i, KT)
                if i == ADDS_AT:
                    halves(1)
                if i == ROOT_AT:
                    inverse_root_of_half(4, 1)
                if i >= 4:
                    dve.wait_ge(y_ready, i - 3)
                dv.tensor_tensor(half_slot(work, i), x[:, k, h], rstd[:, h], ALU.mult).then_inc(norm_ready, 1)
            for c in range(1, CHUNKS, 2):
                t = tile_of[("y", c)]
                full(dve, t)
                dv.tensor_copy(y_rows[:, c, :].rearrange("p (a n) -> p a n", a=2), pair(t)).then_inc(psum_free[t % PAIRS], 1)


_INS = ["x_prompt", "x_sample", "c_prompt", "c_sample", "state_conv", "state_pool", "w_ada", "b_ada", "g_mix", "g_ffn",
        "w_in_ab", "w_dw", "b_dw", "g_conv_ln", "b_conv_ln", "w_pool", "s_pool", "w_out_ab", "w_in_c", "g_v_ln", "b_v_ln",
        "w_spatial", "b_spatial", "w_out_c", "w_ffn1", "w_ffn2", "g_final"]
_OUTS = [("y_prompt", (1, 512, 1024)), ("y_sample", (8, 4, 1024)), ("new_conv_prompt", (1, 1, 30, 512)),
         ("new_pool_prompt", (1, 1, 15, 512)), ("new_conv_sample", (1, 8, 30, 512)), ("new_pool_sample", (1, 8, 15, 512)),
         ("new_v_sample", (1, 8, 4, 1024))]


def kernel(**inputs):
    import numpy as _np
    import concourse.bacc as _bacc
    from concourse import mybir as _mybir
    from concourse.bass_utils import run_bass_kernel_spmd as _run

    nc = _bacc.Bacc("TRN2", target_bir_lowering=False, num_devices=1)
    arrays, ins, outs = {}, {}, {}
    for name in _INS:
        a = _np.ascontiguousarray(inputs[name])
        arrays[f"in_{name}_dram"] = a
        ins[name] = nc.dram_tensor(f"in_{name}_dram", a.shape, _mybir.dt.from_np(a.dtype), kind="ExternalInput").ap()
    for name, shape in _OUTS:
        outs[name] = nc.dram_tensor(f"out_{name}_dram", shape, _mybir.dt.float32, kind="ExternalOutput").ap()
    hybrid_decoder_step(nc, ins, outs)
    r = _run(nc, [arrays], core_ids=[0])
    return tuple(r.results[0][f"out_{name}_dram"] for name, _ in _OUTS)
```
